# Optimizing a Trainium2 kernel written in Bass

```python
import jax, jax.numpy as jnp
from jax import lax
import numpy as np
import math
import jax
import jax.numpy as jnp

D_MODEL = 1024
BATCH = 1
SEQ = 256
DEPTH = 2

HEAD_DIM = 64
SWA_HEADS = 8
SWA_KV_HEADS = 2
SWA_WINDOW = 128
SWA_BLOCK = SWA_WINDOW
RWKV_HEADS = 8
RWKV_DIM = RWKV_HEADS * HEAD_DIM
RWKV_W_LORA = 64
RWKV_A_LORA = 64
RWKV_G_LORA = 128
RWKV_GN_EPS = 64e-5
NSA_HEADS = 16
NSA_KV_HEADS = 4
CMP_LEN = 32
CMP_STRIDE = 16
CMP_HIDDEN = 256
SEL_LEN = 64
N_SEL = 8
NSA_WINDOW = 256
NSA_QBLOCK = 64
N_BRANCH = 3
D_FF = 2816
CONV_WIDTH = 3
NORM_EPS = 1e-6

N_EVEN = (DEPTH + 1) // 2
N_ODD = DEPTH // 2

SWA_Q_COLS = SWA_HEADS * HEAD_DIM
SWA_KV_COLS = SWA_KV_HEADS * HEAD_DIM
SWA_COLS = SWA_Q_COLS + 2 * SWA_KV_COLS
RWKV_SPLITS = (RWKV_DIM, RWKV_DIM, RWKV_DIM, RWKV_W_LORA, RWKV_A_LORA, RWKV_G_LORA)
RWKV_COLS = sum(RWKV_SPLITS)
HY_COLS = SWA_COLS + RWKV_COLS
HY_OUT = SWA_Q_COLS + RWKV_DIM
NSA_KV_COLS = NSA_KV_HEADS * HEAD_DIM
NSA_SPLITS = (NSA_HEADS * HEAD_DIM,) + (NSA_KV_COLS,) * 6 + (NSA_HEADS * N_BRANCH,)
NSA_COLS = sum(NSA_SPLITS)
NSA_OUT = NSA_HEADS * HEAD_DIM


def split_cols(z, sizes):
    return jnp.split(z, [int(c) for c in np.cumsum(sizes)[:-1]], axis=-1)

def rms_norm(x, g):
    xf = x.astype(jnp.float32)
    y = xf * lax.rsqrt(jnp.mean(xf * xf, axis=-1, keepdims=True) + NORM_EPS)
    return (y * g.astype(jnp.float32)).astype(x.dtype)

def alibi_slopes(n_heads):
    return jnp.exp2(-8.0 * jnp.arange(1, n_heads + 1, dtype=jnp.float32) / n_heads)

def masked_softmax(s, valid):
    s = jnp.where(valid, s, -jnp.inf)
    m = jnp.max(s, axis=-1, keepdims=True)
    m = jnp.where(jnp.isfinite(m), m, 0.0)
    p = jnp.where(valid, jnp.exp(s - m), 0.0)
    d = jnp.sum(p, axis=-1, keepdims=True)
    return p / jnp.where(d > 0, d, 1.0)

def swa_sink_attention(q, k, v, sinks, slopes):
    B, T, _ = q.shape
    G, H, D, L = SWA_KV_HEADS, SWA_HEADS, HEAD_DIM, SWA_BLOCK
    R = H // G
    nb = T // L
    f32 = jnp.float32
    qb = q.reshape(B, nb, L, G, R, D).astype(f32) * D ** -0.5

    def band(a):
        a = jnp.pad(a.reshape(B, T, G, D), ((0, 0), (L, 0), (0, 0), (0, 0))).reshape(B, nb + 1, L, G, D)
        return jnp.concatenate([a[:, :-1], a[:, 1:]], axis=2).astype(f32)

    kb, vb = band(k), band(v)
    qpos = jnp.arange(nb)[:, None, None] * L + jnp.arange(L)[None, :, None]
    kpos = jnp.arange(nb)[:, None, None] * L - L + jnp.arange(2 * L)[None, None, :]
    dist = qpos - kpos
    valid = (dist >= 0) & (dist < SWA_WINDOW) & (kpos >= 0)
    s = jnp.einsum('bnqgrd,bnkgd->bngrqk', qb, kb)
    s = s - slopes.reshape(G, R)[None, None, :, :, None, None] * dist.astype(f32)[None, :, None, None]
    s = jnp.where(valid[None, :, None, None], s, -jnp.inf)
    sink = sinks.astype(f32).reshape(G, R)[None, None, :, :, None, None]
    m = jnp.maximum(jnp.max(s, axis=-1, keepdims=True), sink)
    p = jnp.exp(s - m)
    p = p / (jnp.sum(p, axis=-1, keepdims=True) + jnp.exp(sink - m))
    o = jnp.einsum('bngrqk,bnkgd->bnqgrd', p, vb)
    return o.reshape(B, T, H * D)

def rwkv7_time_mix(z, mu, w0, w2, a0, a2, g2, k_k, k_a, r_k, ln_g, ln_b):
    B, T, _ = z.shape
    H, N = RWKV_HEADS, HEAD_DIM
    f32 = jnp.float32
    z_prev = jnp.pad(z, ((0, 0), (1, 0), (0, 0)))[:, :-1]
    z = z + (z_prev - z) * mu
    r, k, v, w_lo, a_lo, g_lo = split_cols(z, RWKV_SPLITS)
    log_w = -jax.nn.softplus(-(w0 + jnp.tanh(w_lo) @ w2).astype(f32)) - 0.5
    decay = jnp.exp(-jnp.exp(log_w))
    a = jax.nn.sigmoid((a0 + a_lo @ a2).astype(f32))
    g = (jax.nn.sigmoid(g_lo) @ g2).astype(f32)
    heads = lambda t: t.astype(f32).reshape(B, T, H, N)
    r, k, v, decay, a = heads(r), heads(k), heads(v), heads(decay), heads(a)
    kk = k * k_k.astype(f32).reshape(H, N)
    kk = kk / jnp.maximum(jnp.linalg.norm(kk, axis=-1, keepdims=True), 1e-12)
    k = k * (1.0 + (a - 1.0) * k_a.astype(f32).reshape(H, N))

    def step(S, inp):
        r_t, w_t, k_t, v_t, kk_t, a_t = inp
        sa = jnp.einsum('bhij,bhj->bhi', S, kk_t)
        S = S * w_t[:, :, None, :] - sa[..., None] * (kk_t * a_t)[:, :, None, :] + v_t[..., None] * k_t[:, :, None, :]
        return S, jnp.einsum('bhij,bhj->bhi', S, r_t)

    seq = tuple(jnp.moveaxis(t, 1, 0) for t in (r, decay, k, v, kk, a))
    _, y = lax.scan(step, jnp.zeros((B, H, N, N), f32), seq)
    y = jnp.moveaxis(y, 0, 1)
    mean = jnp.mean(y, axis=-1, keepdims=True)
    var = jnp.mean(jnp.square(y - mean), axis=-1, keepdims=True)
    y = ((y - mean) * lax.rsqrt(var + RWKV_GN_EPS)).reshape(B, T, RWKV_DIM)
    y = y * ln_g.astype(f32) + ln_b.astype(f32)
    bonus = jnp.sum(r * k * r_k.astype(f32), axis=-1, keepdims=True) * v
    return (y + bonus.reshape(B, T, RWKV_DIM)) * g

def hybrid_swa_rwkv(h, w_in, w_out, sinks, mu, w0, w2, a0, a2, g2, k_k, k_a, r_k, ln_g, ln_b):
    z = h @ w_in
    q, k, v = split_cols(z[..., :SWA_COLS], (SWA_Q_COLS, SWA_KV_COLS, SWA_KV_COLS))
    o_a = swa_sink_attention(q, k, v, sinks, alibi_slopes(SWA_HEADS))
    o_b = rwkv7_time_mix(z[..., SWA_COLS:], mu, w0, w2, a0, a2, g2, k_k, k_a, r_k, ln_g, ln_b)
    o = jnp.concatenate([o_a, o_b], axis=-1).astype(h.dtype)
    return o @ w_out

def compress_blocks(a, idx, pos, w1, w2):
    blocks = a[:, idx] + pos[None, None, :, None, :]
    hdn = jax.nn.gelu(jnp.einsum('bclgd,ldf->bcgf', blocks, w1), approximate=True)
    return jnp.einsum('bcgf,fd->bcgd', hdn, w2)

def nsa_layer(h, w_in, w_out, pos_k, w1_k, w2_k, pos_v, w1_v, w2_v):
    B, T, _ = h.shape
    G, H, D = NSA_KV_HEADS, NSA_HEADS, HEAD_DIM
    R = H // G
    Q = NSA_QBLOCK
    f32 = jnp.float32
    z = h @ w_in
    q, kc, vc, ks, vs, kw, vw, gl = split_cols(z, NSA_SPLITS)
    q = q.reshape(B, T, G, R, D).astype(f32) * D ** -0.5
    kv = lambda t: t.reshape(B, T, G, D)
    kc, vc, ks, vs, kw, vw = kv(kc), kv(vc), kv(ks), kv(vs), kv(kw), kv(vw)
    gates = jax.nn.sigmoid(gl.astype(f32)).reshape(B, T, G, R, N_BRANCH)
    slopes = alibi_slopes(H).reshape(G, R)

    n_cmp = (T - CMP_LEN) // CMP_STRIDE + 1
    cmp_idx = np.arange(n_cmp)[:, None] * CMP_STRIDE + np.arange(CMP_LEN)[None, :]
    k_cmp = compress_blocks(kc, cmp_idx, pos_k, w1_k, w2_k).astype(f32)
    v_cmp = compress_blocks(vc, cmp_idx, pos_v, w1_v, w2_v).astype(f32)
    cmp_end = jnp.asarray(cmp_idx[:, -1], jnp.int32)

    n_blk = T // SEL_LEN
    k_sel = min(N_SEL, n_blk)
    ks_blk = ks.reshape(B, n_blk, SEL_LEN, G, D).transpose(0, 3, 1, 2, 4).astype(f32)
    vs_blk = vs.reshape(B, n_blk, SEL_LEN, G, D).transpose(0, 3, 1, 2, 4).astype(f32)
    ratio, span = SEL_LEN // CMP_STRIDE, CMP_LEN // CMP_STRIDE
    ov = (ratio * np.arange(n_blk)[:, None, None] + np.arange(ratio)[None, :, None]
          - np.arange(span)[None, None, :]).reshape(n_blk, ratio * span)
    ov_valid = jnp.asarray((ov >= 0) & (ov < n_cmp), f32)
    ov = jnp.asarray(np.clip(ov, 0, n_cmp - 1), jnp.int32)
    blk_ids = jnp.arange(n_blk)
    b_ix = jnp.arange(B)[:, None, None, None]
    g_ix = jnp.arange(G)[None, :, None, None]

    kw_pad = jnp.pad(kw, ((0, 0), (NSA_WINDOW, 0), (0, 0), (0, 0))).astype(f32)
    vw_pad = jnp.pad(vw, ((0, 0), (NSA_WINDOW, 0), (0, 0), (0, 0))).astype(f32)

    def block(i):
        t0 = i * Q
        t = t0 + jnp.arange(Q)
        qi = lax.dynamic_slice_in_dim(q, t0, Q, axis=1)
        g_blk = lax.dynamic_slice_in_dim(gates, t0, Q, axis=1)
        dist_c = t[:, None] - cmp_end[None, :]
        s = jnp.einsum('bqgrd,bcgd->bgrqc', qi, k_cmp) - slopes[:, :, None, None] * dist_c.astype(f32)
        p_cmp = masked_softmax(s, dist_c >= 0)
        o_cmp = jnp.einsum('bgrqc,bcgd->bqgrd', p_cmp, v_cmp)
        imp = jnp.sum(jnp.sum(p_cmp, axis=2)[..., ov] * ov_valid, axis=-1)
        cur = (t // SEL_LEN)[:, None]
        forced = (blk_ids == 0) | (blk_ids == cur) | (blk_ids == cur - 1)
        imp = jnp.where(forced, jnp.inf, jnp.where(blk_ids > cur, -jnp.inf, imp))
        _, sel = lax.top_k(imp, k_sel)
        k_g = ks_blk[b_ix, g_ix, sel]
        v_g = vs_blk[b_ix, g_ix, sel]
        kpos = sel[..., None] * SEL_LEN + jnp.arange(SEL_LEN)
        dist_s = (t[:, None, None] - kpos)[:, :, None]
        s = jnp.einsum('bqgrd,bgqnkd->bgrqnk', qi, k_g) - slopes[None, :, :, None, None, None] * dist_s.astype(f32)
        p = masked_softmax(s.reshape(B, G, R, Q, k_sel * SEL_LEN), (dist_s >= 0).reshape(B, G, 1, Q, k_sel * SEL_LEN))
        o_slc = jnp.einsum('bgrqnk,bgqnkd->bqgrd', p.reshape(s.shape), v_g)
        kwi = lax.dynamic_slice_in_dim(kw_pad, t0, NSA_WINDOW + Q, axis=1)
        vwi = lax.dynamic_slice_in_dim(vw_pad, t0, NSA_WINDOW + Q, axis=1)
        kp = t0 - NSA_WINDOW + jnp.arange(NSA_WINDOW + Q)
        dist_w = t[:, None] - kp[None, :]
        valid_w = (dist_w >= 0) & (dist_w < NSA_WINDOW) & (kp[None, :] >= 0)
        s = jnp.einsum('bqgrd,bkgd->bgrqk', qi, kwi) - slopes[:, :, None, None] * dist_w.astype(f32)
        o_win = jnp.einsum('bgrqk,bkgd->bqgrd', masked_softmax(s, valid_w), vwi)
        return g_blk[..., 0, None] * o_cmp + g_blk[..., 1, None] * o_slc + g_blk[..., 2, None] * o_win

    o = lax.map(block, jnp.arange(T // Q))
    o = jnp.moveaxis(o, 0, 1).reshape(B, T, NSA_OUT).astype(h.dtype)
    return o @ w_out

def conv_ffn(h, w_up, conv_w, conv_b, w_down):
    T = h.shape[1]
    gate, val = jnp.split(h @ w_up, 2, axis=-1)
    gp = jnp.pad(gate, ((0, 0), (CONV_WIDTH - 1, 0), (0, 0)))
    conv = conv_b + gp[:, CONV_WIDTH - 1:] * conv_w[CONV_WIDTH - 1]
    for j in range(CONV_WIDTH - 1):
        conv = conv + gp[:, j:j + T] * conv_w[j]
    return (jax.nn.gelu(conv, approximate=True) * val) @ w_down

def first_inputs(seed: int = 0) -> dict:
    key = jax.random.key(seed)
    keys = iter(jax.random.split(key, 48))
    f32 = jnp.float32
    nrm = lambda shape, scale: jax.random.normal(next(keys), shape, f32) * scale
    uni = lambda shape, lo, hi: jax.random.uniform(next(keys), shape, f32, lo, hi)
    NE, NO = N_EVEN, N_ODD
    return {
        "x": nrm((BATCH, SEQ, D_MODEL), 1.0),
        "mix_pre_g": 1.0 + nrm((DEPTH, D_MODEL), 0.05),
        "mix_post_g": 1.0 + nrm((DEPTH, D_MODEL), 0.05),
        "ffn_pre_g": 1.0 + nrm((DEPTH, D_MODEL), 0.05),
        "ffn_post_g": 1.0 + nrm((DEPTH, D_MODEL), 0.05),
        "hy_w_in": nrm((NE, D_MODEL, HY_COLS), D_MODEL ** -0.5),
        "hy_w_out": nrm((NE, HY_OUT, D_MODEL), HY_OUT ** -0.5),
        "swa_sinks": nrm((NE, SWA_HEADS), 0.5),
        "rwkv_mu": uni((NE, RWKV_COLS), 0.0, 1.0),
        "rwkv_w0": uni((NE, RWKV_DIM), -5.0, -1.0),
        "rwkv_w2": nrm((NE, RWKV_W_LORA, RWKV_DIM), 0.1),
        "rwkv_a0": nrm((NE, RWKV_DIM), 0.1),
        "rwkv_a2": nrm((NE, RWKV_A_LORA, RWKV_DIM), 0.1),
        "rwkv_g2": nrm((NE, RWKV_G_LORA, RWKV_DIM), RWKV_G_LORA ** -0.5),
        "rwkv_k_k": 0.85 + nrm((NE, RWKV_DIM), 0.05),
        "rwkv_k_a": 1.0 + nrm((NE, RWKV_DIM), 0.05),
        "rwkv_r_k": nrm((NE, RWKV_HEADS, HEAD_DIM), 0.1),
        "rwkv_ln_g": 1.0 + nrm((NE, RWKV_DIM), 0.05),
        "rwkv_ln_b": nrm((NE, RWKV_DIM), 0.01),
        "nsa_w_in": nrm((NO, D_MODEL, NSA_COLS), D_MODEL ** -0.5),
        "nsa_w_out": nrm((NO, NSA_OUT, D_MODEL), NSA_OUT ** -0.5),
        "nsa_cmp_pos_k": nrm((NO, CMP_LEN, HEAD_DIM), 0.1),
        "nsa_cmp_w1_k": nrm((NO, CMP_LEN, HEAD_DIM, CMP_HIDDEN), (CMP_LEN * HEAD_DIM) ** -0.5),
        "nsa_cmp_w2_k": nrm((NO, CMP_HIDDEN, HEAD_DIM), CMP_HIDDEN ** -0.5),
        "nsa_cmp_pos_v": nrm((NO, CMP_LEN, HEAD_DIM), 0.1),
        "nsa_cmp_w1_v": nrm((NO, CMP_LEN, HEAD_DIM, CMP_HIDDEN), (CMP_LEN * HEAD_DIM) ** -0.5),
        "nsa_cmp_w2_v": nrm((NO, CMP_HIDDEN, HEAD_DIM), CMP_HIDDEN ** -0.5),
        "ffn_w_up": nrm((DEPTH, D_MODEL, 2 * D_FF), D_MODEL ** -0.5),
        "ffn_conv_w": nrm((DEPTH, CONV_WIDTH, D_FF), CONV_WIDTH ** -0.5),
        "ffn_conv_b": nrm((DEPTH, D_FF), 0.01),
        "ffn_w_down": nrm((DEPTH, D_FF, D_MODEL), D_FF ** -0.5),
    }

def first_block(x, mix_pre_g, mix_post_g, ffn_pre_g, ffn_post_g, hy_w_in, hy_w_out, swa_sinks,
              rwkv_mu, rwkv_w0, rwkv_w2, rwkv_a0, rwkv_a2, rwkv_g2, rwkv_k_k, rwkv_k_a, rwkv_r_k,
              rwkv_ln_g, rwkv_ln_b, nsa_w_in, nsa_w_out, nsa_cmp_pos_k, nsa_cmp_w1_k, nsa_cmp_w2_k,
              nsa_cmp_pos_v, nsa_cmp_w1_v, nsa_cmp_w2_v, ffn_w_up, ffn_conv_w, ffn_conv_b, ffn_w_down):
    for layer in range(DEPTH):
        i = layer // 2
        h = rms_norm(x, mix_pre_g[layer])
        if layer % 2 == 0:
            m = hybrid_swa_rwkv(h, hy_w_in[i], hy_w_out[i], swa_sinks[i], rwkv_mu[i], rwkv_w0[i],
                                rwkv_w2[i], rwkv_a0[i], rwkv_a2[i], rwkv_g2[i], rwkv_k_k[i],
                                rwkv_k_a[i], rwkv_r_k[i], rwkv_ln_g[i], rwkv_ln_b[i])
        else:
            m = nsa_layer(h, nsa_w_in[i], nsa_w_out[i], nsa_cmp_pos_k[i], nsa_cmp_w1_k[i],
                          nsa_cmp_w2_k[i], nsa_cmp_pos_v[i], nsa_cmp_w1_v[i], nsa_cmp_w2_v[i])
        x = x + rms_norm(m, mix_post_g[layer])
        h = rms_norm(x, ffn_pre_g[layer])
        x = x + rms_norm(conv_ffn(h, ffn_w_up[layer], ffn_conv_w[layer], ffn_conv_b[layer], ffn_w_down[layer]),
                         ffn_post_g[layer])
    return x


N_MIXERS = 2
N_SSD_LAYERS = (DEPTH + N_MIXERS - 1) // N_MIXERS
N_MLA_LAYERS = DEPTH // N_MIXERS
N_SUBLAYERS = 3

FFN_RES_WEIGHT = 0.5

SSD_EXPAND = 2
D_INNER = SSD_EXPAND * D_MODEL
SSD_HEAD_DIM = 64
SSD_HEADS = D_INNER // SSD_HEAD_DIM
SSD_GROUPS = 8
SSD_HEADS_PER_GROUP = SSD_HEADS // SSD_GROUPS
SSD_STATE = 128
SSD_CONV = 5
SSD_CHUNK = 128
SSD_CONV_CH = D_INNER + 2 * SSD_GROUPS * SSD_STATE
SSD_IN = D_INNER + SSD_CONV_CH + 2 * SSD_HEADS
SSD_NORM_GROUP = D_INNER // SSD_GROUPS

MLA_HEADS = 16
MLA_Q_LORA = 384
MLA_KV_LORA = 256
MLA_NOPE = 64
MLA_ROPE = 32
MLA_V = 64
MLA_QK = MLA_NOPE + MLA_ROPE
MLA_IN = MLA_Q_LORA + MLA_KV_LORA + MLA_ROPE
ROPE_THETA = 10000.0
ATTN_Q_BLOCK = 128
MAX_POS_OFFSET = 1024


def rms_norm_2(x, g):
    xf = x.astype(jnp.float32)
    y = xf * lax.rsqrt(jnp.mean(xf * xf, axis=-1, keepdims=True) + NORM_EPS)
    return (y * g.astype(jnp.float32)).astype(x.dtype)

def modulate(x, g, shift, scale):
    return rms_norm_2(x, g) * (1.0 + scale[:, None, :]) + shift[:, None, :]

def swiglu(h, w_gate, w_up, w_down):
    return (jax.nn.silu(h @ w_gate) * (h @ w_up)) @ w_down

def depthwise_conv_centred(x, w, bias):
    ch = x.shape[-1]
    pad = SSD_CONV // 2
    out = lax.conv_general_dilated(
        x, w[:, None, :], window_strides=(1,), padding=[(pad, pad)],
        dimension_numbers=("NWC", "WIO", "NWC"), feature_group_count=ch)
    return out + bias

def ssd_chunked(x, dt, A, Bm, Cm):
    b, s, g, r, p = x.shape
    n = Bm.shape[-1]
    nc = s // SSD_CHUNK
    q = SSD_CHUNK
    x = x.reshape(b, nc, q, g, r, p)
    dt = dt.reshape(b, nc, q, g, r)
    Bm = Bm.reshape(b, nc, q, g, n)
    Cm = Cm.reshape(b, nc, q, g, n)
    a_cum = jnp.cumsum(dt * A, axis=2)
    xdt = x * dt[..., None]

    seg = a_cum[:, :, :, None] - a_cum[:, :, None, :]
    mask = jnp.tril(jnp.ones((q, q), dtype=bool))[:, :, None, None]
    decay = jnp.exp(jnp.where(mask, seg, -jnp.inf))
    cb = jnp.einsum("bcign,bcjgn->bcijg", Cm, Bm)
    y_diag = jnp.einsum("bcijgr,bcjgrp->bcigrp", cb[..., None] * decay, xdt)

    decay_to_end = jnp.exp(a_cum[:, :, -1:] - a_cum)
    states = jnp.einsum("bcjgn,bcjgrp->bcgrpn", Bm, xdt * decay_to_end[..., None])
    chunk_decay = jnp.exp(a_cum[:, :, -1])

    def step(h, inp):
        st, dec = inp
        return h * dec[..., None, None] + st, h

    h0 = jnp.zeros((b, g, r, p, n), dtype=states.dtype)
    _, h_prev = lax.scan(step, h0, (jnp.moveaxis(states, 1, 0), jnp.moveaxis(chunk_decay, 1, 0)))
    h_prev = jnp.moveaxis(h_prev, 0, 1)

    y_off = jnp.einsum("bcign,bcgrpn->bcigrp", Cm, h_prev) * jnp.exp(a_cum)[..., None]
    return (y_diag + y_off).reshape(b, s, g, r, p)

def ssd_mixer(h, w_in, conv_w, conv_b, dt_bias, a_log, d_skip, norm_g, w_out):
    b, s, _ = h.shape
    g, r = SSD_GROUPS, SSD_HEADS_PER_GROUP
    proj = h @ w_in
    z, xbc, dt_raw = jnp.split(proj, [D_INNER, D_INNER + SSD_CONV_CH], axis=-1)
    xbc = jax.nn.silu(depthwise_conv_centred(xbc, conv_w, conv_b))
    xs, Bm, Cm = jnp.split(xbc, [D_INNER, D_INNER + SSD_GROUPS * SSD_STATE], axis=-1)
    xs = xs.reshape(b, s, g, r, SSD_HEAD_DIM)
    Bm = Bm.reshape(b, s, g, SSD_STATE)
    Cm = Cm.reshape(b, s, g, SSD_STATE)
    dt = jax.nn.softplus(dt_raw.reshape(b, s, 2, g, r) + dt_bias.reshape(2, g, r))
    A = -jnp.exp(a_log).reshape(2, g, r)

    flip = lambda t: jnp.flip(t, axis=1)
    y_fwd = ssd_chunked(xs, dt[:, :, 0], A[0], Bm, Cm)
    y_bwd = flip(ssd_chunked(flip(xs), flip(dt[:, :, 1]), A[1], flip(Bm), flip(Cm)))
    y = y_fwd + y_bwd + xs * d_skip.reshape(g, r)[..., None]

    y = y.reshape(b, s, D_INNER) * jax.nn.silu(z)
    y = rms_norm_2(y.reshape(b, s, g, SSD_NORM_GROUP), norm_g.reshape(g, SSD_NORM_GROUP))
    return y.reshape(b, s, D_INNER) @ w_out

def rope_tables(positions):
    inv_freq = ROPE_THETA ** (-jnp.arange(0, MLA_ROPE, 2, dtype=jnp.float32) / MLA_ROPE)
    ang = positions.astype(jnp.float32)[..., None] * inv_freq
    return jnp.cos(ang)[:, :, None, :], jnp.sin(ang)[:, :, None, :]

def apply_rope_tail(t, cos, sin):
    t_nope, t_pe = t[..., :MLA_NOPE], t[..., MLA_NOPE:]
    x1, x2 = jnp.split(t_pe.astype(jnp.float32), 2, axis=-1)
    rot = jnp.concatenate([x1 * cos - x2 * sin, x2 * cos + x1 * sin], axis=-1).astype(t.dtype)
    return jnp.concatenate([t_nope, rot], axis=-1)

def blocked_attention(q, k, v):
    b, s, h, dq = q.shape
    nq = s // ATTN_Q_BLOCK
    scale = dq ** -0.5
    qb = jnp.moveaxis(q.reshape(b, nq, ATTN_Q_BLOCK, h, dq), 1, 0)

    def one_block(q_blk):
        logits = jnp.einsum("bqhd,bkhd->bhqk", q_blk, k).astype(jnp.float32) * scale
        p = jax.nn.softmax(logits, axis=-1).astype(v.dtype)
        return jnp.einsum("bhqk,bkhv->bqhv", p, v)

    o = lax.map(one_block, qb)
    return jnp.moveaxis(o, 0, 1).reshape(b, s, h, v.shape[-1])

def mla_mixer(h, positions, w_in, q_norm_g, kv_norm_g, w_uq, w_ukv, q_head_g, k_head_g, w_out):
    b, s, _ = h.shape
    q_lat, kv_lat, k_pe = jnp.split(h @ w_in, [MLA_Q_LORA, MLA_Q_LORA + MLA_KV_LORA], axis=-1)
    q = (rms_norm_2(q_lat, q_norm_g) @ w_uq).reshape(b, s, MLA_HEADS, MLA_QK)
    kv = (rms_norm_2(kv_lat, kv_norm_g) @ w_ukv).reshape(b, s, MLA_HEADS, MLA_NOPE + MLA_V)
    k_nope, v = jnp.split(kv, [MLA_NOPE], axis=-1)
    k_pe = jnp.broadcast_to(k_pe[:, :, None, :], (b, s, MLA_HEADS, MLA_ROPE))
    k = jnp.concatenate([k_nope, k_pe], axis=-1)
    q = rms_norm_2(q, q_head_g)
    k = rms_norm_2(k, k_head_g)
    cos, sin = rope_tables(positions)
    q = apply_rope_tail(q, cos, sin)
    k = apply_rope_tail(k, cos, sin)
    o = blocked_attention(q, k, v)
    return o.reshape(b, s, MLA_HEADS * MLA_V) @ w_out

def second_inputs(seed: int = 0) -> dict:
    key = jax.random.key(seed)
    ks = iter(jax.random.split(key, 40))

    def normal(shape, scale):
        return scale * jax.random.normal(next(ks), shape, jnp.float32)

    def gain(shape):
        return 1.0 + 0.05 * jax.random.normal(next(ks), shape, jnp.float32)

    na, nb = N_SSD_LAYERS, N_MLA_LAYERS
    x = normal((BATCH, SEQ, D_MODEL), 1.0)
    c = normal((BATCH, D_MODEL), 1.0)
    positions = (jax.random.randint(next(ks), (BATCH, 1), 0, MAX_POS_OFFSET, dtype=jnp.int32)
                 + jnp.arange(SEQ, dtype=jnp.int32)[None, :])
    norm_g = gain((DEPTH, N_SUBLAYERS, D_MODEL))
    w_mod = normal((DEPTH, D_MODEL, N_SUBLAYERS * 3 * D_MODEL), D_MODEL ** -0.5)
    b_mod = normal((DEPTH, N_SUBLAYERS * 3 * D_MODEL), 0.02)
    ffn_w_gate = normal((DEPTH, 2, D_MODEL, D_FF), D_MODEL ** -0.5)
    ffn_w_up = normal((DEPTH, 2, D_MODEL, D_FF), D_MODEL ** -0.5)
    ffn_w_down = normal((DEPTH, 2, D_FF, D_MODEL), D_FF ** -0.5)

    ssd_w_in = normal((na, D_MODEL, SSD_IN), D_MODEL ** -0.5)
    ssd_conv_w = normal((na, SSD_CONV, SSD_CONV_CH), SSD_CONV ** -0.5)
    ssd_conv_b = normal((na, SSD_CONV_CH), 0.02)
    dt0 = jnp.exp(jax.random.uniform(next(ks), (na, 2, SSD_HEADS), jnp.float32,
                                     math.log(1e-3), math.log(1e-1)))
    ssd_dt_bias = dt0 + jnp.log(-jnp.expm1(-dt0))
    ssd_a_log = jnp.log(jax.random.uniform(next(ks), (na, 2, SSD_HEADS), jnp.float32, 1.0, 16.0))
    ssd_d = gain((na, SSD_HEADS))
    ssd_norm_g = gain((na, D_INNER))
    ssd_w_out = normal((na, D_INNER, D_MODEL), D_INNER ** -0.5)

    mla_w_in = normal((nb, D_MODEL, MLA_IN), D_MODEL ** -0.5)
    mla_q_norm_g = gain((nb, MLA_Q_LORA))
    mla_kv_norm_g = gain((nb, MLA_KV_LORA))
    mla_w_uq = normal((nb, MLA_Q_LORA, MLA_HEADS * MLA_QK), MLA_Q_LORA ** -0.5)
    mla_w_ukv = normal((nb, MLA_KV_LORA, MLA_HEADS * (MLA_NOPE + MLA_V)), MLA_KV_LORA ** -0.5)
    mla_q_head_g = gain((nb, MLA_QK))
    mla_k_head_g = gain((nb, MLA_QK))
    mla_w_out = normal((nb, MLA_HEADS * MLA_V, D_MODEL), (MLA_HEADS * MLA_V) ** -0.5)

    return {
        "x": x, "c": c, "positions": positions,
        "norm_g": norm_g, "w_mod": w_mod, "b_mod": b_mod,
        "ffn_w_gate": ffn_w_gate, "ffn_w_up": ffn_w_up, "ffn_w_down": ffn_w_down,
        "ssd_w_in": ssd_w_in, "ssd_conv_w": ssd_conv_w, "ssd_conv_b": ssd_conv_b,
        "ssd_dt_bias": ssd_dt_bias, "ssd_a_log": ssd_a_log, "ssd_d": ssd_d,
        "ssd_norm_g": ssd_norm_g, "ssd_w_out": ssd_w_out,
        "mla_w_in": mla_w_in, "mla_q_norm_g": mla_q_norm_g, "mla_kv_norm_g": mla_kv_norm_g,
        "mla_w_uq": mla_w_uq, "mla_w_ukv": mla_w_ukv, "mla_q_head_g": mla_q_head_g,
        "mla_k_head_g": mla_k_head_g, "mla_w_out": mla_w_out,
    }

def second_block(x, c, positions, norm_g, w_mod, b_mod, ffn_w_gate, ffn_w_up, ffn_w_down,
              ssd_w_in, ssd_conv_w, ssd_conv_b, ssd_dt_bias, ssd_a_log, ssd_d,
              ssd_norm_g, ssd_w_out,
              mla_w_in, mla_q_norm_g, mla_kv_norm_g, mla_w_uq, mla_w_ukv,
              mla_q_head_g, mla_k_head_g, mla_w_out):
    cond = jax.nn.silu(c)
    for i in range(DEPTH):
        mod = (cond @ w_mod[i] + b_mod[i]).reshape(-1, N_SUBLAYERS, 3, D_MODEL)

        h = modulate(x, norm_g[i, 0], mod[:, 0, 0], mod[:, 0, 1])
        x = x + FFN_RES_WEIGHT * mod[:, 0, 2][:, None, :] * swiglu(
            h, ffn_w_gate[i, 0], ffn_w_up[i, 0], ffn_w_down[i, 0])

        h = modulate(x, norm_g[i, 1], mod[:, 1, 0], mod[:, 1, 1])
        j = i // N_MIXERS
        if i % N_MIXERS == 0:
            y = ssd_mixer(h, ssd_w_in[j], ssd_conv_w[j], ssd_conv_b[j], ssd_dt_bias[j],
                          ssd_a_log[j], ssd_d[j], ssd_norm_g[j], ssd_w_out[j])
        else:
            y = mla_mixer(h, positions, mla_w_in[j], mla_q_norm_g[j], mla_kv_norm_g[j],
                          mla_w_uq[j], mla_w_ukv[j], mla_q_head_g[j], mla_k_head_g[j],
                          mla_w_out[j])
        x = x + mod[:, 1, 2][:, None, :] * y

        h = modulate(x, norm_g[i, 2], mod[:, 2, 0], mod[:, 2, 1])
        x = x + FFN_RES_WEIGHT * mod[:, 2, 2][:, None, :] * swiglu(
            h, ffn_w_gate[i, 1], ffn_w_up[i, 1], ffn_w_down[i, 1])
    return x


def setup_inputs(seed=0):
    out = dict(first_inputs(seed))
    for name, value in second_inputs(seed + 1).items():
        if name != "x":
            out[name + "_2"] = value
    return out


def reference(
    x, mix_pre_g, mix_post_g, ffn_pre_g, ffn_post_g, hy_w_in, hy_w_out, swa_sinks, rwkv_mu,
    rwkv_w0, rwkv_w2, rwkv_a0, rwkv_a2, rwkv_g2, rwkv_k_k, rwkv_k_a, rwkv_r_k, rwkv_ln_g,
    rwkv_ln_b, nsa_w_in, nsa_w_out, nsa_cmp_pos_k, nsa_cmp_w1_k, nsa_cmp_w2_k, nsa_cmp_pos_v,
    nsa_cmp_w1_v, nsa_cmp_w2_v, ffn_w_up, ffn_conv_w, ffn_conv_b, ffn_w_down, c_2, positions_2,
    norm_g_2, w_mod_2, b_mod_2, ffn_w_gate_2, ffn_w_up_2, ffn_w_down_2, ssd_w_in_2,
    ssd_conv_w_2, ssd_conv_b_2, ssd_dt_bias_2, ssd_a_log_2, ssd_d_2, ssd_norm_g_2, ssd_w_out_2,
    mla_w_in_2, mla_q_norm_g_2, mla_kv_norm_g_2, mla_w_uq_2, mla_w_ukv_2, mla_q_head_g_2,
    mla_k_head_g_2, mla_w_out_2,
):
    x = first_block(
        x, mix_pre_g, mix_post_g, ffn_pre_g, ffn_post_g, hy_w_in, hy_w_out, swa_sinks, rwkv_mu,
        rwkv_w0, rwkv_w2, rwkv_a0, rwkv_a2, rwkv_g2, rwkv_k_k, rwkv_k_a, rwkv_r_k, rwkv_ln_g,
        rwkv_ln_b, nsa_w_in, nsa_w_out, nsa_cmp_pos_k, nsa_cmp_w1_k, nsa_cmp_w2_k,
        nsa_cmp_pos_v, nsa_cmp_w1_v, nsa_cmp_w2_v, ffn_w_up, ffn_conv_w, ffn_conv_b, ffn_w_down,
    )
    return second_block(
        x, c_2, positions_2, norm_g_2, w_mod_2, b_mod_2, ffn_w_gate_2, ffn_w_up_2, ffn_w_down_2,
        ssd_w_in_2, ssd_conv_w_2, ssd_conv_b_2, ssd_dt_bias_2, ssd_a_log_2, ssd_d_2,
        ssd_norm_g_2, ssd_w_out_2, mla_w_in_2, mla_q_norm_g_2, mla_kv_norm_g_2, mla_w_uq_2,
        mla_w_ukv_2, mla_q_head_g_2, mla_k_head_g_2, mla_w_out_2,
    )


_drawn_inputs = setup_inputs


def setup_inputs(seed=0):
    import zlib

    import numpy as np

    out = dict(_drawn_inputs(seed))
    spreads = {}
    factors = {'swa_sinks': 2.867,
     'rwkv_ln_b': 5.994,
     'nsa_cmp_pos_k': 8.0,
     'ffn_conv_b': 6.701,
     'b_mod_2': 2.996,
     'ssd_conv_b_2': 8.0,
     'ssd_d_2': 8.0,
     'ssd_norm_g_2': 4.263,
     'mla_q_norm_g_2': 8.0,
     'mla_kv_norm_g_2': 8.0,
     'mla_w_uq_2': 2.71,
     'mla_q_head_g_2': 8.0,
     'mla_k_head_g_2': 8.0}
    for name, (base, spread) in spreads.items():
        noise = np.random.default_rng([zlib.crc32(name.encode()), seed]).standard_normal(out[name].shape)
        drawn = base * np.exp(spread * noise) if base else spread * noise
        out[name] = jnp.asarray(drawn.astype(out[name].dtype))
    for name, factor in factors.items():
        out[name] = (out[name] * factor).astype(out[name].dtype)
    return out
```

```python
import math
from contextlib import ExitStack

import numpy as np
import concourse.bass as bass
from concourse import mybir

F32 = mybir.dt.float32
I32 = mybir.dt.int32
ALU = mybir.AluOpType
ACT = mybir.ActivationFunctionType
AXX = mybir.AxisListType.X

P = 128
T = 256
NT = T // P
D = 1024
KC = D // P
DFF = 2816
NF = DFF // P
HD = 64
EPS = 1e-6
BIG = 1e30
CHUNK = 1024
RING = 4
SLOT = 3 * CHUNK
C64 = 64
LEVELS = 6
N_CMP = (T - 32) // 16 + 1


def alibi(n):
    return [2.0 ** (-8.0 * (i + 1) / n) for i in range(n)]


def constant_table():
    i = np.arange(P)
    col, row = i[None, :], i[:, None]
    out, at, pos = [], {}, 0

    def add(name, a):
        nonlocal pos
        a = np.ascontiguousarray(a, dtype=np.float32).reshape(P, -1)
        at[name] = (pos, a.shape[1])
        pos += a.shape[1]
        out.append(a)

    add("ident", np.eye(P))
    add("headsum", (row // HD == col // HD))
    same = row // C64 == col // C64
    add("lower", same & (col < row))
    add("upper", same & (col > row))
    add("upper_in", same & (col >= row))
    levels, levels_t = [], []
    for l in range(LEVELS):
        m = 1 << l
        low = (row // (2 * m) == col // (2 * m)) & (row % (2 * m) >= m) & (col % (2 * m) < m)
        levels.append(low)
        levels_t.append(low.T)
    add("level", np.stack(levels, 1))
    add("level_t", np.stack(levels_t, 1))
    t = np.arange(T)
    add("scan_keep", np.broadcast_to(t % C64 != 0, (P, T)))
    dist = (i[:, None] - i[None, :]).astype(np.float32)
    add("causal0", np.where(dist >= 0, dist, BIG))
    dist1 = (P + i[:, None] - t[None, :]).astype(np.float32)
    add("causal1", np.where(dist1 >= 0, dist1, BIG))
    add("window1", np.where((dist1 >= 0) & (dist1 < 128), dist1, BIG))
    ends = np.arange(N_CMP) * 16 + 31
    for n in range(NT):
        dc = (n * P + i)[:, None] - ends[None, :]
        add(f"cmp{n}", np.where(dc >= 0, dc, BIG))
        add(f"cmp_any{n}", ((n * P + i)[:, None] >= 31))
    u = (np.arange(NT)[:, None] * P + i[None, :]).T[:, :, None]
    add("tri_f", u <= t[None, None, :])
    add("tri_b", u >= t[None, None, :])
    add("neg_f", np.where(row <= col, 0.0, -BIG))
    add("neg_b", np.where(row >= col, 0.0, -BIG))
    add("inv_freq", np.broadcast_to(10000.0 ** (-np.arange(0, 32, 2) / 32.0), (P, 16)))
    return np.concatenate(out, 1), at


def cols(v):
    return np.asarray(v).reshape(-1, P).T


def col_chunks(w):
    w = np.asarray(w)
    n = w.shape[1] // P
    return np.ascontiguousarray(w.reshape(KC, P, n, P).transpose(2, 1, 0, 3)).reshape(n, P, CHUNK)


def row_chunks(w):
    w = np.asarray(w)
    return np.ascontiguousarray(w.reshape(-1, P, D))


def ffn_chunks(gate, up, down):
    return np.stack([col_chunks(gate), col_chunks(up), row_chunks(down)], 1)


def twice(w, heads):
    w = np.asarray(w).reshape(w.shape[0], heads, HD)
    return np.concatenate([w, w], 2).reshape(w.shape[0], heads * P)


def padded(w, n):
    w = np.asarray(w)
    return np.concatenate([w, np.zeros((w.shape[0], n - w.shape[1]), w.dtype)], 1)


def lay_out(i):
    i = {k: np.asarray(v) for k, v in i.items()}
    params, at, pos = [], {}, 0

    def add(name, a):
        nonlocal pos
        a = np.asarray(a)
        a = a.reshape(P, -1)
        at[name] = (pos, a.shape[1])
        pos += a.shape[1]
        params.append(a)

    def row(name, v):
        v = np.asarray(v).reshape(-1)
        add(name, np.broadcast_to(v, (P, v.size)))

    for name in ("mix_pre_g", "mix_post_g", "ffn_pre_g", "ffn_post_g"):
        for l in range(2):
            add(f"{name}{l}", cols(i[name][l]))
    add("mu", cols(i["rwkv_mu"][0]))
    for name in ("w0", "a0", "k_k", "k_a", "ln_g", "ln_b"):
        add(name, cols(i["rwkv_" + name][0]))
    add("r_k", cols(i["rwkv_r_k"][0].reshape(-1)))
    add("wa2", np.concatenate([i["rwkv_w2"][0], i["rwkv_a2"][0]], 0))
    add("g2", i["rwkv_g2"][0])
    row("sinks", i["swa_sinks"][0])
    for l in range(2):
        for j in range(3):
            add(f"conv_w{l}{j}", cols(i["ffn_conv_w"][l, j]))
        add(f"conv_b{l}", cols(i["ffn_conv_b"][l]))
    for l in range(2):
        for s in range(3):
            add(f"norm_g{l}{s}", cols(i["norm_g_2"][l, s]))
        add(f"b_mod{l}", cols(i["b_mod_2"][l]))
    add("c", cols(i["c_2"][0]))
    for kv in "kv":
        pos_ = i[f"nsa_cmp_pos_{kv}"][0]
        add("pos_" + kv, pos_.reshape(16, 2, HD).transpose(1, 2, 0).reshape(P, 16))
    w2k = i["nsa_cmp_w2_k"][0].reshape(2, P, HD).transpose(1, 0, 2)
    add("cw2_k", np.concatenate([w2k, w2k], 2))
    add("cw2_v", i["nsa_cmp_w2_v"][0].reshape(2, P, HD).transpose(1, 0, 2))
    for j in range(5):
        add(f"sconv_w{j}", cols(i["ssd_conv_w_2"][0, j]))
    add("sconv_b", cols(i["ssd_conv_b_2"][0]))
    add("snorm_g", cols(i["ssd_norm_g_2"][0]))
    add("d_skip", cols(np.repeat(i["ssd_d_2"][0], HD)))
    row("dt_bias", i["ssd_dt_bias_2"][0])
    row("a_log", i["ssd_a_log_2"][0])
    add("q_norm_g", cols(i["mla_q_norm_g_2"][0]))
    add("kv_norm_g", cols(i["mla_kv_norm_g_2"][0]))
    row("q_head_g", i["mla_q_head_g_2"][0])
    row("k_head_g", i["mla_k_head_g_2"][0])

    hy = i["hy_w_in"][0]
    hy = np.concatenate([hy[:, 0:512], twice(hy[:, 512:640], 2), hy[:, 768:2560], hy[:, 640:768]], 1)
    ns = i["nsa_w_in"][0]
    kc, vc, ks, vs, kw, vw = (ns[:, 1024 + 256 * j:1280 + 256 * j] for j in range(6))
    ns = np.concatenate([ns[:, 0:1024], twice(kc, 4), twice(vc, 4), twice(ks, 4), twice(kw, 4), vs, vw,
                         padded(ns[:, 2560:2608], P)], 1)
    cw1 = [i[f"nsa_cmp_w1_{kv}"][0].reshape(2, 8, 2, HD, 256).transpose(0, 2, 3, 1, 4).reshape(2, P, 2048)
           for kv in "kv"]
    arrays = {
        "x": np.ascontiguousarray(i["x"][0].reshape(NT, P, D).transpose(1, 0, 2)).reshape(P, NT * D),
        "params": np.concatenate(params, 1),
        "consts": constant_table()[0],
        "positions": np.ascontiguousarray(i["positions_2"].reshape(NT, P).T),
        "w_hy_in": col_chunks(hy),
        "w_hy_out": row_chunks(i["hy_w_out"][0]),
        "w_ns_in": col_chunks(ns),
        "w_ns_out": row_chunks(i["nsa_w_out"][0]),
        "w_cmp1": np.concatenate(cw1, 0),
        "w_ssd_in": col_chunks(padded(i["ssd_w_in_2"][0], 49 * P)),
        "w_ssd_out": row_chunks(i["ssd_w_out_2"][0]),
        "w_mla_in": col_chunks(padded(i["mla_w_in_2"][0], 6 * P)),
        "w_uq": i["mla_w_uq_2"][0].reshape(3, P, 3, 512).transpose(2, 1, 0, 3).reshape(3, P, 1536),
        "w_ukv": i["mla_w_ukv_2"][0].reshape(2, P, 4, 512).transpose(2, 1, 0, 3).reshape(4, P, 1024),
        "w_mla_out": row_chunks(i["mla_w_out_2"][0]),
    }
    for l in range(2):
        up = i["ffn_w_up"][l]
        arrays[f"w_conv{l}"] = ffn_chunks(up[:, :DFF], up[:, DFF:], i["ffn_w_down"][l])
        arrays[f"w_mod{l}"] = col_chunks(i["w_mod_2"][l])
        for s in range(2):
            arrays[f"w_ffn{l}{s}"] = ffn_chunks(i["ffn_w_gate_2"][l, s], i["ffn_w_up_2"][l, s],
                                                i["ffn_w_down_2"][l, s])
    return {k: np.ascontiguousarray(v) for k, v in arrays.items()}, at


class Progress:

    def __init__(self, sem):
        self.sem, self.n = sem, 0

    def count(self, _ins):
        self.n += 1
        return (self.sem, self.n)


def build(nc, dram, out, pat, cat, stop=None, dbg=None):
    V, A, E, G = nc.vector, nc.scalar, nc.tensor, nc.gpsimd
    ctx = ExitStack()
    with ctx:
        def sb(name, n, dt=F32):
            return ctx.enter_context(nc.sbuf_tensor(name, [P, n], dt))

        params = sb("params", dram["params"].shape[1])
        consts = sb("consts", dram["consts"].shape[1])
        xs_ = sb("x_res", NT * D)
        hT_ = sb("hT", KC * T)
        htok_ = sb("htok", NT * D)
        ring = sb("ring", RING * SLOT)
        rowb = sb("rowb", D)
        modT = sb("modT", 2 * 72)
        small = sb("small", 512)
        arena = sb("arena", (nc.sbuf_bytes_remaining // 4 - 72) // 64 * 64)
        posi = sb("posi", NT, I32)
        psum = ctx.enter_context(nc.psum_tensor("psum", [P, 8, 512], F32))

        pe = Progress(ctx.enter_context(nc.semaphore("pe_done")))
        act = Progress(ctx.enter_context(nc.semaphore("act_done")))
        dve = Progress(ctx.enter_context(nc.semaphore("dve_done")))
        start_loaded = ctx.enter_context(nc.semaphore("start_loaded"))
        stored = ctx.enter_context(nc.semaphore("stored"))
        slot_full = [ctx.enter_context(nc.semaphore(f"slot_full{n}")) for n in range(RING)]

        block = ctx.enter_context(nc.Block())

        def prm(name):
            a, n = pat[name]
            return params[:, a:a + n]

        def cst(name):
            a, n = cat[name]
            return consts[:, a:a + n]

        x = xs_[:, :].rearrange("p (t d) -> p t d", t=NT)
        hT = hT_[:, :].rearrange("p (k t) -> p k t", k=KC)
        htok = htok_[:, :].rearrange("p (t d) -> p t d", t=NT)
        ident = cst("ident")
        acc = psum[:, 0:4, :].rearrange("p (t b) n -> p t (b n)", t=NT)

        def bank(b):
            return psum[:, b, :]

        def banks(b, n):
            return psum[:, b:b + n, :].rearrange("p b n -> p (b n)")

        class Arena:
            def __init__(self):
                self.at = 0

            def take(self, n):
                self.at += n
                assert self.at <= arena.shape[1], (self.at, arena.shape)
                return arena[:, self.at - n:self.at]

        def spread(ap, shape):
            return ap.to_broadcast(shape)

        def vl(ins):
            p = dve.count(ins)
            V.wait_ge(*p)
            return p

        def al(ins):
            p = act.count(ins)
            A.wait_ge(*p)
            return p

        @block.sync
        def _(sp):
            sp.dma_start(xs_[:, :], dram["x"]).then_inc(start_loaded, 16)
            sp.dma_start(consts[:, :], dram["consts"]).then_inc(start_loaded, 16)
            sp.dma_start(params[:, :], dram["params"]).then_inc(start_loaded, 16)
            sp.dma_start(posi[:, :], dram["positions"]).then_inc(start_loaded, 16)
        loaded = (start_loaded, 64)

        @block.vector
        def _(_e):
            V.wait_ge(*loaded)

        @block.scalar
        def _(_e):
            A.wait_ge(*loaded)

        @block.tensor
        def _(_e):
            E.wait_ge(*loaded)

        class Ring:
            n = 0
            used = [None] * RING
            fills = [0] * RING

        def slot_ap(s, w):
            return ring[:, s * SLOT:s * SLOT + w]

        def load(src, chunks):
            s = Ring.n % RING
            Ring.n += 1
            Ring.fills[s] += 1
            w = src.shape[-1]

            @block.sync
            def _(sp):
                if Ring.used[s] is not None:
                    sp.wait_ge(*Ring.used[s])
                sp.dma_start(slot_ap(s, chunks * w).rearrange("p (c w) -> p c w", c=chunks),
                             src.rearrange("c p w -> p c w")).then_inc(slot_full[s], 16)
            return s, (slot_full[s], 16 * Ring.fills[s])

        def rstd_of(ss, n, scale, eps, ready):
            @block.vector
            def _(_e):
                V.wait_ge(*ready)
                Ring.p = vl(V.tensor_scalar(ss, ss, scale, eps, ALU.mult, ALU.add).then_inc(dve.sem, 1))

            @block.scalar
            def _(_e):
                A.wait_ge(*Ring.p)
                Ring.p = act.count(A.activation(ss, ss, ACT.Sqrt).then_inc(act.sem, 1))

            @block.vector
            def _(_e):
                V.wait_ge(*Ring.p)
                Ring.p = vl(V.reciprocal(ss, ss).then_inc(dve.sem, 1))
            return Ring.p

        def norm_transpose(gain, shift, ready):
            ss = small[:, 0:NT]

            @block.scalar
            def _(_e):
                for point in ready:
                    A.wait_ge(*point)
                for t in range(NT):
                    p = al(A.activation(htok[:, t, :], x[:, t, :], ACT.Square, accum_out=ss[:, t:t + 1]).then_inc(act.sem, 1))
                Ring.q = p
            rstd_of(ss, NT, 1.0 / D, EPS, Ring.q)

            @block.vector
            def _(_e):
                for t in range(NT):
                    Ring.q = dve.count(V.tensor_scalar(htok[:, t, :], x[:, t, :], ss[:, t:t + 1], None, ALU.mult).then_inc(dve.sem, 1))
            normed = Ring.q
            done, freed = [], [loaded] * 4
            for k in range(KC):
                b = bank(4 + k % 4)

                @block.tensor
                def _(_e):
                    E.wait_ge(*normed)
                    E.wait_ge(*freed[k % 4])
                    for t in range(NT):
                        ins = E.transpose(b[:, t * P:(t + 1) * P], htok[:, t, k * P:(k + 1) * P], ident)
                    Ring.p = pe.count(ins.then_inc(pe.sem, 1))
                if k % 2:
                    @block.scalar
                    def _(_e):
                        A.wait_ge(*Ring.p)
                        bias = 0.0 if shift is None else shift[:, k:k + 1]
                        freed[k % 4] = act.count(A.activation(hT[:, k, :], b[:, 0:T], ACT.Identity, bias=bias,
                                                             scale=gain[:, k:k + 1]).then_inc(act.sem, 1))
                else:
                    @block.vector
                    def _(_e):
                        V.wait_ge(*Ring.p)
                        if shift is None:
                            ins = V.tensor_scalar(hT[:, k, :], b[:, 0:T], gain[:, k:k + 1], None, ALU.mult)
                        else:
                            ins = V.tensor_scalar(hT[:, k, :], b[:, 0:T], gain[:, k:k + 1], shift[:, k:k + 1],
                                                  ALU.mult, ALU.add)
                        freed[k % 4] = dve.count(ins.then_inc(dve.sem, 1))
                done.append(freed[k % 4])
            return done[-2:]

        def row_of(col, scale, ready):
            @block.tensor
            def _(_e):
                for point in ready:
                    E.wait_ge(*point)
                for k in range(KC):
                    ins = E.matmul(bank(4 + k // 4)[:, (k % 4) * P:(k % 4 + 1) * P],
                                   spread(col[:, k:k + 1], [P, P]), ident, start=True, stop=True)
                Ring.p = pe.count(ins.then_inc(pe.sem, 1))

            @block.scalar
            def _(_e):
                A.wait_ge(*Ring.p)
                Ring.p = al(A.activation(rowb[:, :], banks(4, 2), ACT.Copy, scale=scale).then_inc(act.sem, 1))
            return Ring.p

        def add_normed(ready):
            ss = small[:, 0:NT]

            @block.scalar
            def _(_e):
                for point in ready:
                    A.wait_ge(*point)
                for t in range(NT):
                    Ring.q = al(A.activation(htok[:, t, :], acc[:, t, :], ACT.Square, accum_out=ss[:, t:t + 1]).then_inc(act.sem, 1))
            rstd_of(ss, NT, 1.0 / D, EPS, Ring.q)

            @block.vector
            def _(_e):
                for t in range(NT):
                    dve.count(V.scalar_tensor_tensor(htok[:, t, :], acc[:, t, :], ss[:, t:t + 1], rowb[:, :],
                                                    ALU.mult, ALU.mult).then_inc(dve.sem, 1))
                V.wait_ge(dve.sem, dve.n)
                Ring.p = vl(V.tensor_tensor(xs_[:, :], xs_[:, :], htok_[:, :], ALU.add).then_inc(dve.sem, 1))
            return [Ring.p]

        def add_gated(ready):
            @block.vector
            def _(_e):
                for point in ready:
                    V.wait_ge(*point)
                for t in range(NT):
                    dve.count(V.tensor_tensor(htok[:, t, :], acc[:, t, :], rowb[:, :], ALU.mult).then_inc(dve.sem, 1))
                V.wait_ge(dve.sem, dve.n)
                Ring.p = vl(V.tensor_tensor(xs_[:, :], xs_[:, :], htok_[:, :], ALU.add).then_inc(dve.sem, 1))
            return [Ring.p]

        def project(name, n, evac, ready, first=4, nb=4, tokens=(), widths={}):
            freed = [()] * nb
            for c0 in range(0, n, 3):
                m = min(3, n - c0)
                s, full = load(dram[name][c0:c0 + m], m)
                for c in range(c0, c0 + m):
                    b = bank(first + c % nb)
                    w = slot_ap(s, SLOT).rearrange("p (c k n) -> p c k n", c=3, k=KC)[:, c - c0]

                    @block.tensor
                    def _(_e):
                        E.wait_ge(*full)
                        for point in ready:
                            E.wait_ge(*point)
                        for point in freed[c % nb]:
                            E.wait_ge(*point)
                        if c in tokens:
                            width = widths.get(c, P)
                            for t in range(NT):
                                for k in range(KC):
                                    ins = E.matmul(b[:, t * width:(t + 1) * width], hT[:, k, t * P:(t + 1) * P],
                                                   w[:, k, 0:width], start=k == 0, stop=k == KC - 1)
                        else:
                            for k in range(KC):
                                ins = E.matmul(b[:, 0:T], w[:, k, :], hT[:, k, :], start=k == 0, stop=k == KC - 1)
                        Ring.p = pe.count(ins.then_inc(pe.sem, 1))
                    freed[c % nb] = evac(c, b, Ring.p)
                    Ring.used[s] = (pe.sem, pe.n)

        def out_project(name, n, lhs, ready):
            for c0 in range(0, n, 3):
                m = min(3, n - c0)
                s, full = load(dram[name][c0:c0 + m], m)

                @block.tensor
                def _(_e):
                    E.wait_ge(*full)
                    for point in ready:
                        E.wait_ge(*point)
                    for k in range(c0, c0 + m):
                        w = slot_ap(s, SLOT)[:, (k - c0) * D:(k - c0 + 1) * D]
                        for t in range(NT):
                            for h in range(2):
                                ins = E.matmul(acc[:, t, h * 512:(h + 1) * 512], lhs[:, k, t * P:(t + 1) * P],
                                               w[:, h * 512:(h + 1) * 512], start=k == 0, stop=k == n - 1)
                    Ring.used[s] = pe.count(ins.then_inc(pe.sem, 1))
            return [Ring.used[s]]

        def ffn(name, ready, conv=None, mod=None):
            ar = Arena()
            hid = [ar.take(T) for _ in range(2)]
            sg = [ar.take(T) for _ in range(2)]
            gp = [ar.take(T + 2) for _ in range(2)]
            cv = [ar.take(T) for _ in range(2)]
            src = dram[name]
            PM = 3 if mod is not None else 2
            AM = 2 if conv is not None else 1
            DM = (4 if conv is not None else 1) + (1 if mod is not None else 0)

            if conv is not None:
                @block.vector
                def _(_e):
                    for point in ready:
                        V.wait_ge(*point)
                    for q in range(2):
                        vl(V.memset(gp[q][:, 0:2], 0.0).then_inc(dve.sem, 1))
                ready = list(ready) + [(dve.sem, dve.n)]

                @block.scalar
                def _(_e):
                    A.wait_ge(dve.sem, dve.n)
            PB, AB, DB = pe.n - 1, act.n, dve.n

            def zero(j):
                return 1 if isinstance(j, int) and j == 0 else 0

            def up_done(j):
                return (pe.sem, PB + PM * j + 1 + zero(j))

            def mod_done(j):
                return (pe.sem, PB + PM * j + 2 + zero(j))

            def down_done(j):
                return (pe.sem, PB + PM * (j + 1) + PM)

            def hid_ready(j):
                return (dve.sem, DB + DM * j + (4 if conv is not None else 1))

            def mod_out(j):
                return (dve.sem, DB + DM * j + DM)

            def act_point(j, k):
                return (act.sem, AB + AM * j + k)

            def conv_ready(j):
                return (dve.sem, DB + DM * j + 3)

            slots0 = Ring.n
            per = 2 if mod is not None else 1

            def slot(j, k=0):
                return (slots0 + per * j + k) % RING

            fills0 = list(Ring.fills)

            def full(j, ju, k=0):
                s = slot(ju, k)
                first = next(n for n in range(RING) if (slots0 + n) % RING == s)
                lot = (per * ju + k - first) // RING
                if per == 1:
                    return (slot_full[s], 16 * (fills0[s] + 1 + lot) + 4 * (j - ju))
                return (slot_full[s], 16 * (fills0[s] + 1 + lot) + 8 * (j - ju))

            def sp_step(sp, j, ju, waits):
                s = slot(ju)
                for point in waits:
                    sp.wait_ge(*point)
                sp.dma_start(slot_ap(s, SLOT).rearrange("p (c w) -> p c w", c=3),
                             (src[j] if isinstance(j, int) else
                              src[bass.ds(j, 1)].rearrange("a c p w -> (a c) p w")).rearrange("c p w -> p c w")
                             ).then_inc(slot_full[s], 16)

            def sp_mod(sp, m, s, waits=()):
                for point in waits:
                    sp.wait_ge(*point)
                sp.dma_start(slot_ap(s, SLOT).rearrange("p (c w) -> p c w", c=3),
                             (dram[f"w_mod{mod}"][3 * m:3 * m + 3] if isinstance(m, int) else
                              dram[f"w_mod{mod}"][bass.ds(m * 3, 3)]).rearrange("c p w -> p c w")
                             ).then_inc(slot_full[s], 16)

            def pe_up(j, ju, waits):
                E.wait_ge(*full(j, ju))
                for point in waits:
                    E.wait_ge(*point)
                w = slot_ap(slot(ju), SLOT).rearrange("p (c k n) -> p c k n", c=3, k=KC)
                b = bank(4 + ju % 2)
                for g in range(2):
                    for k in range(KC):
                        ins = E.matmul(b[:, g * T:(g + 1) * T], w[:, g, k, :], hT[:, k, :],
                                       start=k == 0, stop=k == KC - 1)
                ins.then_inc(pe.sem, 1)

            def pe_mod(b, s):
                w = slot_ap(s, SLOT).rearrange("p (c k n) -> p c k n", c=3, k=KC)
                for c in range(3):
                    for k in range(KC):
                        ins = E.matmul(b[:, c:c + 1], w[:, c, k, :], cond[:, k:k + 1], start=k == 0, stop=k == KC - 1)
                ins.then_inc(pe.sem, 1)

            def pe_down(ju, waits, start=False, stop=False):
                for point in waits:
                    E.wait_ge(*point)
                w = slot_ap(slot(ju), SLOT)[:, 2 * CHUNK:]
                for t in range(NT):
                    for h in range(2):
                        ins = E.matmul(acc[:, t, h * 512:(h + 1) * 512], hid[ju % 2][:, t * P:(t + 1) * P],
                                       w[:, h * 512:(h + 1) * 512], start=start, stop=stop)
                ins.then_inc(pe.sem, 1)

            def act_step(j, ju, waits):
                b = bank(4 + ju % 2)
                q = ju % 2
                A.wait_ge(*up_done(j))
                for point in waits:
                    A.wait_ge(*point)
                if conv is None:
                    A.activation(sg[q], b[:, 0:T], ACT.Silu).then_inc(act.sem, 1)
                else:
                    A.activation(gp[q][:, 2:T + 2], b[:, 0:T], ACT.Copy).then_inc(act.sem, 1)
                    A.wait_ge(*conv_ready(j))
                    A.activation(sg[q], cv[q], ACT.Gelu_apprx_tanh).then_inc(act.sem, 1)

            def one(name_, j):
                v = prm(name_)
                return v[:, j:j + 1] if isinstance(j, int) else v[:, bass.ds(j, 1)]

            def dve_step(j, ju, waits):
                b = bank(4 + ju % 2)
                q = ju % 2
                if conv is not None:
                    V.wait_ge(*act_point(j, 1))
                    V.tensor_scalar(cv[q], gp[q][:, 0:T], one(f"conv_w{conv}0", j), one(f"conv_b{conv}", j),
                                    ALU.mult, ALU.add).then_inc(dve.sem, 1)
                    for w in (1, 2):
                        V.wait_ge(dve.sem, DB + DM * j + w)
                        V.scalar_tensor_tensor(cv[q], gp[q][:, w:w + T], one(f"conv_w{conv}{w}", j), cv[q],
                                               ALU.mult, ALU.add).then_inc(dve.sem, 1)
                V.wait_ge(*act_point(j, AM))
                V.wait_ge(*up_done(j))
                for point in waits:
                    V.wait_ge(*point)
                V.tensor_tensor(hid[q], sg[q], b[:, T:2 * T], ALU.mult).then_inc(dve.sem, 1)

            def dve_mod(m, b):
                o = modT[:, mod * 72:(mod + 1) * 72]
                bm = prm(f"b_mod{mod}")
                if isinstance(m, int):
                    o, bm = o[:, 3 * m:3 * m + 3], bm[:, 3 * m:3 * m + 3]
                else:
                    o, bm = o[:, bass.ds(m * 3, 3)], bm[:, bass.ds(m * 3, 3)]
                V.tensor_tensor(o, b[:, 0:3], bm, ALU.add).then_inc(dve.sem, 1)

            for j in range(2):
                @block.sync
                def _(sp):
                    sp_step(sp, j, j, [Ring.used[slot(j)]] if Ring.used[slot(j)] else [])
                    if mod is not None:
                        sp_mod(sp, j, slot(j, 1), [Ring.used[slot(j, 1)]] if Ring.used[slot(j, 1)] else [])

                @block.tensor
                def _(_e):
                    pe_up(j, j, ready)
                    if mod is not None:
                        E.wait_ge(*full(j, j, 1))
                        pe_mod(bank(6 + j % 2), slot(j, 1))
                    if j == 1:
                        pe_down(0, [hid_ready(0)], start=True)

                @block.scalar
                def _(_e):
                    act_step(j, j, [])

                @block.vector
                def _(_e):
                    dve_step(j, j, [])
                    if mod is not None:
                        V.wait_ge(*mod_done(j))
                        dve_mod(j, bank(6 + j % 2))

            @block.sync
            def _(sp):
                with sp.Fori(0, (NF - 2) // 4) as i:
                    for u in range(4):
                        j = i * 4 + (2 + u)
                        if mod is not None:
                            sp_step(sp, j, 2 + u, [(pe.sem, PB + PM * 2 + i * (4 * PM) + u * PM)])
                            sp_mod(sp, j, slot(2 + u, 1))
                        else:
                            sp_step(sp, j, 2 + u, [(pe.sem, PB + 1 + i * (4 * PM) + u * PM)])

            @block.tensor
            def _(_e):
                with E.Fori(0, (NF - 2) // 4) as i:
                    for u in range(4):
                        j = i * 4 + (2 + u)
                        pe_up(j, 2 + u, [hid_ready(i * 4 + u)])
                        if mod is not None:
                            E.wait_ge(*full(j, 2 + u, 1))
                            E.wait_ge(*mod_out(i * 4 + u))
                            pe_mod(bank(6 + u % 2), slot(2 + u, 1))
                        pe_down(1 + u, [hid_ready(i * 4 + (1 + u))])

            @block.scalar
            def _(_e):
                with A.Fori(0, (NF - 2) // 4) as i:
                    for u in range(4):
                        act_step(i * 4 + (2 + u), 2 + u, [hid_ready(i * 4 + u)])

            @block.vector
            def _(_e):
                with V.Fori(0, (NF - 2) // 4) as i:
                    for u in range(4):
                        j = i * 4 + (2 + u)
                        dve_step(j, 2 + u, [down_done(i * 4 + u)])
                        if mod is not None:
                            V.wait_ge(*mod_done(j))
                            dve_mod(j, bank(6 + u % 2))

            @block.tensor
            def _(_e):
                pe_down(NF - 1, [hid_ready(NF - 1)], stop=True)
            pe.n = PB + 1 + PM * NF
            act.n = AB + AM * NF
            dve.n = DB + DM * NF
            final = (pe.sem, pe.n)
            for k in range(per * NF):
                Ring.fills[(slots0 + k) % RING] += 1
            Ring.n = slots0 + per * NF
            Ring.used = [final] * RING
            if mod is not None:
                for m in range(NF, 24):
                    s, fullp = load(dram[f"w_mod{mod}"][3 * m:3 * m + 3], 3)

                    @block.tensor
                    def _(_e):
                        E.wait_ge(*fullp)
                        E.wait_ge(dve.sem, dve.n)
                        pe_mod(bank(6), s)
                        pe.n += 1
                        Ring.used[s] = (pe.sem, pe.n)

                    @block.vector
                    def _(_e):
                        V.wait_ge(pe.sem, pe.n)
                        dve_mod(m, bank(6))
                        dve.n += 1
            return [final]

        def attend(units, ar, keys, ready):
            s_buf = [ar.take(4 * keys).rearrange("p (h k) -> p h k", h=4) for _ in range(2)]
            nblk = max(u["blocks"] for u in units)
            pT = [[ar.take(4 * P) for _ in range(u_blocks)] for u_blocks in
                  [max(u["blocks"] for u in units if u["branch"] == b) for b in sorted({u["branch"] for u in units})]]
            st = ar.take(2 * 16)
            state = {"s_free": [loaded] * 2, "p_free": [loaded] * 2, "t_free": loaded, "o_free": [loaded] * 2,
                     "pT_free": loaded}
            nout = [0]

            def front(n, u):
                q = n % 2
                nk = u["keys"]
                sc = banks(2 * q, 2).rearrange("p (o e k) -> p e o k", o=2, e=2)
                s = s_buf[q]
                stats = st[:, 16 * q:16 * q + 16]
                mx, rs, nm, xtra = (stats[:, 4 * a:4 * a + 4] for a in range(4))

                @block.tensor
                def _(_e):
                    for point in ready:
                        E.wait_ge(*point)
                    E.wait_ge(*state["s_free"][q])
                    for i in range(4):
                        ins = E.matmul(sc[:, i // 2, i % 2, 0:nk], u["q"](i), u["k"](i), start=True, stop=True)
                    Ring.p = pe.count(ins.then_inc(pe.sem, 1))

                @block.vector
                def _(_e):
                    V.wait_ge(*Ring.p)
                    V.wait_ge(*state["p_free"][q])
                    if u["dist"] is not None:
                        for i in range(4):
                            p = dve.count(V.scalar_tensor_tensor(s[:, i, 0:nk], u["dist"], -u["slopes"][i],
                                                                sc[:, i // 2, i % 2, 0:nk], ALU.mult, ALU.add).then_inc(dve.sem, 1))
                        V.wait_ge(*p)
                        state["s_free"][q] = p
                        vl(V.tensor_reduce(mx, s[:, :, 0:nk], AXX, ALU.max).then_inc(dve.sem, 1))
                    else:
                        vl(V.tensor_reduce(mx.rearrange("p (e o) -> p e o", e=2), sc[:, :, :, 0:nk], AXX, ALU.max).then_inc(dve.sem, 1))
                    if u.get("sinks") is not None:
                        vl(V.tensor_tensor(mx, mx, u["sinks"], ALU.max).then_inc(dve.sem, 1))
                        vl(V.tensor_tensor(xtra, u["sinks"], mx, ALU.subtract).then_inc(dve.sem, 1))
                    Ring.p = vl(V.tensor_scalar(nm, mx, -u["scale"], None, ALU.mult).then_inc(dve.sem, 1))

                @block.scalar
                def _(_e):
                    A.wait_ge(*Ring.p)
                    for i in range(4):
                        src = s[:, i, 0:nk] if u["dist"] is not None else sc[:, i // 2, i % 2, 0:nk]
                        p = act.count(A.activation(s[:, i, 0:nk], src, ACT.Exp, bias=nm[:, i:i + 1],
                                                  scale=u["scale"], accum_out=rs[:, i:i + 1]).then_inc(act.sem, 1))
                    if u["dist"] is None:
                        state["s_free"][q] = p
                    if u.get("sinks") is not None:
                        p = act.count(A.activation(xtra, xtra, ACT.Exp).then_inc(act.sem, 1))
                    u["exp"] = p

            def back(n, u):
                q = n % 2
                nk = u["keys"]
                s = s_buf[q]
                stats = st[:, 16 * q:16 * q + 16]
                mx, rs, nm, xtra = (stats[:, 4 * a:4 * a + 4] for a in range(4))

                @block.vector
                def _(_e):
                    V.wait_ge(*u["exp"])
                    if u.get("sinks") is not None:
                        vl(V.tensor_tensor(rs, rs, xtra, ALU.add).then_inc(dve.sem, 1))
                    vl(V.reciprocal(rs, rs).then_inc(dve.sem, 1))
                    if u.get("gates") is not None:
                        vl(V.tensor_tensor(rs, rs, u["gates"], ALU.mult).then_inc(dve.sem, 1))
                    Ring.p = vl(V.tensor_tensor(s[:, :, 0:nk], s[:, :, 0:nk],
                                                spread(rs.rearrange("p (h o) -> p h o", o=1), [P, 4, nk]), ALU.mult).then_inc(dve.sem, 1))
                normed = Ring.p

                @block.tensor
                def _(_e):
                    E.wait_ge(*normed)
                    E.wait_ge(*state["t_free"])
                    for b in range(u["blocks"]):
                        w = min(P, nk - b * P)
                        for i in range(4):
                            ins = E.transpose(bank(4 + b)[0:w, i * P:(i + 1) * P], s[:, i, b * P:b * P + w], ident)
                    Ring.p = pe.count(ins.then_inc(pe.sem, 1))
                state["p_free"][q] = Ring.p

                @block.scalar
                def _(_e):
                    A.wait_ge(*Ring.p)
                    A.wait_ge(*state["pT_free"])
                    for b in range(u["blocks"]):
                        w = min(P, nk - b * P)
                        state["t_free"] = act.count(A.activation(pT[u["branch"]][b][0:w, :], bank(4 + b)[0:w, :],
                                                                ACT.Copy).then_inc(act.sem, 1))
                if not u["last"]:
                    return
                z = nout[0] % 2
                nout[0] += 1
                ob = bank(6 + z)

                @block.tensor
                def _(_e):
                    E.wait_ge(*state["t_free"])
                    E.wait_ge(*state["o_free"][z])
                    for i in range(4):
                        o = ob[(i % 2) * HD:(i % 2 + 1) * HD, (i // 2) * P:(i // 2 + 1) * P]
                        todo = [(v, b) for v in u["parts"] for b in range(v["blocks"])]
                        for m, (v, b) in enumerate(todo):
                            w = min(P, v["keys"] - b * P)
                            ins = E.matmul(o, v["v"](i, b), pT[v["branch"]][b][0:w, i * P:(i + 1) * P],
                                           start=m == 0, stop=m == len(todo) - 1)
                    Ring.p = pe.count(ins.then_inc(pe.sem, 1))
                state["pT_free"] = Ring.p

                @block.vector
                def _(_e):
                    V.wait_ge(*Ring.p)
                    state["o_free"][z] = dve.count(V.tensor_copy(
                        u["out"], ob[:, 0:2 * P].rearrange("p (c n) -> p c n", c=2)).then_inc(dve.sem, 1))

            for n, u in enumerate(units):
                front(n, u)
                if n:
                    back(n - 1, units[n - 1])
            back(len(units) - 1, units[-1])
            return [(dve.sem, dve.n)]

        def hybrid(ready):
            h_ready = norm_transpose(prm("mix_pre_g0"), None, ready)
            ar = Arena()
            four = lambda: ar.take(4 * T)
            r_, k_, v_, ld_, cum_, a_, g_, kk_, bon_, t1_, t2_ = (four() for _ in range(11))
            wa, glo = g_[:, 0:T], g_[:, T:2 * T]
            omm = small[:, 16:30]
            omka = small[:, 32:36]
            mark0 = ar.at
            qT = ar.take(4 * T).rearrange("p (c t) -> p c t", c=4)
            kT = ar.take(2 * T).rearrange("p (c t) -> p c t", c=2)
            vtok = ar.take(NT * P).rearrange("p (t d) -> p t d", t=NT)
            mu = prm("mu")

            @block.vector
            def _(_e):
                vl(V.tensor_scalar(omm, mu, -1.0, 1.0, ALU.mult, ALU.add).then_inc(dve.sem, 1))
                Ring.q = vl(V.tensor_scalar(omka, prm("k_a"), -1.0, 1.0, ALU.mult, ALU.add).then_inc(dve.sem, 1))
            coef = Ring.q

            def evac(c, b, p):
                if c < 4:
                    @block.scalar
                    def _(_e):
                        A.wait_ge(*p)
                        Ring.q = act.count(A.activation(qT[:, c, :], b[:, 0:T], ACT.Copy, scale=HD ** -0.5).then_inc(act.sem, 1))
                elif c < 6:
                    @block.scalar
                    def _(_e):
                        A.wait_ge(*p)
                        Ring.q = act.count(A.activation(kT[:, c - 4, :], b[:, 0:T], ACT.Copy).then_inc(act.sem, 1))
                elif c == 20:
                    @block.scalar
                    def _(_e):
                        A.wait_ge(*p)
                        Ring.q = act.count(A.activation(vtok, b[:, 0:T].rearrange("p (t d) -> p t d", t=NT), ACT.Copy).then_inc(act.sem, 1))
                else:
                    m = c - 6
                    dst = ([r_] * 4 + [k_] * 4 + [v_] * 4)[m][:, (m % 4) * T:(m % 4 + 1) * T] if m < 12 else \
                        (wa if m == 12 else glo)

                    @block.scalar
                    def _(_e):
                        A.wait_ge(*p)
                        A.wait_ge(*coef)
                        Ring.q = act.count(A.activation(dst, b[:, 0:T], ACT.Copy, scale=omm[:, m:m + 1]).then_inc(act.sem, 1))

                    @block.vector
                    def _(_e):
                        V.wait_ge(*Ring.q)
                        Ring.q = dve.count(V.scalar_tensor_tensor(dst[:, 1:T], b[:, 0:T - 1], mu[:, m:m + 1],
                                                                 dst[:, 1:T], ALU.mult, ALU.add).then_inc(dve.sem, 1))
                return (Ring.q,)

            project("w_hy_in", 21, evac, h_ready, tokens=(20,))
            projected = [(dve.sem, dve.n), (act.sem, act.n), (pe.sem, pe.n)]
            oT = hT

            slopes = alibi(8)
            sinks = prm("sinks")
            units = []
            for g in range(2):
                for t in range(NT):
                    u = dict(branch=0, scale=1.0, slopes=slopes[4 * g:4 * g + 4], sinks=sinks[:, 4 * g:4 * g + 4],
                             keys=(t + 1) * P, blocks=t + 1, last=True,
                             dist=cst("causal0") if t == 0 else cst("window1"),
                             q=lambda i, g=g, t=t: qT[(i % 2) * HD:(i % 2 + 1) * HD, 2 * g + i // 2, t * P:(t + 1) * P],
                             k=lambda i, g=g, t=t: kT[(i % 2) * HD:(i % 2 + 1) * HD, g, 0:(t + 1) * P],
                             v=lambda i, b, g=g: vtok[:, b, g * HD:(g + 1) * HD],
                             out=oT[:, 2 * g:2 * g + 2, t * P:(t + 1) * P])
                    u["parts"] = [u]
                    units.append(u)
            attend(units, ar, T, projected)
            swa_done = [(dve.sem, dve.n), (act.sem, act.n), (pe.sem, pe.n)]
            ar.at = mark0

            r, k, v, ld, cum, a, g, kk, bon, t1, t2 = (
                z.rearrange("p (c t) -> p c t", c=4) for z in (r_, k_, v_, ld_, cum_, a_, g_, kk_, bon_, t1_, t2_))

            @block.scalar
            def _(_e):
                for point in swa_done:
                    A.wait_ge(*point)
                A.activation(wa[0:64, :], wa[0:64, :], ACT.Tanh)
                Ring.p = act.count(A.activation(glo, glo, ACT.Sigmoid).then_inc(act.sem, 1))
            wps, aps, gps = (banks(2 * n, 2).rearrange("p (c t) -> p c t", c=4) for n in range(3))

            @block.tensor
            def _(_e):
                E.wait_ge(*Ring.p)
                for point in swa_done:
                    E.wait_ge(*point)
                wa2, g2 = prm("wa2"), prm("g2")
                for c in range(4):
                    cs = slice(c * P, (c + 1) * P)
                    E.matmul(wps[:, c, :], wa2[0:64, cs], wa[0:64, :], start=True, stop=True)
                    E.matmul(aps[:, c, :], wa2[64:128, cs], wa[64:128, :], start=True, stop=True)
                    ins = E.matmul(gps[:, c, :], g2[:, cs], glo, start=True, stop=True)
                Ring.p = pe.count(ins.then_inc(pe.sem, 1))

            @block.scalar
            def _(_e):
                A.wait_ge(*Ring.p)
                for c in range(4):
                    A.activation(ld[:, c, :], wps[:, c, :], ACT.Sigmoid, bias=prm("w0")[:, c:c + 1])
                Ring.q = act.count(A.activation(a[:, 0, :], aps[:, 0, :], ACT.Sigmoid, bias=prm("a0")[:, 0:1]).then_inc(act.sem, 1))
                for c in range(1, 4):
                    A.activation(a[:, c, :], aps[:, c, :], ACT.Sigmoid, bias=prm("a0")[:, c:c + 1])
                Ring.p = act.count(A.activation(g_, banks(4, 2), ACT.Copy).then_inc(act.sem, 1))

            @block.vector
            def _(_e):
                V.wait_ge(*Ring.q)
                for point in swa_done:
                    V.wait_ge(*point)
                vl(V.tensor_scalar(ld_, ld_, -math.exp(-0.5), None, ALU.mult).then_inc(dve.sem, 1))
                for c in range(4):
                    V.tensor_tensor_scan(cum[:, c, :], cst("scan_keep"), ld[:, c, :], 0.0, ALU.mult, ALU.add)
                for c in range(4):
                    p = dve.count(V.tensor_scalar(kk[:, c, :], k[:, c, :], prm("k_k")[:, c:c + 1], None, ALU.mult).then_inc(dve.sem, 1))
                V.wait_ge(*p)
                Ring.q = vl(V.tensor_tensor(t1_, kk_, kk_, ALU.mult).then_inc(dve.sem, 1))

            def head_sum(src, ready_):
                @block.tensor
                def _(_e):
                    E.wait_ge(*ready_)
                    for h in range(2):
                        ins = E.matmul(bank(6 + h), cst("headsum"), src[:, h * 512:(h + 1) * 512], start=True, stop=True)
                    Ring.p = pe.count(ins.then_inc(pe.sem, 1))
                return Ring.p

            act_gate = Ring.p
            p = head_sum(t1_, Ring.q)

            @block.scalar
            def _(_e):
                A.wait_ge(*p)
                Ring.p = act.count(A.activation(t2_, banks(6, 2), ACT.Sqrt).then_inc(act.sem, 1))

            @block.vector
            def _(_e):
                V.wait_ge(*Ring.p)
                V.wait_ge(*act_gate)
                vl(V.tensor_scalar(t2_, t2_, 1e-12, None, ALU.max).then_inc(dve.sem, 1))
                vl(V.reciprocal(t2_, t2_).then_inc(dve.sem, 1))
                vl(V.tensor_tensor(kk_, kk_, t2_, ALU.mult).then_inc(dve.sem, 1))
                for c in range(4):
                    p_ = dve.count(V.tensor_scalar(t1[:, c, :], a[:, c, :], prm("k_a")[:, c:c + 1], omka[:, c:c + 1],
                                                  ALU.mult, ALU.add).then_inc(dve.sem, 1))
                V.wait_ge(*p_)
                vl(V.tensor_tensor(k_, k_, t1_, ALU.mult).then_inc(dve.sem, 1))
                vl(V.scalar_tensor_tensor(a_, kk_, -1.0, a_, ALU.mult, ALU.mult).then_inc(dve.sem, 1))
                for c in range(4):
                    p_ = dve.count(V.scalar_tensor_tensor(t1[:, c, :], r[:, c, :], prm("r_k")[:, c:c + 1], k[:, c, :],
                                                         ALU.mult, ALU.mult).then_inc(dve.sem, 1))
                Ring.q = p_
            p = head_sum(t1_, Ring.q)

            @block.vector
            def _(_e):
                V.wait_ge(*p)
                vl(V.tensor_tensor(bon_, banks(6, 2), v_, ALU.mult).then_inc(dve.sem, 1))
                Ring.q = vl(V.tensor_tensor(t1_, cum_, ld_, ALU.subtract).then_inc(dve.sem, 1))

            @block.scalar
            def _(_e):
                A.wait_ge(*Ring.q)
                A.activation(t1_, t1_, ACT.Exp)
                A.activation(t2_, cum_, ACT.Exp, scale=-1.0)
                al(A.activation(ld_, cum_, ACT.Exp).then_inc(act.sem, 1))
                Ring.q = (act.sem, act.n)
            e1 = ld

            @block.vector
            def _(_e):
                V.wait_ge(*Ring.q)
                V.tensor_tensor(kk_, kk_, t1_, ALU.mult)
                V.tensor_tensor(a_, a_, t2_, ALU.mult)
                V.tensor_tensor(k_, k_, t2_, ALU.mult)
                Ring.q = vl(V.tensor_tensor(r_, r_, ld_, ALU.mult).then_inc(dve.sem, 1))
            scaled = Ring.q
            kap, bet, kh, rh = kk, a, k, r

            vt = htok_[:, 0:1024].rearrange("p (t d) -> p t d", t=NT)
            bt = htok_[:, 1024:2048].rearrange("p (t d) -> p t d", t=NT)
            kt = cum_.rearrange("p (t d) -> p t d", t=NT)
            n = 0
            for src, dst in ((v, vt), (bet, bt), (kh, kt)):
                for t in range(NT):
                    @block.tensor
                    def _(_e):
                        E.wait_ge(*scaled)
                        for c in range(4):
                            ins = E.transpose(bank(n)[:, c * P:(c + 1) * P], src[:, c, t * P:(t + 1) * P], ident)
                        Ring.p = pe.count(ins.then_inc(pe.sem, 1))

                    @block.scalar
                    def _(_e):
                        A.wait_ge(*Ring.p)
                        Ring.p = act.count(A.activation(dst[:, t, :], bank(n), ACT.Copy).then_inc(act.sem, 1))
                    n += 1
            tok_done = Ring.p

            def mat(t, h):
                return 8 * t + 4 * (h % 2) + h // 2

            L, LT, X, XT, A2 = (ar.take(16 * P).rearrange("p (m s) -> p m s", m=16) for _ in range(5))
            L_, LT_, X_, XT_, A2_ = (z.rearrange("p m s -> p (m s)") for z in (L, LT, X, XT, A2))
            bank_free = [tok_done] * 8

            def gram(lhs, rhs, mask, dst, first, ready_):
                for q in range(4):
                    b = first + q

                    @block.tensor
                    def _(_e):
                        for point in ready_:
                            E.wait_ge(*point)
                        E.wait_ge(*bank_free[b])
                        for m in range(4 * q, 4 * q + 4):
                            t, h = m // 8, 2 * (m % 4) + (m // 4) % 2
                            hs, ts = slice((h % 2) * HD, (h % 2 + 1) * HD), slice(t * P, (t + 1) * P)
                            ins = E.matmul(bank(b)[:, (m % 4) * P:(m % 4 + 1) * P], lhs[hs, h // 2, ts],
                                           rhs[hs, h // 2, ts], start=True, stop=True)
                        Ring.p = pe.count(ins.then_inc(pe.sem, 1))

                    @block.vector
                    def _(_e):
                        V.wait_ge(*Ring.p)
                        bank_free[b] = dve.count(V.tensor_tensor(
                            dst[:, 4 * q:4 * q + 4, :], bank(b).rearrange("p (m s) -> p m s", m=4),
                            spread(mask.rearrange("p (o s) -> p o s", o=1), [P, 4, P]), ALU.mult).then_inc(dve.sem, 1))
                return bank_free[first + 3]

            gram(kap, bet, cst("lower"), L, 0, [scaled])
            gram(bet, kap, cst("upper"), LT, 4, [scaled])
            lev = cst("level").rearrange("p (l s) -> p l s", l=LEVELS)
            levt = cst("level_t").rearrange("p (l s) -> p l s", l=LEVELS)

            def levels(m):
                return spread(m.rearrange("p (o s) -> p o s", o=1), [P, 16, P])

            @block.vector
            def _(_e):
                V.wait_ge(dve.sem, dve.n)
                V.tensor_tensor(X, L, levels(lev[:, 0, :]), ALU.mult)
                vl(V.tensor_tensor(XT, LT, levels(levt[:, 0, :]), ALU.mult).then_inc(dve.sem, 1))
                V.tensor_tensor(X, X, levels(ident), ALU.add)
                Ring.q = vl(V.tensor_tensor(XT, XT, levels(ident), ALU.add).then_inc(dve.sem, 1))
            LM = arena[:, t1_.offset if False else 9 * 1024:11 * 1024]
            LMv = LM.rearrange("p (m s) -> p m s", m=16)
            x_ready = Ring.q
            lm_free = x_ready
            for l in range(1, LEVELS):
                lm_pts, t_pts = [], []
                for q in range(4):
                    @block.vector
                    def _(_e):
                        V.wait_ge(*lm_free)
                        lm_pts.append(dve.count(V.tensor_tensor(
                            LMv[:, 4 * q:4 * q + 4, :], LT[:, 4 * q:4 * q + 4, :],
                            spread(levt[:, l:l + 1, :], [P, 4, P]), ALU.mult).then_inc(dve.sem, 1)))
                for q in range(4):
                    @block.tensor
                    def _(_e):
                        E.wait_ge(*lm_pts[q])
                        E.wait_ge(*x_ready)
                        E.wait_ge(*bank_free[q])
                        for m in range(4 * q, 4 * q + 4):
                            ins = E.matmul(bank(q)[:, (m % 4) * P:(m % 4 + 1) * P], LMv[:, m, :], X[:, m, :],
                                           start=True, stop=True)
                        Ring.p = pe.count(ins.then_inc(pe.sem, 1))

                    @block.scalar
                    def _(_e):
                        A.wait_ge(*Ring.p)
                        A.wait_ge(*x_ready)
                        t_pts.append(act.count(A.activation(A2_[:, q * 512:(q + 1) * 512], bank(q), ACT.Copy).then_inc(act.sem, 1)))
                lm_free = Ring.p
                upd = []
                for lhs, rhs, dst, first in ((XT, A2, X_, 4), (A2, XT, XT_, 0)):
                    for q in range(4):
                        @block.tensor
                        def _(_e):
                            E.wait_ge(*t_pts[q])
                            E.wait_ge(*bank_free[first + q])
                            for m in range(4 * q, 4 * q + 4):
                                ins = E.matmul(bank(first + q)[:, (m % 4) * P:(m % 4 + 1) * P], lhs[:, m, :],
                                               rhs[:, m, :], start=True, stop=True)
                            upd.append((pe.count(ins.then_inc(pe.sem, 1)), dst, first + q, q))
                for p, dst, b, q in upd:
                    @block.vector
                    def _(_e):
                        V.wait_ge(*upd[q + 4][0])
                        bank_free[b] = dve.count(V.tensor_tensor(dst[:, q * 512:(q + 1) * 512],
                                                                dst[:, q * 512:(q + 1) * 512], bank(b), ALU.add).then_inc(dve.sem, 1))
                x_ready = bank_free[3]
            inv_done = [x_ready, (pe.sem, pe.n)]
            MT, A1 = L, LT

            @block.vector
            def _(_e):
                for point in inv_done:
                    V.wait_ge(*point)
                V.wait_ge(act.sem, act.n)
            gram(kh, kap, cst("upper"), MT, 0, inv_done)
            gram(bet, rh, cst("upper_in"), A1, 4, inv_done)
            gram(kh, rh, cst("upper_in"), A2, 0, inv_done)
            gram_done = (dve.sem, dve.n)
            ST = ar.take(4 * HD).rearrange("p (c i) -> p c i", c=4)
            MV = X_[:, 0:1024].rearrange("p (t d) -> p t d", t=NT)
            Pv, Uv = t1_[:, 0:512], t1_[:, 512:1024]
            y = t2

            @block.tensor
            def _(_e):
                E.wait_ge(*gram_done)
                for t in range(NT):
                    for h in range(8):
                        hc = slice(h * HD, (h + 1) * HD)
                        E.matmul(bank(4 + t)[:, hc], MT[:, mat(t, h), :], vt[:, t, hc], start=True, stop=True)
                    for h in range(8):
                        ps, hc = slice((h % 2) * HD, (h % 2 + 1) * HD), slice(h * HD, (h + 1) * HD)
                        ins = E.matmul(bank(6 + t)[ps, (h // 2) * P:(h // 2 + 1) * P], vt[:, t, hc],
                                       A2[:, mat(t, h), :], start=True, stop=True)
                Ring.p = pe.count(ins.then_inc(pe.sem, 1))

            @block.vector
            def _(_e):
                V.wait_ge(*Ring.p)
                V.wait_ge(*gram_done)
                V.memset(ST, 0.0)
                V.tensor_copy(MV, banks(4, 2).rearrange("p (t d) -> p t d", t=NT))
                for t in range(NT):
                    Ring.q = vl(V.tensor_copy(y[:, :, t * P:(t + 1) * P], bank(6 + t).rearrange("p (c n) -> p c n", c=4)).then_inc(dve.sem, 1))
            s_ready = Ring.q
            for c4 in range(T // C64):
                t, hb = c4 // 2, (c4 % 2) * 64
                hs = slice(hb, hb + 64)
                tok = slice(t * P + hb, t * P + hb + 64)

                @block.tensor
                def _(_e):
                    E.wait_ge(*s_ready)
                    for h in (0, 2, 4, 6, 1, 3, 5, 7):
                        ps, c = slice((h % 2) * HD, (h % 2 + 1) * HD), h // 2
                        ins = E.matmul(bank(h % 2)[hs, c * HD:(c + 1) * HD], kap[ps, c, tok], ST[ps, c, :],
                                       start=True, stop=True)
                    Ring.p = pe.count(ins.then_inc(pe.sem, 1))

                @block.vector
                def _(_e):
                    V.wait_ge(*Ring.p)
                    for o in range(2):
                        Ring.q = dve.count(V.tensor_tensor(
                            Pv[hs, :].rearrange("p (c o i) -> p c o i", o=2, i=HD)[:, :, o, :],
                            bank(o)[hs, 0:T].rearrange("p (c i) -> p c i", c=4),
                            MV[hs, t, :].rearrange("p (c o i) -> p c o i", o=2, i=HD)[:, :, o, :], ALU.add).then_inc(dve.sem, 1))

                @block.tensor
                def _(_e):
                    E.wait_ge(*Ring.q)
                    for h in range(8):
                        ins = E.matmul(bank(2)[hs, h * HD:(h + 1) * HD], XT[hs, mat(t, h), hs],
                                       Pv[hs, h * HD:(h + 1) * HD], start=True, stop=True)
                    Ring.p = pe.count(ins.then_inc(pe.sem, 1))

                @block.vector
                def _(_e):
                    V.wait_ge(*Ring.p)
                    Ring.q = dve.count(V.tensor_copy(Uv[hs, :], bank(2)[hs, :]).then_inc(dve.sem, 1))

                @block.tensor
                def _(_e):
                    E.wait_ge(*Ring.q)
                    for h in range(8):
                        ps, c = slice((h % 2) * HD, (h % 2 + 1) * HD), h // 2
                        o, hc = bank(3)[ps, c * HD:(c + 1) * HD], slice(h * HD, (h + 1) * HD)
                        E.matmul(o, bt[hs, t, hc], Uv[hs, hc], start=True, stop=False)
                        ins = E.matmul(o, kt[hs, t, hc], vt[hs, t, hc], start=False, stop=True)
                    Ring.p = pe.count(ins.then_inc(pe.sem, 1))
                    for h in range(8):
                        ps, c = slice((h % 2) * HD, (h % 2 + 1) * HD), h // 2
                        E.matmul(bank(6)[ps, c * HD:(c + 1) * HD], Uv[hs, h * HD:(h + 1) * HD],
                                 A1[hs, mat(t, h), hs], start=True, stop=True)
                    for h in (0, 2, 4, 6, 1, 3, 5, 7):
                        ps, c = slice((h % 2) * HD, (h % 2 + 1) * HD), h // 2
                        ins = E.matmul(bank(4 + h % 2)[ps, c * HD:(c + 1) * HD], ST[ps, c, :], rh[ps, c, tok],
                                       start=True, stop=True)
                    Ring.q = pe.count(ins.then_inc(pe.sem, 1))

                @block.vector
                def _(_e):
                    V.wait_ge(*Ring.q)
                    for o in range(2):
                        ps = slice(o * HD, (o + 1) * HD)
                        V.tensor_tensor(y[ps, :, tok], y[ps, :, tok],
                                        bank(4 + o)[ps, 0:T].rearrange("p (c n) -> p c n", c=4), ALU.add)
                    vl(V.tensor_tensor(ST, ST, bank(3)[:, 0:T].rearrange("p (c n) -> p c n", c=4), ALU.add).then_inc(dve.sem, 1))
                    V.tensor_tensor(y[:, :, tok], y[:, :, tok],
                                    bank(6)[:, 0:T].rearrange("p (c n) -> p c n", c=4), ALU.add)
                    Ring.q = vl(V.tensor_tensor(ST, ST, spread(e1[:, :, c4 * 64 + 63:c4 * 64 + 64], [P, 4, HD]), ALU.mult).then_inc(dve.sem, 1))
                s_ready = Ring.q

            p = head_sum(t2_, s_ready)

            @block.vector
            def _(_e):
                V.wait_ge(*p)
                Ring.q = vl(V.scalar_tensor_tensor(t2_, banks(6, 2), -1.0 / HD, t2_, ALU.mult, ALU.add).then_inc(dve.sem, 1))

            @block.scalar
            def _(_e):
                A.wait_ge(*Ring.q)
                Ring.q = act.count(A.activation(t1_, t2_, ACT.Square).then_inc(act.sem, 1))
            p = head_sum(t1_, Ring.q)

            @block.vector
            def _(_e):
                V.wait_ge(*p)
                Ring.q = vl(V.tensor_scalar(t1_, banks(6, 2), 1.0 / HD, 64e-5, ALU.mult, ALU.add).then_inc(dve.sem, 1))

            @block.scalar
            def _(_e):
                A.wait_ge(*Ring.q)
                Ring.q = act.count(A.activation(t1_, t1_, ACT.Sqrt).then_inc(act.sem, 1))

            @block.vector
            def _(_e):
                V.wait_ge(*Ring.q)
                vl(V.reciprocal(t1_, t1_).then_inc(dve.sem, 1))
                vl(V.tensor_tensor(t2_, t2_, t1_, ALU.mult).then_inc(dve.sem, 1))
                for c in range(4):
                    p_ = dve.count(V.tensor_scalar(t2[:, c, :], t2[:, c, :], prm("ln_g")[:, c:c + 1],
                                                  prm("ln_b")[:, c:c + 1], ALU.mult, ALU.add).then_inc(dve.sem, 1))
                V.wait_ge(*p_)
                vl(V.tensor_tensor(t2_, t2_, bon_, ALU.add).then_inc(dve.sem, 1))
                Ring.q = vl(V.tensor_tensor(oT[:, 4:8, :], t2, g, ALU.mult).then_inc(dve.sem, 1))
            done = out_project("w_hy_out", 8, oT, [Ring.q])
            r_row = row_of(prm("mix_post_g0"), 1.0, [])
            return add_normed(done + [r_row])

        def nsa(ready):
            h_ready = norm_transpose(prm("mix_pre_g1"), None, ready)
            ar = Arena()
            qT = ar.take(8 * T).rearrange("p (c t) -> p c t", c=8)
            kc2, vc2, ksT, kwT = (ar.take(4 * T).rearrange("p (c t) -> p c t", c=4) for _ in range(4))
            vs, vw = (ar.take(NT * T).rearrange("p (t d) -> p t d", t=NT) for _ in range(2))
            gates = ar.take(NT * 48).rearrange("p (t n) -> p t n", t=NT)

            def evac(c, b, p):
                @block.scalar
                def _(_e):
                    A.wait_ge(*p)
                    bt = b[:, 0:T]
                    if c < 8:
                        ins = A.activation(qT[:, c, :], bt, ACT.Copy, scale=HD ** -0.5)
                    elif c < 16:
                        dst = (kc2, vc2)[(c - 8) // 4][:, (c - 8) % 4, :]
                        A.activation(dst[0:64, :], bt[0:64, :], ACT.Copy)
                        ins = A.activation(dst[64:128, 0:T - 1], bt[64:128, 1:T], ACT.Copy)
                    elif c < 24:
                        ins = A.activation((ksT, kwT)[(c - 16) // 4][:, (c - 16) % 4, :], bt, ACT.Copy)
                    elif c < 28:
                        m = c - 24
                        ins = A.activation((vs, vw)[m // 2][:, :, (m % 2) * P:(m % 2 + 1) * P],
                                           bt.rearrange("p (t d) -> p t d", t=NT), ACT.Copy)
                    else:
                        ins = A.activation(gates, b[:, 0:96].rearrange("p (t n) -> p t n", t=NT), ACT.Sigmoid)
                    Ring.q = act.count(ins.then_inc(act.sem, 1))
                return (Ring.q,)

            project("w_ns_in", 29, evac, h_ready, tokens=(24, 25, 26, 27, 28), widths={28: 48})
            projected = [(act.sem, act.n), (pe.sem, pe.n)]
            oT = hT
            blk = [ar.take(16 * 4 * N_CMP).rearrange("p (j g c) -> p j g c", j=16, g=4) for _ in range(2)]
            hdn = [ar.take(2 * 4 * N_CMP).rearrange("p (f n) -> p f n", f=2) for _ in range(2)]
            kcmp = ar.take(4 * N_CMP).rearrange("p (g c) -> p g c", g=4)
            vcmp = ar.take(4 * HD).rearrange("p (g d) -> p g d", g=4)
            gcmp = ar.take(NT * 16).rearrange("p (t h) -> p t h", t=NT)

            @block.vector
            def _(_e):
                for point in projected:
                    V.wait_ge(*point)
                for kv in range(2):
                    src, pos = (kc2, vc2)[kv], prm("pos_" + "kv"[kv])
                    for j in range(16):
                        p = dve.count(V.tensor_scalar(blk[kv][:, j, :, :], src[:, :, 2 * j:2 * j + 16 * (N_CMP - 1) + 1:16],
                                                     pos[:, j:j + 1], None, ALU.add).then_inc(dve.sem, 1))
                for t in range(NT):
                    p = dve.count(V.tensor_scalar(gcmp[:, t, :], gates[:, t, 0:48:3], cst(f"cmp_any{t}"), None, ALU.mult).then_inc(dve.sem, 1))
                Ring.q = p
            blocks_ready = Ring.q
            for kv in range(2):
                pts = []
                for half in range(2):
                    s, full = load(dram["w_cmp1"][2 * kv + half:2 * kv + half + 1], 1)
                    w = slot_ap(s, 2048).rearrange("p (j f) -> p j f", j=8)
                    pts.append((s, w, full))

                @block.tensor
                def _(_e):
                    E.wait_ge(*blocks_ready)
                    E.wait_ge(*pts[0][2])
                    E.wait_ge(*pts[1][2])
                    for f in range(2):
                        for j in range(16):
                            ins = E.matmul(bank(4 + f)[:, kv * 64:kv * 64 + 60], pts[j // 8][1][:, j % 8, f * P:(f + 1) * P],
                                           blk[kv][:, j, :, :], start=j == 0, stop=j == 15)
                    Ring.p = pe.count(ins.then_inc(pe.sem, 1))
                Ring.used[pts[0][0]] = Ring.used[pts[1][0]] = Ring.p

                @block.scalar
                def _(_e):
                    A.wait_ge(*Ring.p)
                    for f in range(2):
                        ins = A.activation(hdn[kv][:, f, :], bank(4 + f)[:, kv * 64:kv * 64 + 60], ACT.Gelu_apprx_tanh)
                    Ring.q = act.count(ins.then_inc(act.sem, 1))

                @block.tensor
                def _(_e):
                    E.wait_ge(*Ring.q)
                    if kv == 0:
                        w2 = prm("cw2_k").rearrange("p (f n) -> p f n", f=2)
                        for f in range(2):
                            ins = E.matmul(bank(6)[:, 0:60], w2[:, f, :], hdn[0][:, f, :], start=f == 0, stop=f == 1)
                    else:
                        w2 = prm("cw2_v").rearrange("p (f n) -> p f n", f=2)
                        for gq in range(4):
                            for f in range(2):
                                ins = E.matmul(bank(7)[0:N_CMP, gq * HD:(gq + 1) * HD],
                                               hdn[1][:, f, gq * N_CMP:(gq + 1) * N_CMP], w2[:, f, :],
                                               start=f == 0, stop=f == 1)
                    Ring.p = pe.count(ins.then_inc(pe.sem, 1))

                @block.scalar
                def _(_e):
                    A.wait_ge(*Ring.p)
                    if kv == 0:
                        al(A.activation(kcmp, bank(6)[:, 0:60].rearrange("p (g c) -> p g c", g=4), ACT.Copy).then_inc(act.sem, 1))
                    else:
                        al(A.activation(vcmp[0:N_CMP], bank(7)[0:N_CMP, 0:4 * HD].rearrange("p (g d) -> p g d", g=4), ACT.Copy).then_inc(act.sem, 1))
            slopes = alibi(16)
            units = []
            for gq in range(4):
                for t in range(NT):
                    parts = []
                    for br in range(3):
                        kk_ = (kcmp, ksT, kwT)[br]
                        nk = N_CMP if br == 0 else (t + 1) * P
                        u = dict(branch=br, scale=1.0, slopes=slopes[4 * gq:4 * gq + 4], keys=nk,
                                 blocks=1 if br == 0 else t + 1, last=br == 2,
                                 dist=cst(f"cmp{t}") if br == 0 else cst(f"causal{t}"),
                                 gates=gcmp[:, t, 4 * gq:4 * gq + 4] if br == 0 else
                                 gates[:, t, 12 * gq + br:12 * gq + 12:3],
                                 q=lambda i, gq=gq, t=t: qT[(i % 2) * HD:(i % 2 + 1) * HD, 2 * gq + i // 2, t * P:(t + 1) * P],
                                 k=lambda i, gq=gq, nk=nk, kk_=kk_: kk_[(i % 2) * HD:(i % 2 + 1) * HD, gq, 0:nk],
                                 out=oT[:, 2 * gq:2 * gq + 2, t * P:(t + 1) * P])
                        if br == 0:
                            u["v"] = lambda i, b, gq=gq: vcmp[0:N_CMP, gq, :]
                        else:
                            u["v"] = lambda i, b, gq=gq, br=br: (vs, vw)[br - 1][:, b, gq * HD:(gq + 1) * HD]
                        parts.append(u)
                        units.append(u)
                    parts[-1]["parts"] = parts
            o_ready = attend(units, ar, T, [(act.sem, act.n), (dve.sem, dve.n), (pe.sem, pe.n)])
            done = out_project("w_ns_out", 8, oT, o_ready)
            r_row = row_of(prm("mix_post_g1"), 1.0, o_ready)
            return add_normed(done + [r_row])

        def conv_ffn(l, ready):
            h_ready = norm_transpose(prm(f"ffn_pre_g{l}"), None, ready)
            r_row = row_of(prm(f"ffn_post_g{l}"), 1.0, h_ready)
            done = ffn(f"w_conv{l}", h_ready + [r_row], conv=l, mod=l)
            return add_normed(done)

        cond = small[:, 40:48]
        gm = small[:, 48:56]

        def mod_col(l, s, kind):
            a = l * 72 + (3 * s + kind) * 8
            return modT[:, a:a + 8]

        def modulated(l, s, ready):
            @block.vector
            def _(_e):
                for point in ready:
                    V.wait_ge(*point)
                vl(V.tensor_scalar(gm, mod_col(l, s, 1), 1.0, None, ALU.add).then_inc(dve.sem, 1))
                Ring.q = vl(V.tensor_tensor(gm, gm, prm(f"norm_g{l}{s}"), ALU.mult).then_inc(dve.sem, 1))
            return norm_transpose(gm, mod_col(l, s, 0), list(ready) + [Ring.q])

        def silu_ffn(l, s, w, ready):
            h_ready = modulated(l, s, ready)
            r_row = row_of(mod_col(l, s, 2), 0.5, h_ready)
            done = ffn(f"w_ffn{l}{w}", h_ready + [r_row])
            return add_gated(done + [r_row])

        def ssd(ready):
            h_ready = modulated(0, 1, ready)
            ar = Arena()
            zs_ = ar.take(16 * T)
            xb_ = ar.take(32 * T)
            zs, xb = (z.rearrange("p (c t) -> p c t", t=T) for z in (zs_, xb_))
            xt = ar.take(NT * 2048).rearrange("p (t d) -> p t d", t=NT)
            base = ar.at
            pad = [ar.take(T + 4) for _ in range(2)]
            cv = [ar.take(T) for _ in range(2)]
            dt, dtA, acum = (ar.take(NT * 64) for _ in range(3))
            tmp = [ar.take(NT * 64) for _ in range(3)]
            acT = ar.take(T)
            Arow = ar.take(64)
            d3 = lambda z: z.rearrange("p (t n) -> p t n", t=NT)

            @block.vector
            def _(_e):
                for point in h_ready:
                    V.wait_ge(*point)
                for q in range(2):
                    V.memset(pad[q][:, 0:2], 0.0)
                    vl(V.memset(pad[q][:, T + 2:T + 4], 0.0).then_inc(dve.sem, 1))
            pad_ready = (dve.sem, dve.n)
            cv_free = [loaded] * 2

            def evac(c, b, p):
                if c < 16:
                    @block.scalar
                    def _(_e):
                        A.wait_ge(*p)
                        A.wait_ge(*pad_ready)
                        Ring.q = act.count(A.activation(zs[:, c, :], b[:, 0:T], ACT.Silu).then_inc(act.sem, 1))
                    return (Ring.q,)
                if c < 48:
                    m = c - 16
                    q = m % 2

                    @block.scalar
                    def _(_e):
                        A.wait_ge(*p)
                        A.wait_ge(*cv_free[q])
                        Ring.q = act.count(A.activation(pad[q][:, 2:T + 2], b[:, 0:T], ACT.Copy).then_inc(act.sem, 1))
                    freed = Ring.q

                    @block.vector
                    def _(_e):
                        V.wait_ge(*Ring.q)
                        V.wait_ge(*cv_silu[q])
                        vl(V.tensor_scalar(cv[q], pad[q][:, 0:T], prm("sconv_w0")[:, m:m + 1], None, ALU.mult).then_inc(dve.sem, 1))
                        for j in range(1, 5):
                            Ring.q = vl(V.scalar_tensor_tensor(cv[q], pad[q][:, j:j + T], prm(f"sconv_w{j}")[:, m:m + 1],
                                                               cv[q], ALU.mult, ALU.add).then_inc(dve.sem, 1))
                    cv_free[q] = Ring.q
                    pend.append((m, q, Ring.q))
                    if len(pend) > 1:
                        silu_out()
                    return (freed,)
                while pend:
                    silu_out()

                @block.vector
                def _(_e):
                    V.wait_ge(*p)
                    bias = prm("dt_bias")
                    bb = spread(bias.rearrange("p (o n) -> p o n", o=1), [P, NT, 64])
                    vl(V.tensor_tensor(d3(dt), d3(b[:, 0:2 * 64]), bb, ALU.add).then_inc(dve.sem, 1))
                    vl(V.tensor_scalar(tmp[0], dt, -1.0, None, ALU.mult).then_inc(dve.sem, 1))
                    Ring.q = vl(V.tensor_tensor(tmp[0], tmp[0], dt, ALU.min).then_inc(dve.sem, 1))
                return (Ring.q,)

            pend, cv_silu = [], [loaded] * 2

            def silu_out():
                m, q, p = pend.pop(0)

                @block.scalar
                def _(_e):
                    A.wait_ge(*p)
                    cv_silu[q] = act.count(A.activation(xb[:, m, :], cv[q], ACT.Silu, bias=prm("sconv_b")[:, m:m + 1]).then_inc(act.sem, 1))

            project("w_ssd_in", 49, evac, h_ready, tokens=(48,), widths={48: 64})
            neg_abs = Ring.q

            @block.scalar
            def _(_e):
                A.wait_ge(*neg_abs)
                A.activation(Arow, prm("a_log"), ACT.Exp)
                Ring.q = al(A.activation(tmp[0], tmp[0], ACT.Exp).then_inc(act.sem, 1))

            @block.vector
            def _(_e):
                V.wait_ge(*Ring.q)
                vl(V.tensor_scalar(tmp[1], tmp[0], 2.0, None, ALU.add).then_inc(dve.sem, 1))
                vl(V.reciprocal(tmp[1], tmp[1]).then_inc(dve.sem, 1))
                vl(V.tensor_tensor(tmp[0], tmp[0], tmp[1], ALU.mult).then_inc(dve.sem, 1))
                vl(V.tensor_tensor(tmp[1], tmp[0], tmp[0], ALU.mult).then_inc(dve.sem, 1))
                vl(V.tensor_scalar(tmp[2], tmp[1], 1.0 / 17, 1.0 / 15, ALU.mult, ALU.add).then_inc(dve.sem, 1))
                for n in range(13, 0, -2):
                    vl(V.tensor_tensor(tmp[2], tmp[2], tmp[1], ALU.mult).then_inc(dve.sem, 1))
                    vl(V.tensor_scalar(tmp[2], tmp[2], 1.0 / n, None, ALU.add).then_inc(dve.sem, 1))
                vl(V.tensor_tensor(tmp[2], tmp[2], tmp[0], ALU.mult).then_inc(dve.sem, 1))
                vl(V.tensor_scalar(dt, dt, 0.0, None, ALU.max).then_inc(dve.sem, 1))
                vl(V.scalar_tensor_tensor(dt, tmp[2], 2.0, dt, ALU.mult, ALU.add).then_inc(dve.sem, 1))
                Ring.q = vl(V.scalar_tensor_tensor(d3(dtA), d3(dt), -1.0,
                                                   spread(Arow.rearrange("p (o n) -> p o n", o=1), [P, NT, 64]),
                                                   ALU.mult, ALU.mult).then_inc(dve.sem, 1))
            trif, trib = (cst(n).rearrange("p (u t) -> p u t", u=NT) for n in ("tri_f", "tri_b"))
            in_done = [Ring.q, (act.sem, act.n), (pe.sem, pe.n)]

            @block.tensor
            def _(_e):
                for point in in_done:
                    E.wait_ge(*point)
                for t in range(NT):
                    for d, tri in enumerate((trif, trib)):
                        for u in range(NT):
                            E.matmul(bank(0)[:, t * 64 + d * 32:t * 64 + d * 32 + 32], tri[:, u, t * P:(t + 1) * P],
                                     d3(dtA)[:, u, d * 32:(d + 1) * 32], start=u == 0, stop=u == NT - 1)
                for d, tri in enumerate((trif, trib)):
                    for u in range(NT):
                        ins = E.matmul(bank(1)[d * 32:(d + 1) * 32, 0:T], d3(dtA)[:, u, d * 32:(d + 1) * 32],
                                       tri[:, u, :], start=u == 0, stop=u == NT - 1)
                Ring.p = pe.count(ins.then_inc(pe.sem, 1))

            @block.vector
            def _(_e):
                V.wait_ge(*Ring.p)
                V.tensor_copy(acum, bank(0)[:, 0:NT * 64])
                Ring.q = vl(V.tensor_copy(acT[0:64, :], bank(1)[0:64, 0:T]).then_inc(dve.sem, 1))
            ac_ready = Ring.q
            freed = [loaded] * 4
            for n in range(8):
                t, c0 = n // 4, (n % 4) * 4

                @block.tensor
                def _(_e):
                    for point in in_done:
                        E.wait_ge(*point)
                    E.wait_ge(*freed[n % 4])
                    for c in range(4):
                        ins = E.transpose(bank(4 + n % 4)[:, c * P:(c + 1) * P], xb[:, c0 + c, t * P:(t + 1) * P], ident)
                    Ring.p = pe.count(ins.then_inc(pe.sem, 1))

                @block.scalar
                def _(_e):
                    A.wait_ge(*Ring.p)
                    freed[n % 4] = act.count(A.activation(xt[:, t, c0 * P:(c0 + 4) * P], bank(4 + n % 4), ACT.Copy).then_inc(act.sem, 1))
            xt_ready = freed[3]
            ar.at = base + 2 * (T + 4) + 2 * T + 6 * NT * 64 + T + 64
            G_ = [ar.take(768) for _ in range(2)]
            xd = [ar.take(NT * 2 * T).rearrange("p (u d n) -> p u d n", u=NT, d=2) for _ in range(2)]
            ee = [ar.take(768) for _ in range(3)]
            ee_free, g_free, arow_free, y_free = [loaded] * 3, [loaded] * 2, [loaded] * 2, [loaded] * 2
            ee_ready = [loaded] * 3
            acu, dt3 = d3(acum), d3(dt)
            negf, negb = cst("neg_f"), cst("neg_b")
            g_state = {}

            def group(gi):
                q = gi % 2

                @block.tensor
                def _(_e):
                    E.wait_ge(*xt_ready)
                    E.wait_ge(*ac_ready)
                    E.wait_ge(*g_free[q])
                    E.wait_ge(*g_state.get("psum", loaded))
                    for u in range(NT):
                        ins = E.matmul(bank(4)[:, u * T:(u + 1) * T], xb[:, 16 + gi, u * P:(u + 1) * P],
                                       xb[:, 24 + gi, :], start=True, stop=True)
                    Ring.p = pe.count(ins.then_inc(pe.sem, 1))

                @block.scalar
                def _(_e):
                    A.wait_ge(*Ring.p)
                    A.wait_ge(*g_free[q])
                    b = bank(4)
                    A.activation(G_[q][:, 0:256], b[:, 0:256], ACT.Copy)
                    A.activation(G_[q][:, 256:384], b[:, 384:512], ACT.Copy)
                    A.activation(G_[q][:, 384:512], b[:, 0:128], ACT.Copy)
                    Ring.q = act.count(A.activation(G_[q][:, 512:768], b[:, 256:512], ACT.Copy).then_inc(act.sem, 1))
                g_state["psum"] = g_state["G", q] = Ring.q

                @block.vector
                def _(_e):
                    V.wait_ge(*xt_ready)
                    V.wait_ge(*ac_ready)
                    V.wait_ge(*g_free[q])
                    for u in range(NT):
                        for d in range(2):
                            dd = dt3[:, u, d * 32 + 4 * gi:d * 32 + 4 * gi + 4].rearrange("p (r o) -> p r o", o=1)
                            Ring.q = dve.count(V.tensor_tensor(
                                xd[q][:, u, d, :].rearrange("p (r n) -> p r n", r=4),
                                xt[:, u, gi * T:(gi + 1) * T].rearrange("p (r n) -> p r n", r=4),
                                spread(dd, [P, 4, HD]), ALU.mult).then_inc(dve.sem, 1))
                g_state["x", q] = Ring.q

            def front(h):
                b = bank(h % 2)
                e = ee[h % 3]

                @block.tensor
                def _(_e):
                    E.wait_ge(*ac_ready)
                    E.wait_ge(*arow_free[h % 2])
                    for d in range(2):
                        ins = E.matmul(b[:, d * T:(d + 1) * T], spread(ident[0:64, d * 32 + h:d * 32 + h + 1], [64, P]),
                                       acT[0:64, :], start=True, stop=True)
                    Ring.p = pe.count(ins.then_inc(pe.sem, 1))

                @block.vector
                def _(_e):
                    V.wait_ge(*Ring.p)
                    V.wait_ge(*ee_free[h % 3])
                    for lo, w, src, u, d, neg in ((0, 128, 0, 0, 0, negf), (256, 128, 128, 1, 0, negf),
                                                  (384, 128, T, 0, 1, negb), (640, 128, T + 128, 1, 1, negb)):
                        V.scalar_tensor_tensor(e[:, lo:lo + w], b[:, src:src + w], acu[:, u, d * 32 + h:d * 32 + h + 1],
                                               neg, ALU.subtract, ALU.add)
                    V.tensor_scalar(e[:, 128:256], b[:, 128:256], acu[:, 0, h:h + 1], None, ALU.subtract)
                    arow_free[h % 2] = dve.count(V.tensor_scalar(e[:, 512:640], b[:, T:T + 128],
                                                                acu[:, 1, 32 + h:33 + h], None, ALU.subtract).then_inc(dve.sem, 1))

                @block.scalar
                def _(_e):
                    A.wait_ge(*arow_free[h % 2])
                    ee_ready[h % 3] = act.count(A.activation(e, e, ACT.Exp).then_inc(act.sem, 1))

            def back(h):
                gi, rr, q = h // 4, h % 4, (h // 4) % 2
                e = ee[h % 3]

                @block.vector
                def _(_e):
                    V.wait_ge(*ee_ready[h % 3])
                    V.wait_ge(*g_state["G", q])
                    Ring.q = dve.count(V.tensor_tensor(e, e, G_[q], ALU.mult).then_inc(dve.sem, 1))
                hp = (h % 2) * HD
                yb = bank(2 + (h // 2) % 2)

                @block.tensor
                def _(_e):
                    E.wait_ge(*Ring.q)
                    E.wait_ge(*g_state["x", q])
                    E.wait_ge(*(y_free[(h // 2) % 2] if h % 2 == 0 else loaded))
                    o = yb[hp:hp + HD, 0:T]
                    xr = lambda u, d: xd[q][:, u, d, rr * HD:(rr + 1) * HD]
                    E.matmul(o, xr(0, 0), e[:, 0:256], start=True, stop=False)
                    E.matmul(o, xr(1, 1), e[:, 512:768], start=False, stop=False)
                    E.matmul(o[:, 128:256], xr(1, 0), e[:, 256:384], start=False, stop=False)
                    ins = E.matmul(o[:, 0:128], xr(0, 1), e[:, 384:512], start=False, stop=True)
                    ee_free[h % 3] = pe.count(ins.then_inc(pe.sem, 1))
                if h % 4 == 3:
                    g_free[q] = ee_free[h % 3]
                if h % 2:
                    c = h // 2

                    @block.vector
                    def _(_e):
                        V.wait_ge(*ee_free[h % 3])
                        y_free[c % 2] = vl(V.scalar_tensor_tensor(xb[:, c, :], xb[:, c, :], prm("d_skip")[:, c:c + 1],
                                                                  yb[:, 0:T], ALU.mult, ALU.add).then_inc(dve.sem, 1))
                        vl(V.tensor_tensor(xb[:, c, :], xb[:, c, :], zs[:, c, :], ALU.mult).then_inc(dve.sem, 1))

            group(0)
            for h in range(32):
                front(h)
                if h % 4 == 1 and h // 4 + 1 < 8:
                    group(h // 4 + 1)
                if h:
                    back(h - 1)
            back(31)
            y_done = [(dve.sem, dve.n), (pe.sem, pe.n)]

            sq = zs_
            inv = xt.rearrange("p t d -> p (t d)")[:, 0:2048]

            @block.scalar
            def _(_e):
                for point in y_done:
                    A.wait_ge(*point)
                Ring.q = act.count(A.activation(sq, xb_[:, 0:16 * T], ACT.Square).then_inc(act.sem, 1))
            ones = inv[:, 0:1]

            @block.vector
            def _(_e):
                for point in y_done:
                    V.wait_ge(*point)
                Ring.p = dve.count(V.memset(Arow[:, 0:1], 1.0).then_inc(dve.sem, 1))

            @block.tensor
            def _(_e):
                E.wait_ge(*Ring.q)
                E.wait_ge(*Ring.p)
                for gi in range(8):
                    for c in range(2):
                        ins = E.matmul(banks(gi // 2, 1)[:, (gi % 2) * T:(gi % 2 + 1) * T], spread(Arow[:, 0:1], [P, P]),
                                       zs[:, 2 * gi + c, :], start=c == 0, stop=c == 1)
                Ring.p = pe.count(ins.then_inc(pe.sem, 1))

            @block.vector
            def _(_e):
                V.wait_ge(*Ring.p)
                Ring.q = vl(V.tensor_scalar(inv, banks(0, 4), 1.0 / T, EPS, ALU.mult, ALU.add).then_inc(dve.sem, 1))

            @block.scalar
            def _(_e):
                A.wait_ge(*Ring.q)
                Ring.q = act.count(A.activation(inv, inv, ACT.Sqrt).then_inc(act.sem, 1))

            @block.vector
            def _(_e):
                V.wait_ge(*Ring.q)
                vl(V.reciprocal(inv, inv).then_inc(dve.sem, 1))
                for c in range(16):
                    Ring.q = dve.count(V.scalar_tensor_tensor(xb[:, c, :], xb[:, c, :], prm("snorm_g")[:, c:c + 1],
                                                             inv[:, (c // 2) * T:(c // 2 + 1) * T], ALU.mult, ALU.mult).then_inc(dve.sem, 1))
            done = out_project("w_ssd_out", 16, xb, [Ring.q])
            r_row = row_of(mod_col(0, 1, 2), 1.0, [])
            return add_gated(done + [r_row])

        def mla(ready):
            h_ready = modulated(1, 1, ready)
            ar = Arena()
            zt = ar.take(NT * 672).rearrange("p (t n) -> p t n", t=NT)
            qlT = ar.take(3 * T).rearrange("p (c t) -> p c t", c=3)
            klT = ar.take(2 * T).rearrange("p (c t) -> p c t", c=2)
            qt = ar.take(NT * 1536).rearrange("p (t h n) -> p t h n", t=NT, h=16)
            kt = ar.take(NT * 1536).rearrange("p (t h n) -> p t h n", t=NT, h=16)
            vt = ar.take(NT * 1024).rearrange("p (t h n) -> p t h n", t=NT, h=16)
            qT = ar.take(16 * T).rearrange("p (h t) -> p h t", h=16)
            kT = ar.take(16 * T).rearrange("p (h t) -> p h t", h=16)
            ang, cosr, sinr, rn = (small[:, 64 + 32 * n:96 + 32 * n] for n in range(4))
            sc = small[:, 192:256]
            t3 = lambda z, n: z.rearrange("p (t n) -> p t n", t=n)

            def evac(c, b, p):
                w = 32 if c == 5 else P

                @block.scalar
                def _(_e):
                    A.wait_ge(*p)
                    Ring.q = act.count(A.activation(zt[:, :, c * P:c * P + w],
                                                   b[:, 0:2 * w].rearrange("p (t d) -> p t d", t=NT), ACT.Copy).then_inc(act.sem, 1))
                return (Ring.q,)
            project("w_mla_in", 6, evac, h_ready, tokens=range(6), widths={5: 32})
            z_ready = Ring.q
            ss = small[:, 0:4]

            @block.scalar
            def _(_e):
                A.wait_ge(*z_ready)
                for t in range(NT):
                    al(A.activation(htok[:, 0, 0:384], zt[:, t, 0:384], ACT.Square, accum_out=ss[:, t:t + 1]).then_inc(act.sem, 1))
                    Ring.q = al(A.activation(htok[:, 1, 0:256], zt[:, t, 384:640], ACT.Square, accum_out=ss[:, 2 + t:3 + t]).then_inc(act.sem, 1))

            @block.vector
            def _(_e):
                V.wait_ge(*Ring.q)
                V.tensor_scalar(ss[:, 0:2], ss[:, 0:2], 1.0 / 384, EPS, ALU.mult, ALU.add)
                Ring.q = vl(V.tensor_scalar(ss[:, 2:4], ss[:, 2:4], 1.0 / 256, EPS, ALU.mult, ALU.add).then_inc(dve.sem, 1))
                V.tensor_copy(sc[:, 0:NT], posi[:, :])
                vl(V.memset(rn, 0.0).then_inc(dve.sem, 1))
                for t in range(NT):
                    vl(V.tensor_scalar(ang[:, 16 * t:16 * t + 16], cst("inv_freq"), sc[:, t:t + 1], None, ALU.mult).then_inc(dve.sem, 1))
                two_pi = 2 * math.pi
                c1 = 6.28125
                c2 = float(np.float32(math.floor((two_pi - c1) * 2 ** 20) / 2 ** 20))
                c3 = two_pi - c1 - c2
                magic = 12582912.0
                lim = 3.1415925
                for dst, quarter in ((sinr, 0.0), (cosr, 0.25)):
                    vl(V.tensor_scalar(rn, ang, 1.0 / two_pi, quarter, ALU.mult, ALU.add).then_inc(dve.sem, 1))
                    vl(V.tensor_scalar(rn, rn, magic, None, ALU.add).then_inc(dve.sem, 1))
                    vl(V.tensor_scalar(rn, rn, -magic, None, ALU.add).then_inc(dve.sem, 1))
                    vl(V.scalar_tensor_tensor(dst, rn, -c1, ang, ALU.mult, ALU.add).then_inc(dve.sem, 1))
                    vl(V.scalar_tensor_tensor(dst, rn, -c2, dst, ALU.mult, ALU.add).then_inc(dve.sem, 1))
                    vl(V.scalar_tensor_tensor(dst, rn, -c3, dst, ALU.mult, ALU.add).then_inc(dve.sem, 1))
                    if quarter:
                        vl(V.tensor_scalar(dst, dst, math.pi / 2, None, ALU.add).then_inc(dve.sem, 1))
                    Ring.p = vl(V.tensor_scalar(dst, dst, lim, -lim, ALU.min, ALU.max).then_inc(dve.sem, 1))

            @block.scalar
            def _(_e):
                A.wait_ge(*Ring.q)
                Ring.q = act.count(A.activation(ss, ss, ACT.Sqrt).then_inc(act.sem, 1))
                A.wait_ge(*Ring.p)
                A.activation(sinr, sinr, ACT.Sin)
                Ring.p = act.count(A.activation(cosr, cosr, ACT.Sin).then_inc(act.sem, 1))
            rope_ready = Ring.p

            @block.vector
            def _(_e):
                V.wait_ge(*Ring.q)
                vl(V.reciprocal(ss, ss).then_inc(dve.sem, 1))
                for t in range(NT):
                    V.tensor_scalar(zt[:, t, 0:384], zt[:, t, 0:384], ss[:, t:t + 1], None, ALU.mult)
                    Ring.q = dve.count(V.tensor_scalar(zt[:, t, 384:640], zt[:, t, 384:640], ss[:, 2 + t:3 + t], None, ALU.mult).then_inc(dve.sem, 1))
            lat = Ring.q
            pts = []
            for c in range(5):
                @block.tensor
                def _(_e):
                    E.wait_ge(*lat)
                    for t in range(NT):
                        ins = E.transpose(bank(c)[:, t * P:(t + 1) * P], zt[:, t, c * P:(c + 1) * P], ident)
                    Ring.p = pe.count(ins.then_inc(pe.sem, 1))

                @block.vector
                def _(_e):
                    V.wait_ge(*Ring.p)
                    dst = qlT[:, c, :] if c < 3 else klT[:, c - 3, :]
                    gain = prm("q_norm_g")[:, c:c + 1] if c < 3 else prm("kv_norm_g")[:, c - 3:c - 2]
                    pts.append(dve.count(V.tensor_scalar(dst, bank(c)[:, 0:T], gain, None, ALU.mult).then_inc(dve.sem, 1)))
            lat_ready = pts[-1]
            freed = [lat_ready] * 8
            n = 0
            for name, nb_, kk_, src in (("w_uq", 3, 3, qlT), ("w_ukv", 4, 2, klT)):
                for c in range(nb_):
                    s, full = load(dram[name][c:c + 1], 1)
                    w = slot_ap(s, kk_ * 512).rearrange("p (k n) -> p k n", k=kk_)
                    for t in range(NT):
                        b = n % 8
                        n += 1

                        @block.tensor
                        def _(_e):
                            E.wait_ge(*full)
                            E.wait_ge(*lat_ready)
                            E.wait_ge(*freed[b])
                            for k in range(kk_):
                                ins = E.matmul(bank(b), src[:, k, t * P:(t + 1) * P], w[:, k, :],
                                               start=k == 0, stop=k == kk_ - 1)
                            Ring.p = pe.count(ins.then_inc(pe.sem, 1))

                        @block.scalar
                        def _(_e):
                            A.wait_ge(*Ring.p)
                            if name == "w_uq":
                                ins = A.activation(qt[:, t].rearrange("p h n -> p (h n)")[:, c * 512:(c + 1) * 512],
                                                   bank(b), ACT.Copy)
                            else:
                                v4 = bank(b).rearrange("p (h n) -> p h n", h=4)
                                A.activation(kt[:, t, 4 * c:4 * c + 4, 0:64], v4[:, :, 0:64], ACT.Copy)
                                ins = A.activation(vt[:, t, 4 * c:4 * c + 4, :], v4[:, :, 64:128], ACT.Copy)
                            freed[b] = act.count(ins.then_inc(act.sem, 1))
                    Ring.used[s] = (pe.sem, pe.n)
            up_ready = (act.sem, act.n)
            scr = qT.rearrange("p h t -> p (h t)")[:, 0:1536].rearrange("p (h n) -> p h n", h=16)
            rot = kT.rearrange("p h t -> p (h t)")[:, 0:1024].rearrange("p (a h n) -> p a h n", a=4, h=16)
            hs_ = sc.rearrange("p (a t h) -> p a t h", a=2, t=NT)

            @block.vector
            def _(_e):
                V.wait_ge(*up_ready)
                for t in range(NT):
                    vl(V.tensor_copy(kt[:, t, :, 64:96], spread(zt[:, t, 640:672].rearrange("p (o n) -> p o n", o=1),
                                                                [P, 16, 32])).then_inc(dve.sem, 1))
                for a_, src in enumerate((qt, kt)):
                    for t in range(NT):
                        vl(V.tensor_tensor(scr, src[:, t], src[:, t], ALU.mult).then_inc(dve.sem, 1))
                        vl(V.tensor_reduce(hs_[:, a_, t, :], scr, AXX, ALU.add).then_inc(dve.sem, 1))
                Ring.q = (dve.sem, dve.n)
            rstd_of(sc, 64, 1.0 / 96, EPS, Ring.q)

            @block.vector
            def _(_e):
                V.wait_ge(*rope_ready)
                for a_, (src, gain) in enumerate(((qt, prm("q_head_g")), (kt, prm("k_head_g")))):
                    for t in range(NT):
                        vl(V.tensor_tensor(src[:, t], src[:, t], spread(hs_[:, a_, t, :].rearrange("p (h o) -> p h o", o=1),
                                                                        [P, 16, 96]), ALU.mult).then_inc(dve.sem, 1))
                        vl(V.tensor_tensor(src[:, t], src[:, t], spread(gain.rearrange("p (o n) -> p o n", o=1),
                                                                        [P, 16, 96]), ALU.mult).then_inc(dve.sem, 1))
                        co, si = (spread(z[:, 16 * t:16 * t + 16].rearrange("p (o n) -> p o n", o=1), [P, 16, 16])
                                  for z in (cosr, sinr))
                        x1, x2 = src[:, t, :, 64:80], src[:, t, :, 80:96]
                        V.tensor_tensor(rot[:, 0], x1, co, ALU.mult)
                        V.tensor_tensor(rot[:, 1], x2, si, ALU.mult)
                        V.tensor_tensor(rot[:, 2], x2, co, ALU.mult)
                        vl(V.tensor_tensor(rot[:, 3], x1, si, ALU.mult).then_inc(dve.sem, 1))
                        V.tensor_tensor(x1, rot[:, 0], rot[:, 1], ALU.subtract)
                        vl(V.tensor_tensor(x2, rot[:, 2], rot[:, 3], ALU.add).then_inc(dve.sem, 1))
                Ring.q = (dve.sem, dve.n)
            roped = Ring.q
            n = 0
            for src, dst in ((qt, qT), (kt, kT)):
                for t in range(NT):
                    for h0 in range(0, 16, 4):
                        b = n % 8
                        n += 1

                        @block.tensor
                        def _(_e):
                            E.wait_ge(*roped)
                            E.wait_ge(*freed[b])
                            for i in range(4):
                                ins = E.transpose(bank(b)[0:96, i * P:(i + 1) * P], src[:, t, h0 + i, :], ident)
                            Ring.p = pe.count(ins.then_inc(pe.sem, 1))

                        @block.scalar
                        def _(_e):
                            A.wait_ge(*Ring.p)
                            A.wait_ge(*roped)
                            freed[b] = act.count(A.activation(dst[0:96, h0:h0 + 4, t * P:(t + 1) * P],
                                                             bank(b)[0:96, :].rearrange("p (h n) -> p h n", h=4), ACT.Copy).then_inc(act.sem, 1))
            oT = hT
            ar.at = NT * 672 + 5 * T
            units = []
            for gq in range(4):
                for t in range(NT):
                    u = dict(branch=0, scale=96 ** -0.5, keys=T, blocks=2, last=True, dist=None,
                             q=lambda i, gq=gq, t=t: qT[0:96, 4 * gq + i, t * P:(t + 1) * P],
                             k=lambda i, gq=gq: kT[0:96, 4 * gq + i, :],
                             v=lambda i, b, gq=gq: vt[:, b, 4 * gq + i, :],
                             out=oT[:, 2 * gq:2 * gq + 2, t * P:(t + 1) * P])
                    u["parts"] = [u]
                    units.append(u)
            o_ready = attend(units, ar, T, [(act.sem, act.n), (pe.sem, pe.n), (dve.sem, dve.n)])
            done = out_project("w_mla_out", 8, oT, o_ready)
            r_row = row_of(mod_col(1, 1, 2), 1.0, o_ready)
            return add_gated(done + [r_row])

        @block.scalar
        def _(_e):
            Ring.q = al(A.activation(cond, prm("c"), ACT.Silu).then_inc(act.sem, 1))

        stages = [hybrid, lambda r: conv_ffn(0, r), nsa, lambda r: conv_ffn(1, r),
                  lambda r: silu_ffn(0, 0, 0, r), ssd, lambda r: silu_ffn(0, 2, 1, r),
                  lambda r: silu_ffn(1, 0, 0, r), mla, lambda r: silu_ffn(1, 2, 1, r)]
        at = [Ring.q]
        for n, stage in enumerate(stages):
            if dbg is not None and n not in dbg:
                continue
            at = stage(at)

        @block.sync
        def _(sp):
            for point in at:
                sp.wait_ge(*point)
            sp.dma_start(out, xs_[:, :]).then_inc(stored, 16)
            sp.wait_ge(stored, 16)


def kernel(**inputs):
    import concourse.bacc as bacc
    from concourse.bass_utils import run_bass_kernel_spmd

    arrays, pat = lay_out(inputs)
    cat = constant_table()[1]
    nc = bacc.Bacc("TRN2", target_bir_lowering=False, num_devices=1)
    dram = {}
    for name, a in arrays.items():
        dram[name] = nc.dram_tensor("in_" + name, a.shape, mybir.dt.from_np(a.dtype), kind="ExternalInput").ap()
    out = nc.dram_tensor("out_x", (P, NT * D), F32, kind="ExternalOutput").ap()
    build(nc, dram, out, pat, cat)
    r = run_bass_kernel_spmd(nc, [{"in_" + n: a for n, a in arrays.items()}], core_ids=[0])
    y = r.results[0]["out_x"].reshape(P, NT, D).transpose(1, 0, 2).reshape(1, T, D)
    return np.ascontiguousarray(y)
```

```python
import math
from contextlib import ExitStack

import numpy as np
import concourse.bass as bass
from concourse import mybir

F32 = mybir.dt.float32
F32R = mybir.dt.float32r
I32 = mybir.dt.int32
ALU = mybir.AluOpType
ACT = mybir.ActivationFunctionType
AXX = mybir.AxisListType.X

P = 128
T = 256
NT = T // P
D = 1024
KC = D // P
DFF = 2816
NF = DFF // P
HD = 64
EPS = 1e-6
BIG = 1e30
CHUNK = 1024
RING = 4
SLOT = 3 * CHUNK
C64 = 64
LEVELS = 6
N_CMP = (T - 32) // 16 + 1


def alibi(n):
    return [2.0 ** (-8.0 * (i + 1) / n) for i in range(n)]


def constant_table():
    i = np.arange(P)
    col, row = i[None, :], i[:, None]
    out, at, pos = [], {}, 0

    def add(name, a):
        nonlocal pos
        a = np.ascontiguousarray(a, dtype=np.float32).reshape(P, -1)
        at[name] = (pos, a.shape[1])
        pos += a.shape[1]
        out.append(a)

    add("ident", np.eye(P))
    add("headsum", (row // HD == col // HD))
    same = row // C64 == col // C64
    add("lower", same & (col < row))
    add("upper", same & (col > row))
    add("upper_in", same & (col >= row))
    levels, levels_t = [], []
    for l in range(LEVELS):
        m = 1 << l
        low = (row // (2 * m) == col // (2 * m)) & (row % (2 * m) >= m) & (col % (2 * m) < m)
        levels.append(low)
        levels_t.append(low.T)
    add("level", np.stack(levels, 1))
    add("level_t", np.stack(levels_t, 1))
    t = np.arange(T)
    add("scan_keep", np.broadcast_to(t % C64 != 0, (P, T)))
    dist = (i[:, None] - i[None, :]).astype(np.float32)
    add("causal0", np.where(dist >= 0, dist, BIG))
    dist1 = (P + i[:, None] - t[None, :]).astype(np.float32)
    add("causal1", np.where(dist1 >= 0, dist1, BIG))
    add("window1", np.where((dist1 >= 0) & (dist1 < 128), dist1, BIG))
    ends = np.arange(N_CMP) * 16 + 31
    for n in range(NT):
        dc = (n * P + i)[:, None] - ends[None, :]
        add(f"cmp{n}", np.where(dc >= 0, dc, BIG))
        add(f"cmp_any{n}", ((n * P + i)[:, None] >= 31))
    u = (np.arange(NT)[:, None] * P + i[None, :]).T[:, :, None]
    add("tri_f", u <= t[None, None, :])
    add("tri_b", u >= t[None, None, :])
    add("neg_f", np.where(row <= col, 0.0, -BIG))
    add("neg_b", np.where(row >= col, 0.0, -BIG))
    add("inv_freq", np.broadcast_to(10000.0 ** (-np.arange(0, 32, 2) / 32.0), (P, 16)))
    return np.concatenate(out, 1), at


def cols(v):
    return np.asarray(v).reshape(-1, P).T


def col_chunks(w):
    w = np.asarray(w)
    n = w.shape[1] // P
    return np.ascontiguousarray(w.reshape(KC, P, n, P).transpose(2, 1, 0, 3)).reshape(n, P, CHUNK)


def row_chunks(w):
    w = np.asarray(w)
    return np.ascontiguousarray(w.reshape(-1, P, D))


def ffn_chunks(gate, up, down):
    return np.stack([col_chunks(gate), col_chunks(up), row_chunks(down)], 1)


def twice(w, heads):
    w = np.asarray(w).reshape(w.shape[0], heads, HD)
    return np.concatenate([w, w], 2).reshape(w.shape[0], heads * P)


def padded(w, n):
    w = np.asarray(w)
    return np.concatenate([w, np.zeros((w.shape[0], n - w.shape[1]), w.dtype)], 1)


def lay_out(i):
    i = {k: np.asarray(v) for k, v in i.items()}
    params, at, pos = [], {}, 0

    def add(name, a):
        nonlocal pos
        a = np.asarray(a)
        a = a.reshape(P, -1)
        at[name] = (pos, a.shape[1])
        pos += a.shape[1]
        params.append(a)

    def row(name, v):
        v = np.asarray(v).reshape(-1)
        add(name, np.broadcast_to(v, (P, v.size)))

    for name in ("mix_pre_g", "mix_post_g", "ffn_pre_g", "ffn_post_g"):
        for l in range(2):
            add(f"{name}{l}", cols(i[name][l]))
    add("mu", cols(i["rwkv_mu"][0]))
    for name in ("w0", "a0", "k_k", "k_a", "ln_g", "ln_b"):
        add(name, cols(i["rwkv_" + name][0]))
    add("r_k", cols(i["rwkv_r_k"][0].reshape(-1)))
    add("wa2", np.concatenate([i["rwkv_w2"][0], i["rwkv_a2"][0]], 0))
    add("g2", i["rwkv_g2"][0])
    row("sinks", i["swa_sinks"][0])
    for l in range(2):
        for j in range(3):
            add(f"conv_w{l}{j}", cols(i["ffn_conv_w"][l, j]))
        add(f"conv_b{l}", cols(i["ffn_conv_b"][l]))
    for l in range(2):
        for s in range(3):
            add(f"norm_g{l}{s}", cols(i["norm_g_2"][l, s]))
        add(f"b_mod{l}", cols(i["b_mod_2"][l]))
    add("c", cols(i["c_2"][0]))
    for kv in "kv":
        pos_ = i[f"nsa_cmp_pos_{kv}"][0]
        add("pos_" + kv, pos_.reshape(16, 2, HD).transpose(1, 2, 0).reshape(P, 16))
    w2k = i["nsa_cmp_w2_k"][0].reshape(2, P, HD).transpose(1, 0, 2)
    add("cw2_k", np.concatenate([w2k, w2k], 2))
    add("cw2_v", i["nsa_cmp_w2_v"][0].reshape(2, P, HD).transpose(1, 0, 2))
    for j in range(5):
        add(f"sconv_w{j}", cols(i["ssd_conv_w_2"][0, j]))
    add("sconv_b", cols(i["ssd_conv_b_2"][0]))
    add("snorm_g", cols(i["ssd_norm_g_2"][0]))
    add("d_skip", cols(np.repeat(i["ssd_d_2"][0], HD)))
    row("dt_bias", i["ssd_dt_bias_2"][0])
    row("a_log", i["ssd_a_log_2"][0])
    add("q_norm_g", cols(i["mla_q_norm_g_2"][0]))
    add("kv_norm_g", cols(i["mla_kv_norm_g_2"][0]))
    row("q_head_g", i["mla_q_head_g_2"][0])
    row("k_head_g", i["mla_k_head_g_2"][0])

    hy = i["hy_w_in"][0]
    hy = np.concatenate([hy[:, 0:512], twice(hy[:, 512:640], 2), hy[:, 768:2560], hy[:, 640:768]], 1)
    ns = i["nsa_w_in"][0]
    kc, vc, ks, vs, kw, vw = (ns[:, 1024 + 256 * j:1280 + 256 * j] for j in range(6))
    ns = np.concatenate([ns[:, 0:1024], twice(kc, 4), twice(vc, 4), twice(ks, 4), twice(kw, 4), vs, vw,
                         padded(ns[:, 2560:2608], P)], 1)
    cw1 = [i[f"nsa_cmp_w1_{kv}"][0].reshape(2, 8, 2, HD, 256).transpose(0, 2, 3, 1, 4).reshape(2, P, 2048)
           for kv in "kv"]
    arrays = {
        "x": np.ascontiguousarray(i["x"][0].reshape(NT, P, D).transpose(1, 0, 2)).reshape(P, NT * D),
        "params": np.concatenate(params, 1),
        "consts": constant_table()[0],
        "positions": np.ascontiguousarray(i["positions_2"].reshape(NT, P).T),
        "w_hy_in": col_chunks(hy),
        "w_hy_out": row_chunks(i["hy_w_out"][0]),
        "w_ns_in": col_chunks(ns),
        "w_ns_out": row_chunks(i["nsa_w_out"][0]),
        "w_cmp1": np.concatenate(cw1, 0),
        "w_ssd_in": col_chunks(padded(i["ssd_w_in_2"][0], 49 * P)),
        "w_ssd_out": row_chunks(i["ssd_w_out_2"][0]),
        "w_mla_in": col_chunks(padded(i["mla_w_in_2"][0], 6 * P)),
        "w_uq": i["mla_w_uq_2"][0].reshape(3, P, 3, 512).transpose(2, 1, 0, 3).reshape(3, P, 1536),
        "w_ukv": i["mla_w_ukv_2"][0].reshape(2, P, 4, 512).transpose(2, 1, 0, 3).reshape(4, P, 1024),
        "w_mla_out": row_chunks(i["mla_w_out_2"][0]),
    }
    for l in range(2):
        up = i["ffn_w_up"][l]
        arrays[f"w_conv{l}"] = ffn_chunks(up[:, :DFF], up[:, DFF:], i["ffn_w_down"][l])
        arrays[f"w_mod{l}"] = col_chunks(i["w_mod_2"][l])
        for s in range(2):
            arrays[f"w_ffn{l}{s}"] = ffn_chunks(i["ffn_w_gate_2"][l, s], i["ffn_w_up_2"][l, s],
                                                i["ffn_w_down_2"][l, s])
    return {k: np.ascontiguousarray(v) for k, v in arrays.items()}, at


class Progress:

    def __init__(self, sem):
        self.sem, self.n = sem, 0

    def count(self, _ins):
        self.n += 1
        return (self.sem, self.n)


def build(nc, dram, out, pat, cat, stop=None, dbg=None):
    V, A, E, G = nc.vector, nc.scalar, nc.tensor, nc.gpsimd
    ctx = ExitStack()
    with ctx:
        def sb(name, n, dt=F32):
            return ctx.enter_context(nc.sbuf_tensor(name, [P, n], dt))

        params = sb("params", dram["params"].shape[1])
        consts = sb("consts", dram["consts"].shape[1])
        xs_ = sb("x_res", NT * D)
        hT_ = sb("hT", KC * T)
        htok_ = sb("htok", NT * D)
        ring = sb("ring", RING * SLOT)
        rowb = sb("rowb", D)
        modT = sb("modT", 2 * 72)
        small = sb("small", 512)
        modw = sb("modw", SLOT)
        posi = sb("posi", NT, I32)
        psum = ctx.enter_context(nc.psum_tensor("psum", [P, 8, 512], F32))

        pe = Progress(ctx.enter_context(nc.semaphore("pe_done")))
        act = Progress(ctx.enter_context(nc.semaphore("act_done")))
        dve = Progress(ctx.enter_context(nc.semaphore("dve_done")))
        start_loaded = ctx.enter_context(nc.semaphore("start_loaded"))
        stored = ctx.enter_context(nc.semaphore("stored"))
        slot_full = [ctx.enter_context(nc.semaphore(f"slot_full{n}")) for n in range(RING)]

        block = ctx.enter_context(nc.Block())

        def prm(name):
            a, n = pat[name]
            return params[:, a:a + n]

        def cst(name):
            a, n = cat[name]
            return consts[:, a:a + n]

        x = xs_[:, :].rearrange("p (t d) -> p t d", t=NT)
        hT = hT_[:, :].rearrange("p (k t) -> p k t", k=KC)
        htok = htok_[:, :].rearrange("p (t d) -> p t d", t=NT)
        ident = cst("ident")
        acc = psum[:, 0:4, :].rearrange("p (t b) n -> p t (b n)", t=NT)

        def bank(b):
            return psum[:, b, :]

        def banks(b, n):
            return psum[:, b:b + n, :].rearrange("p b n -> p (b n)")

        class Arena:
            made = 0

            def __init__(self):
                self.stack = ctx.enter_context(ExitStack())

            def take(self, n, dt=F32):
                Arena.made += 1
                return self.stack.enter_context(nc.sbuf_tensor(f"buf{Arena.made}", [P, n], dt))[:, :]

            def close(self):
                self.stack.close()

        def spread(ap, shape):
            return ap.to_broadcast(shape)

        def vl(ins):
            p = dve.count(ins)
            V.wait_ge(*p)
            return p

        def al(ins):
            p = act.count(ins)
            A.wait_ge(*p)
            return p

        @block.sync
        def _(sp):
            sp.dma_start(xs_[:, :], dram["x"]).then_inc(start_loaded, 16)
            sp.dma_start(consts[:, :], dram["consts"]).then_inc(start_loaded, 16)
            sp.dma_start(params[:, :], dram["params"]).then_inc(start_loaded, 16)
            sp.dma_start(posi[:, :], dram["positions"]).then_inc(start_loaded, 16)
        loaded = (start_loaded, 64)

        @block.vector
        def _(_e):
            V.wait_ge(*loaded)

        @block.scalar
        def _(_e):
            A.wait_ge(*loaded)

        @block.tensor
        def _(_e):
            E.wait_ge(*loaded)

        class Ring:
            n = 0
            used = [[] for _ in range(RING)]
            fills = [0] * RING

        def slot_ap(s, w):
            return ring[:, s * SLOT:s * SLOT + w]

        def load(src, chunks):
            s = Ring.n % RING
            Ring.n += 1
            Ring.fills[s] += 1
            w = src.shape[-1]
            waits = Ring.used[s]

            @block.sync
            def _(sp):
                for point in waits:
                    sp.wait_ge(*point)
                sp.dma_start(slot_ap(s, chunks * w).rearrange("p (c w) -> p c w", c=chunks),
                             src.rearrange("c p w -> p c w")).then_inc(slot_full[s], 16)
            return s, (slot_full[s], 16 * Ring.fills[s])

        def rstd_of(ss, n, scale, eps, ready):
            @block.vector
            def _(_e):
                V.wait_ge(*ready)
                Ring.p = vl(V.tensor_scalar(ss, ss, scale, eps, ALU.mult, ALU.add).then_inc(dve.sem, 1))

            @block.scalar
            def _(_e):
                A.wait_ge(*Ring.p)
                Ring.p = act.count(A.activation(ss, ss, ACT.Sqrt).then_inc(act.sem, 1))

            @block.vector
            def _(_e):
                V.wait_ge(*Ring.p)
                Ring.p = vl(V.reciprocal(ss, ss).then_inc(dve.sem, 1))
            return Ring.p

        def whole(ap):
            return ap.bitcast(F32)

        def halves(ar, n):
            return ar.take(2 * n * T, F32R).rearrange("p (a k t) -> p a k t", a=2, k=n)

        def norm_transpose(gain, shift, ready, parts):
            ss = small[:, 0:NT]

            @block.scalar
            def _(_e):
                for point in ready:
                    A.wait_ge(*point)
                for t in range(NT):
                    p = al(A.activation(htok[:, t, :], x[:, t, :], ACT.Square, accum_out=ss[:, t:t + 1]).then_inc(act.sem, 1))
                Ring.q = p
            rstd_of(ss, NT, 1.0 / D, EPS, Ring.q)

            @block.vector
            def _(_e):
                for t in range(NT):
                    Ring.q = dve.count(V.tensor_scalar(htok[:, t, :], x[:, t, :], ss[:, t:t + 1], None, ALU.mult).then_inc(dve.sem, 1))
            normed = Ring.q
            freed = [loaded] * 4
            for k in range(KC):
                b = bank(4 + k % 4)

                @block.tensor
                def _(_e):
                    E.wait_ge(*normed)
                    E.wait_ge(*freed[k % 4])
                    for t in range(NT):
                        ins = E.transpose(b[:, t * P:(t + 1) * P], htok[:, t, k * P:(k + 1) * P], ident)
                    Ring.p = pe.count(ins.then_inc(pe.sem, 1))

                @block.scalar
                def _(_e):
                    A.wait_ge(*Ring.p)
                    bias = 0.0 if shift is None else shift[:, k:k + 1]
                    freed[k % 4] = act.count(A.activation(hT[:, k, :], b[:, 0:T], ACT.Identity, bias=bias,
                                                          scale=gain[:, k:k + 1]).then_inc(act.sem, 1))

                if parts is None:
                    Ring.q = freed[k % 4]
                    continue

                @block.vector
                def _(_e):
                    V.wait_ge(*freed[k % 4])
                    vl(V.tensor_copy(parts[:, 0, k, :], hT[:, k, :]).then_inc(dve.sem, 1))
                    Ring.q = dve.count(V.tensor_tensor(parts[:, 1, k, :], hT[:, k, :], whole(parts[:, 0, k, :]),
                                                       ALU.subtract).then_inc(dve.sem, 1))
            return [Ring.q]

        def row_of(col, scale, ready):
            @block.tensor
            def _(_e):
                for point in ready:
                    E.wait_ge(*point)
                for k in range(KC):
                    ins = E.matmul(bank(4 + k // 4)[:, (k % 4) * P:(k % 4 + 1) * P],
                                   spread(col[:, k:k + 1], [P, P]), ident, start=True, stop=True)
                Ring.p = pe.count(ins.then_inc(pe.sem, 1))

            @block.scalar
            def _(_e):
                A.wait_ge(*Ring.p)
                Ring.p = al(A.activation(rowb[:, :], banks(4, 2), ACT.Copy, scale=scale).then_inc(act.sem, 1))
            return Ring.p

        def add_normed(ready):
            ss = small[:, 0:NT]

            @block.scalar
            def _(_e):
                for point in ready:
                    A.wait_ge(*point)
                for t in range(NT):
                    Ring.q = al(A.activation(htok[:, t, :], acc[:, t, :], ACT.Square, accum_out=ss[:, t:t + 1]).then_inc(act.sem, 1))
            rstd_of(ss, NT, 1.0 / D, EPS, Ring.q)

            @block.vector
            def _(_e):
                for t in range(NT):
                    dve.count(V.scalar_tensor_tensor(htok[:, t, :], acc[:, t, :], ss[:, t:t + 1], rowb[:, :],
                                                    ALU.mult, ALU.mult).then_inc(dve.sem, 1))
                V.wait_ge(dve.sem, dve.n)
                Ring.p = vl(V.tensor_tensor(xs_[:, :], xs_[:, :], htok_[:, :], ALU.add).then_inc(dve.sem, 1))
            return [Ring.p]

        def add_gated(ready):
            @block.vector
            def _(_e):
                for point in ready:
                    V.wait_ge(*point)
                for t in range(NT):
                    dve.count(V.tensor_tensor(htok[:, t, :], acc[:, t, :], rowb[:, :], ALU.mult).then_inc(dve.sem, 1))
                V.wait_ge(dve.sem, dve.n)
                Ring.p = vl(V.tensor_tensor(xs_[:, :], xs_[:, :], htok_[:, :], ALU.add).then_inc(dve.sem, 1))
            return [Ring.p]

        PASSES = ((0, 0), (0, 1), (1, 0))

        def split_chunk(raw, parts, full, free):
            @block.scalar
            def _(_e):
                A.wait_ge(*full)
                A.wait_ge(*free)
                Ring.p = act.count(A.activation(parts[:, 0, :], raw, ACT.Copy).then_inc(act.sem, 1))

            @block.vector
            def _(_e):
                V.wait_ge(*Ring.p)
                V.wait_ge(*full)
                Ring.p = dve.count(V.tensor_tensor(parts[:, 1, :], raw, whole(parts[:, 0, :]),
                                                   ALU.subtract).then_inc(dve.sem, 1))
            return Ring.p

        def weight_parts(ar, n=3):
            return [ar.take(2 * CHUNK, F32R).rearrange("p (a w) -> p a w", a=2) for _ in range(n)]

        def project(name, n, evac, ready, h, wp, tokens=(), widths={}):
            freed = [()] * 4
            wp_free = [loaded] * len(wp)
            made = {}

            def prepare(c):
                if c % 3 == 0:
                    m = min(3, n - c)
                    made["slot"], made["full"] = load(dram[name][c:c + m], m)
                s, full = made["slot"], made["full"]
                raw = slot_ap(s, SLOT)[:, (c % 3) * CHUNK:(c % 3 + 1) * CHUNK]
                if c in tokens:
                    made[c] = (s, raw, full)
                else:
                    p = split_chunk(raw, wp[c % len(wp)], full, wp_free[c % len(wp)])
                    made[c] = (s, raw, p)
                    Ring.used[s] = [p]

            prepare(0)
            for c in range(n):
                if c + 1 < n:
                    prepare(c + 1)
                s, raw, point_w = made[c]
                b = bank(4 + c % 4)

                @block.tensor
                def _(_e):
                    E.wait_ge(*point_w)
                    for point in ready:
                        E.wait_ge(*point)
                    for point in freed[c % 4]:
                        E.wait_ge(*point)
                    if c in tokens:
                        w = raw.rearrange("p (k n) -> p k n", k=KC)
                        width = widths.get(c, P)
                        for t in range(NT):
                            for k in range(KC):
                                ins = E.matmul(b[:, t * width:(t + 1) * width], hT[:, k, t * P:(t + 1) * P],
                                               w[:, k, 0:width], start=k == 0, stop=k == KC - 1)
                    else:
                        w = wp[c % len(wp)].rearrange("p a (k n) -> p a k n", k=KC)
                        for k in range(KC):
                            for n_, (wa, ha) in enumerate(PASSES):
                                ins = E.matmul(b[:, 0:T], w[:, wa, k, :], h[:, ha, k, :], start=k + n_ == 0,
                                               stop=k == KC - 1 and n_ == 2)
                    Ring.p = pe.count(ins.then_inc(pe.sem, 1))
                if c in tokens:
                    Ring.used[s] = Ring.used[s][-1:] + [Ring.p] if c % 3 else [Ring.p]
                else:
                    wp_free[c % len(wp)] = Ring.p
                freed[c % 4] = evac(c, b, Ring.p)

        def out_project(name, n, lhs, ready):
            ar = Arena()
            parts = halves(ar, n)
            wp = weight_parts(ar)
            wp_free = [loaded] * 3
            for k in range(n):
                if k % 3 == 0:
                    m = min(3, n - k)
                    s, full = load(dram[name][k:k + m], m)

                @block.scalar
                def _(_e):
                    for point in ready:
                        A.wait_ge(*point)
                    Ring.p = act.count(A.activation(parts[:, 0, k, :], lhs[:, k, :], ACT.Copy).then_inc(act.sem, 1))

                @block.vector
                def _(_e):
                    V.wait_ge(*Ring.p)
                    dve.count(V.tensor_tensor(parts[:, 1, k, :], lhs[:, k, :], whole(parts[:, 0, k, :]),
                                              ALU.subtract).then_inc(dve.sem, 1))
                Ring.used[s] = [split_chunk(slot_ap(s, SLOT)[:, (k % 3) * D:(k % 3 + 1) * D], wp[k % 3], full,
                                            wp_free[k % 3])]

                @block.tensor
                def _(_e):
                    E.wait_ge(*Ring.used[s][0])
                    for t in range(NT):
                        for h in range(2):
                            for n_, (wa, la) in enumerate(PASSES):
                                ins = E.matmul(acc[:, t, h * 512:(h + 1) * 512], parts[:, la, k, t * P:(t + 1) * P],
                                               wp[k % 3][:, wa, h * 512:(h + 1) * 512], start=k + n_ == 0,
                                               stop=k == n - 1 and n_ == 2)
                    wp_free[k % 3] = pe.count(ins.then_inc(pe.sem, 1))
            ar.close()
            return [(pe.sem, pe.n)]

        cond = small[:, 40:48]
        one_col = small[:, 4:5]

        mod_full = ctx.enter_context(nc.semaphore("mod_full"))
        mod_loads = [0]
        MOD_PIECES = 12

        def ffn(name, ready, h, ar, conv=None, mod=None):
            src = dram[name]
            wu = [ar.take(4 * CHUNK, F32R).rearrange("p (a w) -> p a w", a=2) for _ in range(2)]
            wd = [ar.take(2 * CHUNK, F32R).rearrange("p (a w) -> p a w", a=2) for _ in range(2)]
            hr = [ar.take(2 * T, F32R).rearrange("p (a w) -> p a w", a=2) for _ in range(2)]
            sg = [htok_[:, q * T:(q + 1) * T] for q in range(2)]
            cv = [htok_[:, (2 + q) * T:(3 + q) * T] for q in range(2)]
            hf = [htok_[:, 4 * T:5 * T]] * 2 if conv is not None else cv
            gp = [htok_[:, 5 * T + 4 + q * (T + 4):6 * T + 6 + q * (T + 4)] for q in range(2)]
            if mod is not None:
                macc = ar.take(MOD_PIECES * 3 * P)
                msrc = dram[f"w_mod{mod[0]}"]
                mod0 = 36 * mod[1]
            c3 = conv is not None
            if c3:
                @block.vector
                def _(_e):
                    for point in ready:
                        V.wait_ge(*point)
                    for q in range(2):
                        vl(V.memset(gp[q][:, 0:2], 0.0).then_inc(dve.sem, 1))
                gp_ready = (dve.sem, dve.n)

                @block.scalar
                def _(_e):
                    A.wait_ge(*gp_ready)

            AM = 4 if c3 else 3
            DM = 8 if c3 else 5
            MM = KC if mod is not None else 0
            PB, AB, DB = pe.n - 1, act.n - (AM - 2), dve.n - (DM - 2) + MM
            P0, A0, D0 = pe.n, act.n, dve.n

            def zero(j):
                return isinstance(j, int) and j == 0

            def up_done(j):
                return (pe.sem, P0 + 1) if zero(j) else (pe.sem, PB + 2 * j + 1)

            def down_done(j):
                return (pe.sem, PB + 2 * (j + 1) + 2)

            def act_at(j, k):
                return (act.sem, A0 + (1 if k == 1 else 2)) if zero(j) else (act.sem, AB + AM * j + k)

            def dve_at(q, u, k):
                if zero(q) and u == 0:
                    return (dve.sem, D0 + (1 if k == 1 else 2))
                return (dve.sem, DB + (2 * DM + MM) * q + DM * u + k)

            def prev(q, u, back):
                return q + (u - back) // 2, (u - back) % 2

            slots0 = Ring.n
            fills0 = list(Ring.fills)

            def slot(ju):
                return (slots0 + ju) % RING

            def full(q, ju):
                return (slot_full[slot(ju)], 16 * (fills0[slot(ju)] + 1 + ju // RING) + 16 * q)

            def sp_step(sp, q4, ju, waits):
                j = q4 * 4 + ju
                for point in waits:
                    sp.wait_ge(*point)
                sp.dma_start(slot_ap(slot(ju), SLOT).rearrange("p (c w) -> p c w", c=3),
                             (src[j] if isinstance(j, int) else
                              src[bass.ds(j, 1)].rearrange("a c p w -> (a c) p w")).rearrange("c p w -> p c w")
                             ).then_inc(slot_full[slot(ju)], 16)

            def sp_mod(sp, m, waits):
                for point in waits:
                    sp.wait_ge(*point)
                rows = msrc[mod0 + 3 * m:mod0 + 3 * m + 3] if isinstance(m, int) else msrc[bass.ds(m * 3 + mod0, 3)]
                sp.dma_start(modw[:, :].rearrange("p (c w) -> p c w", c=3),
                             rows.rearrange("c p w -> p c w")).then_inc(mod_full, 16)

            def pe_up(q, u, ju):
                E.wait_ge(*dve_at(q, u, 1))
                if not (isinstance(q, int) and q == 0):
                    E.wait_ge(*dve_at(*prev(q, u, 1), DM - 3))
                w = wu[u].rearrange("p a (c k n) -> p a c k n", c=2, k=KC)
                b = bank(4 + u)
                for g in range(2):
                    for k in range(KC):
                        for n_, (wa, ha) in enumerate(PASSES):
                            ins = E.matmul(b[:, g * T:(g + 1) * T], w[:, wa, g, k, :], h[:, ha, k, :],
                                           start=k + n_ == 0, stop=k == KC - 1 and n_ == 2)
                ins.then_inc(pe.sem, 1)

            def pe_down(q, u, start=False, stop=False, last=None):
                E.wait_ge(*(last or dve_at(q, u, DM - 1)))
                z = 1 - u
                for t in range(NT):
                    for g in range(2):
                        for n_, (wa, ha) in enumerate(PASSES):
                            ins = E.matmul(acc[:, t, g * 512:(g + 1) * 512], hr[z][:, ha, t * P:(t + 1) * P],
                                           wd[z][:, wa, g * 512:(g + 1) * 512], start=start and n_ == 0,
                                           stop=stop and n_ == 2)
                ins.then_inc(pe.sem, 1)

            def act_hidden(q, u, j):
                z = 1 - u
                b = bank(4 + z)
                A.wait_ge(*up_done(j - 1))
                if not c3:
                    if not isinstance(j, int):
                        A.wait_ge(*dve_at(*prev(q, u, 2), DM - 3))
                    A.activation(sg[z], b[:, 0:T], ACT.Silu).then_inc(act.sem, 1)
                else:
                    A.activation(gp[z][:, 2:T + 2], b[:, 0:T], ACT.Copy).then_inc(act.sem, 1)
                    A.wait_ge(*dve_at(q, u, 4))
                    A.activation(sg[z], cv[z], ACT.Gelu_apprx_tanh).then_inc(act.sem, 1)

            def act_step(q, u, ju, q4):
                j = q * 2 + u
                raw = slot_ap(slot(ju), SLOT)
                A.wait_ge(*full(q4, ju))
                if not isinstance(j, int):
                    A.wait_ge(*up_done(j - 2))
                A.activation(wu[u][:, 0, :], raw[:, 0:2 * CHUNK], ACT.Copy).then_inc(act.sem, 1)
                if not zero(j):
                    act_hidden(q, u, j)
                if not isinstance(j, int):
                    A.wait_ge(*down_done(j - 2))
                A.activation(wd[u][:, 0, :], raw[:, 2 * CHUNK:], ACT.Copy).then_inc(act.sem, 1)

            def one(name_, j):
                v = prm(name_)
                return v[:, j:j + 1] if isinstance(j, int) else v[:, bass.ds(j, 1)]

            def dve_hidden(q, u, j):
                z = 1 - u
                b = bank(4 + z)
                if c3:
                    V.wait_ge(*act_at(j, 2))
                    V.tensor_scalar(cv[z], gp[z][:, 0:T], one(f"conv_w{conv}0", j - 1), one(f"conv_b{conv}", j - 1),
                                    ALU.mult, ALU.add).then_inc(dve.sem, 1)
                    for w in (1, 2):
                        V.wait_ge(*dve_at(q, u, 1 + w))
                        V.scalar_tensor_tensor(cv[z], gp[z][:, w:w + T], one(f"conv_w{conv}{w}", j - 1), cv[z],
                                               ALU.mult, ALU.add).then_inc(dve.sem, 1)
                V.wait_ge(*act_at(j, AM - 1))
                V.wait_ge(*up_done(j - 1))
                V.tensor_tensor(hf[z], sg[z], b[:, T:2 * T], ALU.mult).then_inc(dve.sem, 1)
                V.wait_ge(*dve_at(q, u, DM - 3))
                if not isinstance(j, int):
                    V.wait_ge(*down_done(j - 3))
                V.tensor_copy(hr[z][:, 0, :], hf[z]).then_inc(dve.sem, 1)
                V.wait_ge(*dve_at(q, u, DM - 2))
                V.tensor_tensor(hr[z][:, 1, :], hf[z], whole(hr[z][:, 0, :]), ALU.subtract).then_inc(dve.sem, 1)

            def dve_step(q, u, ju, q4):
                j = q * 2 + u
                raw = slot_ap(slot(ju), SLOT)
                V.wait_ge(*full(q4, ju))
                V.wait_ge(*act_at(j, 1))
                V.tensor_tensor(wu[u][:, 1, :], raw[:, 0:2 * CHUNK], whole(wu[u][:, 0, :]),
                                ALU.subtract).then_inc(dve.sem, 1)
                if not zero(j):
                    dve_hidden(q, u, j)
                V.wait_ge(*act_at(j, AM))
                V.tensor_tensor(wd[u][:, 1, :], raw[:, 2 * CHUNK:], whole(wd[u][:, 0, :]),
                                ALU.subtract).then_inc(dve.sem, 1)

            def dve_mod(m, before):
                w = modw[:, :].rearrange("p (c k n) -> p c k n", c=3, k=KC)
                o = (macc[:, m * 3 * P:(m + 1) * 3 * P] if isinstance(m, int) else
                     macc[:, bass.ds(m * (3 * P), 3 * P)]).rearrange("p (c n) -> p c n", c=3)
                V.wait_ge(mod_full, 16 * (mod_loads[0] + 1) + m * 16)
                V.tensor_scalar(o, w[:, :, 0, :], cond[:, 0:1], None, ALU.mult).then_inc(dve.sem, 1)
                for k in range(1, KC):
                    V.wait_ge(dve.sem, before + k)
                    V.scalar_tensor_tensor(o, w[:, :, k, :], cond[:, k:k + 1], o, ALU.mult, ALU.add
                                           ).then_inc(dve.sem, 1)

            for j in range(2):
                before = Ring.used[slot(j)]

                @block.sync
                def _(sp):
                    sp_step(sp, 0, j, before)
                    if mod is not None:
                        sp_mod(sp, j, [(dve.sem, D0 + (2 + MM if j else 0))] if D0 else [])

                @block.tensor
                def _(_e):
                    if j == 0:
                        for point in ready:
                            E.wait_ge(*point)
                    pe_up(0, j, j)
                    if j == 1:
                        pe_down(0, 1, start=True)

                @block.scalar
                def _(_e):
                    if j == 0:
                        for point in ready:
                            A.wait_ge(*point)
                    act_step(0, j, j, 0)

                @block.vector
                def _(_e):
                    if j == 0:
                        for point in ready:
                            V.wait_ge(*point)
                    dve_step(0, j, j, 0)
                    if mod is not None:
                        dve_mod(j, D0 + 2 if j == 0 else DB + 2 * DM)

            @block.sync
            def _(sp):
                with sp.Fori(0, (NF - 2) // 4) as i:
                    for u in range(4):
                        q = i * 2 + (1 + u // 2)
                        sp_step(sp, i, 2 + u, [dve_at(*prev(q, u % 2, 2), DM) if u > 1 else
                                               (dve.sem, DB + (2 * DM + MM) * 2 * i + DM * (u + 1))])
                        if mod is not None and u % 2:
                            sp_mod(sp, i * 2 + (2 + u // 2), [dve_at(q, 0, 0)])

            @block.tensor
            def _(_e):
                with E.Fori(0, (NF - 2) // 4) as i:
                    for u in range(4):
                        q = i * 2 + (1 + u // 2)
                        pe_up(q, u % 2, 2 + u)
                        pe_down(q, u % 2)

            @block.scalar
            def _(_e):
                with A.Fori(0, (NF - 2) // 4) as i:
                    for u in range(4):
                        act_step(i * 2 + (1 + u // 2), u % 2, 2 + u, i)

            @block.vector
            def _(_e):
                with V.Fori(0, (NF - 2) // 4) as i:
                    for u in range(4):
                        q = i * 2 + (1 + u // 2)
                        dve_step(q, u % 2, 2 + u, i)
                        if mod is not None and u % 2:
                            dve_mod(i * 2 + (2 + u // 2), DB + (2 * DM + MM) * q + 2 * DM)

            D1 = DB + (2 * DM + MM) * (NF // 2)
            A1 = AB + AM * NF

            @block.scalar
            def _(_e):
                z = 1
                b = bank(4 + z)
                A.wait_ge(*up_done(NF - 1))
                if not c3:
                    A.activation(sg[z], b[:, 0:T], ACT.Silu).then_inc(act.sem, 1)
                else:
                    A.activation(gp[z][:, 2:T + 2], b[:, 0:T], ACT.Copy).then_inc(act.sem, 1)
                    A.wait_ge(dve.sem, D1 + 3)
                    A.activation(sg[z], cv[z], ACT.Gelu_apprx_tanh).then_inc(act.sem, 1)

            @block.vector
            def _(_e):
                z = 1
                b = bank(4 + z)
                k = 0
                if c3:
                    V.wait_ge(act.sem, A1 + 1)
                    V.tensor_scalar(cv[z], gp[z][:, 0:T], one(f"conv_w{conv}0", NF - 1), one(f"conv_b{conv}", NF - 1),
                                    ALU.mult, ALU.add).then_inc(dve.sem, 1)
                    for w in (1, 2):
                        V.wait_ge(dve.sem, D1 + w)
                        V.scalar_tensor_tensor(cv[z], gp[z][:, w:w + T], one(f"conv_w{conv}{w}", NF - 1), cv[z],
                                               ALU.mult, ALU.add).then_inc(dve.sem, 1)
                    k = 3
                V.wait_ge(act.sem, A1 + AM - 2)
                V.tensor_tensor(hf[z], sg[z], b[:, T:2 * T], ALU.mult).then_inc(dve.sem, 1)
                V.wait_ge(dve.sem, D1 + k + 1)
                V.wait_ge(*down_done(NF - 3))
                V.tensor_copy(hr[z][:, 0, :], hf[z]).then_inc(dve.sem, 1)
                V.wait_ge(dve.sem, D1 + k + 2)
                V.tensor_tensor(hr[z][:, 1, :], hf[z], whole(hr[z][:, 0, :]), ALU.subtract).then_inc(dve.sem, 1)
            dve.n = D1 + (6 if c3 else 3)
            act.n = A1 + AM - 2
            hidden = (dve.sem, dve.n)

            @block.tensor
            def _(_e):
                pe_down(0, 0, stop=True, last=hidden)
            pe.n = PB + 1 + 2 * NF
            final = (pe.sem, pe.n)
            for k in range(NF):
                Ring.fills[(slots0 + k) % RING] += 1
            Ring.n = slots0 + NF
            Ring.used = [[(dve.sem, D1)] for _ in range(RING)]
            if mod is None:
                return [final]
            mod_loads[0] += MOD_PIECES

            @block.tensor
            def _(_e):
                E.wait_ge(*hidden)
                for c in range(3 * MOD_PIECES):
                    ins = E.matmul(bank(6)[:, c:c + 1], macc[:, c * P:(c + 1) * P], one_col, start=True, stop=True)
                Ring.p = pe.count(ins.then_inc(pe.sem, 1))

            @block.vector
            def _(_e):
                V.wait_ge(*Ring.p)
                vl(V.tensor_tensor(modT[:, 72 * mod[0] + mod0:72 * mod[0] + mod0 + 36], bank(6)[:, 0:36],
                                   prm(f"b_mod{mod[0]}")[:, mod0:mod0 + 36], ALU.add).then_inc(dve.sem, 1))
            return [final, Ring.p]

        def attend(units, keys, ready):
            ar = Arena()
            s_buf = [ar.take(4 * keys).rearrange("p (h k) -> p h k", h=4) for _ in range(2)]
            nblk = max(u["blocks"] for u in units)
            pT = [[ar.take(4 * P) for _ in range(u_blocks)] for u_blocks in
                  [max(u["blocks"] for u in units if u["branch"] == b) for b in sorted({u["branch"] for u in units})]]
            st = ar.take(2 * 16)
            state = {"s_free": [loaded] * 2, "p_free": [loaded] * 2, "t_free": loaded, "o_free": [loaded] * 2,
                     "pT_free": loaded}
            nout = [0]

            def front(n, u):
                q = n % 2
                nk = u["keys"]
                sc = banks(2 * q, 2).rearrange("p (o e k) -> p e o k", o=2, e=2)
                s = s_buf[q]
                stats = st[:, 16 * q:16 * q + 16]
                mx, rs, nm, xtra = (stats[:, 4 * a:4 * a + 4] for a in range(4))

                @block.tensor
                def _(_e):
                    for point in ready:
                        E.wait_ge(*point)
                    E.wait_ge(*state["s_free"][q])
                    for i in range(4):
                        ins = E.matmul(sc[:, i // 2, i % 2, 0:nk], u["q"](i), u["k"](i), start=True, stop=True)
                    Ring.p = pe.count(ins.then_inc(pe.sem, 1))

                @block.vector
                def _(_e):
                    V.wait_ge(*Ring.p)
                    V.wait_ge(*state["p_free"][q])
                    if u["dist"] is not None:
                        for i in range(4):
                            p = dve.count(V.scalar_tensor_tensor(s[:, i, 0:nk], u["dist"], -u["slopes"][i],
                                                                sc[:, i // 2, i % 2, 0:nk], ALU.mult, ALU.add).then_inc(dve.sem, 1))
                        V.wait_ge(*p)
                        state["s_free"][q] = p
                        vl(V.tensor_reduce(mx, s[:, :, 0:nk], AXX, ALU.max).then_inc(dve.sem, 1))
                    else:
                        vl(V.tensor_reduce(mx.rearrange("p (e o) -> p e o", e=2), sc[:, :, :, 0:nk], AXX, ALU.max).then_inc(dve.sem, 1))
                    if u.get("sinks") is not None:
                        vl(V.tensor_tensor(mx, mx, u["sinks"], ALU.max).then_inc(dve.sem, 1))
                        vl(V.tensor_tensor(xtra, u["sinks"], mx, ALU.subtract).then_inc(dve.sem, 1))
                    Ring.p = vl(V.tensor_scalar(nm, mx, -u["scale"], None, ALU.mult).then_inc(dve.sem, 1))

                @block.scalar
                def _(_e):
                    A.wait_ge(*Ring.p)
                    for i in range(4):
                        src = s[:, i, 0:nk] if u["dist"] is not None else sc[:, i // 2, i % 2, 0:nk]
                        p = act.count(A.activation(s[:, i, 0:nk], src, ACT.Exp, bias=nm[:, i:i + 1],
                                                  scale=u["scale"], accum_out=rs[:, i:i + 1]).then_inc(act.sem, 1))
                    if u["dist"] is None:
                        state["s_free"][q] = p
                    if u.get("sinks") is not None:
                        p = act.count(A.activation(xtra, xtra, ACT.Exp).then_inc(act.sem, 1))
                    u["exp"] = p

            def back(n, u):
                q = n % 2
                nk = u["keys"]
                s = s_buf[q]
                stats = st[:, 16 * q:16 * q + 16]
                mx, rs, nm, xtra = (stats[:, 4 * a:4 * a + 4] for a in range(4))

                @block.vector
                def _(_e):
                    V.wait_ge(*u["exp"])
                    if u.get("sinks") is not None:
                        vl(V.tensor_tensor(rs, rs, xtra, ALU.add).then_inc(dve.sem, 1))
                    vl(V.reciprocal(rs, rs).then_inc(dve.sem, 1))
                    if u.get("gates") is not None:
                        vl(V.tensor_tensor(rs, rs, u["gates"], ALU.mult).then_inc(dve.sem, 1))
                    Ring.p = vl(V.tensor_tensor(s[:, :, 0:nk], s[:, :, 0:nk],
                                                spread(rs.rearrange("p (h o) -> p h o", o=1), [P, 4, nk]), ALU.mult).then_inc(dve.sem, 1))
                normed = Ring.p

                @block.tensor
                def _(_e):
                    E.wait_ge(*normed)
                    E.wait_ge(*state["t_free"])
                    for b in range(u["blocks"]):
                        w = min(P, nk - b * P)
                        for i in range(4):
                            ins = E.transpose(bank(4 + b)[0:w, i * P:(i + 1) * P], s[:, i, b * P:b * P + w], ident)
                    Ring.p = pe.count(ins.then_inc(pe.sem, 1))
                state["p_free"][q] = Ring.p

                @block.scalar
                def _(_e):
                    A.wait_ge(*Ring.p)
                    A.wait_ge(*state["pT_free"])
                    for b in range(u["blocks"]):
                        w = min(P, nk - b * P)
                        state["t_free"] = act.count(A.activation(pT[u["branch"]][b][0:w, :], bank(4 + b)[0:w, :],
                                                                ACT.Copy).then_inc(act.sem, 1))
                if not u["last"]:
                    return
                z = nout[0] % 2
                nout[0] += 1
                ob = bank(6 + z)

                @block.tensor
                def _(_e):
                    E.wait_ge(*state["t_free"])
                    E.wait_ge(*state["o_free"][z])
                    for i in range(4):
                        o = ob[(i % 2) * HD:(i % 2 + 1) * HD, (i // 2) * P:(i // 2 + 1) * P]
                        todo = [(v, b) for v in u["parts"] for b in range(v["blocks"])]
                        for m, (v, b) in enumerate(todo):
                            w = min(P, v["keys"] - b * P)
                            ins = E.matmul(o, v["v"](i, b), pT[v["branch"]][b][0:w, i * P:(i + 1) * P],
                                           start=m == 0, stop=m == len(todo) - 1)
                    Ring.p = pe.count(ins.then_inc(pe.sem, 1))
                state["pT_free"] = Ring.p

                @block.vector
                def _(_e):
                    V.wait_ge(*Ring.p)
                    state["o_free"][z] = dve.count(V.tensor_copy(
                        u["out"], ob[:, 0:2 * P].rearrange("p (c n) -> p c n", c=2)).then_inc(dve.sem, 1))

            for n, u in enumerate(units):
                front(n, u)
                if n:
                    back(n - 1, units[n - 1])
            back(len(units) - 1, units[-1])
            ar.close()
            return [(dve.sem, dve.n), (act.sem, act.n), (pe.sem, pe.n)]

        def hybrid(ready):
            ar = Arena()
            r_, k_, v_, ld_, cum_, a_, g_, kk_, bon_ = (ar.take(4 * T) for _ in range(9))
            t12 = ar.take(8 * T)
            t1_, t2_ = t12[:, 0:4 * T], t12[:, 4 * T:8 * T]
            wa, glo = g_[:, 0:T], g_[:, T:2 * T]
            omm = small[:, 16:30]
            omka = small[:, 32:36]
            swa = Arena()
            qT = swa.take(4 * T).rearrange("p (c t) -> p c t", c=4)
            kT = swa.take(2 * T).rearrange("p (c t) -> p c t", c=2)
            vtok = swa.take(NT * P).rearrange("p (t d) -> p t d", t=NT)
            mu = prm("mu")
            proj = Arena()
            h = halves(proj, KC)
            wp = weight_parts(proj, 2)
            h_ready = norm_transpose(prm("mix_pre_g0"), None, ready, h)

            @block.vector
            def _(_e):
                vl(V.tensor_scalar(omm, mu, -1.0, 1.0, ALU.mult, ALU.add).then_inc(dve.sem, 1))
                Ring.q = vl(V.tensor_scalar(omka, prm("k_a"), -1.0, 1.0, ALU.mult, ALU.add).then_inc(dve.sem, 1))
            coef = Ring.q

            def evac(c, b, p):
                if c < 4:
                    @block.scalar
                    def _(_e):
                        A.wait_ge(*p)
                        Ring.q = act.count(A.activation(qT[:, c, :], b[:, 0:T], ACT.Copy, scale=HD ** -0.5).then_inc(act.sem, 1))
                elif c < 6:
                    @block.scalar
                    def _(_e):
                        A.wait_ge(*p)
                        Ring.q = act.count(A.activation(kT[:, c - 4, :], b[:, 0:T], ACT.Copy).then_inc(act.sem, 1))
                elif c == 20:
                    @block.scalar
                    def _(_e):
                        A.wait_ge(*p)
                        Ring.q = act.count(A.activation(vtok, b[:, 0:T].rearrange("p (t d) -> p t d", t=NT), ACT.Copy).then_inc(act.sem, 1))
                else:
                    m = c - 6
                    dst = ([r_] * 4 + [k_] * 4 + [v_] * 4)[m][:, (m % 4) * T:(m % 4 + 1) * T] if m < 12 else \
                        (wa if m == 12 else glo)

                    @block.scalar
                    def _(_e):
                        A.wait_ge(*p)
                        A.wait_ge(*coef)
                        Ring.q = act.count(A.activation(dst, b[:, 0:T], ACT.Copy, scale=omm[:, m:m + 1]).then_inc(act.sem, 1))

                    @block.vector
                    def _(_e):
                        V.wait_ge(*Ring.q)
                        Ring.q = dve.count(V.scalar_tensor_tensor(dst[:, 1:T], b[:, 0:T - 1], mu[:, m:m + 1],
                                                                 dst[:, 1:T], ALU.mult, ALU.add).then_inc(dve.sem, 1))
                return (Ring.q,)

            project("w_hy_in", 21, evac, h_ready, h, wp, tokens=(20,))
            proj.close()
            projected = [(dve.sem, dve.n), (act.sem, act.n), (pe.sem, pe.n)]
            oT = hT

            slopes = alibi(8)
            sinks = prm("sinks")
            units = []
            for g in range(2):
                for t in range(NT):
                    u = dict(branch=0, scale=1.0, slopes=slopes[4 * g:4 * g + 4], sinks=sinks[:, 4 * g:4 * g + 4],
                             keys=(t + 1) * P, blocks=t + 1, last=True,
                             dist=cst("causal0") if t == 0 else cst("window1"),
                             q=lambda i, g=g, t=t: qT[(i % 2) * HD:(i % 2 + 1) * HD, 2 * g + i // 2, t * P:(t + 1) * P],
                             k=lambda i, g=g, t=t: kT[(i % 2) * HD:(i % 2 + 1) * HD, g, 0:(t + 1) * P],
                             v=lambda i, b, g=g: vtok[:, b, g * HD:(g + 1) * HD],
                             out=oT[:, 2 * g:2 * g + 2, t * P:(t + 1) * P])
                    u["parts"] = [u]
                    units.append(u)
            attend(units, T, projected)
            swa.close()
            swa_done = [(dve.sem, dve.n), (act.sem, act.n), (pe.sem, pe.n)]

            r, k, v, ld, cum, a, g, kk, bon, t1, t2 = (
                z.rearrange("p (c t) -> p c t", c=4) for z in (r_, k_, v_, ld_, cum_, a_, g_, kk_, bon_, t1_, t2_))

            @block.scalar
            def _(_e):
                for point in swa_done:
                    A.wait_ge(*point)
                A.activation(wa[0:64, :], wa[0:64, :], ACT.Tanh)
                Ring.p = act.count(A.activation(glo, glo, ACT.Sigmoid).then_inc(act.sem, 1))
            wps, aps, gps = (banks(2 * n, 2).rearrange("p (c t) -> p c t", c=4) for n in range(3))

            @block.tensor
            def _(_e):
                E.wait_ge(*Ring.p)
                for point in swa_done:
                    E.wait_ge(*point)
                wa2, g2 = prm("wa2"), prm("g2")
                for c in range(4):
                    cs = slice(c * P, (c + 1) * P)
                    E.matmul(wps[:, c, :], wa2[0:64, cs], wa[0:64, :], start=True, stop=True)
                    E.matmul(aps[:, c, :], wa2[64:128, cs], wa[64:128, :], start=True, stop=True)
                    ins = E.matmul(gps[:, c, :], g2[:, cs], glo, start=True, stop=True)
                Ring.p = pe.count(ins.then_inc(pe.sem, 1))

            @block.scalar
            def _(_e):
                A.wait_ge(*Ring.p)
                for c in range(4):
                    A.activation(ld[:, c, :], wps[:, c, :], ACT.Sigmoid, bias=prm("w0")[:, c:c + 1])
                Ring.q = act.count(A.activation(a[:, 0, :], aps[:, 0, :], ACT.Sigmoid, bias=prm("a0")[:, 0:1]).then_inc(act.sem, 1))
                for c in range(1, 4):
                    A.activation(a[:, c, :], aps[:, c, :], ACT.Sigmoid, bias=prm("a0")[:, c:c + 1])
                Ring.p = act.count(A.activation(g_, banks(4, 2), ACT.Copy).then_inc(act.sem, 1))

            @block.vector
            def _(_e):
                V.wait_ge(*Ring.q)
                for point in swa_done:
                    V.wait_ge(*point)
                vl(V.tensor_scalar(ld_, ld_, -math.exp(-0.5), None, ALU.mult).then_inc(dve.sem, 1))
                for c in range(4):
                    V.tensor_tensor_scan(cum[:, c, :], cst("scan_keep"), ld[:, c, :], 0.0, ALU.mult, ALU.add)
                for c in range(4):
                    p = dve.count(V.tensor_scalar(kk[:, c, :], k[:, c, :], prm("k_k")[:, c:c + 1], None, ALU.mult).then_inc(dve.sem, 1))
                V.wait_ge(*p)
                Ring.q = vl(V.tensor_tensor(t1_, kk_, kk_, ALU.mult).then_inc(dve.sem, 1))

            def head_sum(src, ready_):
                @block.tensor
                def _(_e):
                    E.wait_ge(*ready_)
                    for h in range(2):
                        ins = E.matmul(bank(6 + h), cst("headsum"), src[:, h * 512:(h + 1) * 512], start=True, stop=True)
                    Ring.p = pe.count(ins.then_inc(pe.sem, 1))
                return Ring.p

            act_gate = Ring.p
            p = head_sum(t1_, Ring.q)

            @block.scalar
            def _(_e):
                A.wait_ge(*p)
                Ring.p = act.count(A.activation(t2_, banks(6, 2), ACT.Sqrt).then_inc(act.sem, 1))

            @block.vector
            def _(_e):
                V.wait_ge(*Ring.p)
                V.wait_ge(*act_gate)
                vl(V.tensor_scalar(t2_, t2_, 1e-12, None, ALU.max).then_inc(dve.sem, 1))
                vl(V.reciprocal(t2_, t2_).then_inc(dve.sem, 1))
                vl(V.tensor_tensor(kk_, kk_, t2_, ALU.mult).then_inc(dve.sem, 1))
                for c in range(4):
                    p_ = dve.count(V.tensor_scalar(t1[:, c, :], a[:, c, :], prm("k_a")[:, c:c + 1], omka[:, c:c + 1],
                                                  ALU.mult, ALU.add).then_inc(dve.sem, 1))
                V.wait_ge(*p_)
                vl(V.tensor_tensor(k_, k_, t1_, ALU.mult).then_inc(dve.sem, 1))
                vl(V.scalar_tensor_tensor(a_, kk_, -1.0, a_, ALU.mult, ALU.mult).then_inc(dve.sem, 1))
                for c in range(4):
                    p_ = dve.count(V.scalar_tensor_tensor(t1[:, c, :], r[:, c, :], prm("r_k")[:, c:c + 1], k[:, c, :],
                                                         ALU.mult, ALU.mult).then_inc(dve.sem, 1))
                Ring.q = p_
            p = head_sum(t1_, Ring.q)

            @block.vector
            def _(_e):
                V.wait_ge(*p)
                vl(V.tensor_tensor(bon_, banks(6, 2), v_, ALU.mult).then_inc(dve.sem, 1))
                Ring.q = vl(V.tensor_tensor(t1_, cum_, ld_, ALU.subtract).then_inc(dve.sem, 1))

            @block.scalar
            def _(_e):
                A.wait_ge(*Ring.q)
                A.activation(t1_, t1_, ACT.Exp)
                A.activation(t2_, cum_, ACT.Exp, scale=-1.0)
                al(A.activation(ld_, cum_, ACT.Exp).then_inc(act.sem, 1))
                Ring.q = (act.sem, act.n)
            e1 = ld

            @block.vector
            def _(_e):
                V.wait_ge(*Ring.q)
                V.tensor_tensor(kk_, kk_, t1_, ALU.mult)
                V.tensor_tensor(a_, a_, t2_, ALU.mult)
                V.tensor_tensor(k_, k_, t2_, ALU.mult)
                Ring.q = vl(V.tensor_tensor(r_, r_, ld_, ALU.mult).then_inc(dve.sem, 1))
            scaled = Ring.q
            kap, bet, kh, rh = kk, a, k, r

            vt = htok_[:, 0:1024].rearrange("p (t d) -> p t d", t=NT)
            bt = htok_[:, 1024:2048].rearrange("p (t d) -> p t d", t=NT)
            kt = cum_.rearrange("p (t d) -> p t d", t=NT)
            n = 0
            for src, dst in ((v, vt), (bet, bt), (kh, kt)):
                for t in range(NT):
                    @block.tensor
                    def _(_e):
                        E.wait_ge(*scaled)
                        for c in range(4):
                            ins = E.transpose(bank(n)[:, c * P:(c + 1) * P], src[:, c, t * P:(t + 1) * P], ident)
                        Ring.p = pe.count(ins.then_inc(pe.sem, 1))

                    @block.scalar
                    def _(_e):
                        A.wait_ge(*Ring.p)
                        Ring.p = act.count(A.activation(dst[:, t, :], bank(n), ACT.Copy).then_inc(act.sem, 1))
                    n += 1
            tok_done = Ring.p

            def mat(t, h):
                return 8 * t + 4 * (h % 2) + h // 2

            L, LT, X, XT, A2 = (ar.take(16 * P).rearrange("p (m s) -> p m s", m=16) for _ in range(5))
            L_, LT_, X_, XT_, A2_ = (z.rearrange("p m s -> p (m s)") for z in (L, LT, X, XT, A2))
            bank_free = [tok_done] * 8

            def gram(lhs, rhs, mask, dst, first, ready_):
                for q in range(4):
                    b = first + q

                    @block.tensor
                    def _(_e):
                        for point in ready_:
                            E.wait_ge(*point)
                        E.wait_ge(*bank_free[b])
                        for m in range(4 * q, 4 * q + 4):
                            t, h = m // 8, 2 * (m % 4) + (m // 4) % 2
                            hs, ts = slice((h % 2) * HD, (h % 2 + 1) * HD), slice(t * P, (t + 1) * P)
                            ins = E.matmul(bank(b)[:, (m % 4) * P:(m % 4 + 1) * P], lhs[hs, h // 2, ts],
                                           rhs[hs, h // 2, ts], start=True, stop=True)
                        Ring.p = pe.count(ins.then_inc(pe.sem, 1))

                    @block.vector
                    def _(_e):
                        V.wait_ge(*Ring.p)
                        bank_free[b] = dve.count(V.tensor_tensor(
                            dst[:, 4 * q:4 * q + 4, :], bank(b).rearrange("p (m s) -> p m s", m=4),
                            spread(mask.rearrange("p (o s) -> p o s", o=1), [P, 4, P]), ALU.mult).then_inc(dve.sem, 1))
                return bank_free[first + 3]

            gram(kap, bet, cst("lower"), L, 0, [scaled])
            gram(bet, kap, cst("upper"), LT, 4, [scaled])
            lev = cst("level").rearrange("p (l s) -> p l s", l=LEVELS)
            levt = cst("level_t").rearrange("p (l s) -> p l s", l=LEVELS)

            def levels(m):
                return spread(m.rearrange("p (o s) -> p o s", o=1), [P, 16, P])

            @block.vector
            def _(_e):
                V.wait_ge(dve.sem, dve.n)
                V.tensor_tensor(X, L, levels(lev[:, 0, :]), ALU.mult)
                vl(V.tensor_tensor(XT, LT, levels(levt[:, 0, :]), ALU.mult).then_inc(dve.sem, 1))
                V.tensor_tensor(X, X, levels(ident), ALU.add)
                Ring.q = vl(V.tensor_tensor(XT, XT, levels(ident), ALU.add).then_inc(dve.sem, 1))
            LMv = t12.rearrange("p (m s) -> p m s", m=16)
            x_ready = Ring.q
            lm_free = x_ready
            for l in range(1, LEVELS):
                lm_pts, t_pts = [], []
                for q in range(4):
                    @block.vector
                    def _(_e):
                        V.wait_ge(*lm_free)
                        lm_pts.append(dve.count(V.tensor_tensor(
                            LMv[:, 4 * q:4 * q + 4, :], LT[:, 4 * q:4 * q + 4, :],
                            spread(levt[:, l:l + 1, :], [P, 4, P]), ALU.mult).then_inc(dve.sem, 1)))
                for q in range(4):
                    @block.tensor
                    def _(_e):
                        E.wait_ge(*lm_pts[q])
                        E.wait_ge(*x_ready)
                        E.wait_ge(*bank_free[q])
                        for m in range(4 * q, 4 * q + 4):
                            ins = E.matmul(bank(q)[:, (m % 4) * P:(m % 4 + 1) * P], LMv[:, m, :], X[:, m, :],
                                           start=True, stop=True)
                        Ring.p = pe.count(ins.then_inc(pe.sem, 1))

                    @block.scalar
                    def _(_e):
                        A.wait_ge(*Ring.p)
                        A.wait_ge(*x_ready)
                        t_pts.append(act.count(A.activation(A2_[:, q * 512:(q + 1) * 512], bank(q), ACT.Copy).then_inc(act.sem, 1)))
                lm_free = Ring.p
                upd = []
                for lhs, rhs, dst, first in ((XT, A2, X_, 4), (A2, XT, XT_, 0)):
                    for q in range(4):
                        @block.tensor
                        def _(_e):
                            E.wait_ge(*t_pts[q])
                            E.wait_ge(*bank_free[first + q])
                            for m in range(4 * q, 4 * q + 4):
                                ins = E.matmul(bank(first + q)[:, (m % 4) * P:(m % 4 + 1) * P], lhs[:, m, :],
                                               rhs[:, m, :], start=True, stop=True)
                            upd.append((pe.count(ins.then_inc(pe.sem, 1)), dst, first + q, q))
                for p, dst, b, q in upd:
                    @block.vector
                    def _(_e):
                        V.wait_ge(*upd[q + 4][0])
                        bank_free[b] = dve.count(V.tensor_tensor(dst[:, q * 512:(q + 1) * 512],
                                                                dst[:, q * 512:(q + 1) * 512], bank(b), ALU.add).then_inc(dve.sem, 1))
                x_ready = bank_free[3]
            inv_done = [x_ready, (pe.sem, pe.n)]
            MT, A1 = L, LT

            @block.vector
            def _(_e):
                for point in inv_done:
                    V.wait_ge(*point)
                V.wait_ge(act.sem, act.n)
            gram(kh, kap, cst("upper"), MT, 0, inv_done)
            gram(bet, rh, cst("upper_in"), A1, 4, inv_done)
            gram(kh, rh, cst("upper_in"), A2, 0, inv_done)
            gram_done = (dve.sem, dve.n)
            ST = ar.take(4 * HD).rearrange("p (c i) -> p c i", c=4)
            MV = X_[:, 0:1024].rearrange("p (t d) -> p t d", t=NT)
            Pv, Uv = t1_[:, 0:512], t1_[:, 512:1024]
            y = t2

            @block.tensor
            def _(_e):
                E.wait_ge(*gram_done)
                for t in range(NT):
                    for h in range(8):
                        hc = slice(h * HD, (h + 1) * HD)
                        E.matmul(bank(4 + t)[:, hc], MT[:, mat(t, h), :], vt[:, t, hc], start=True, stop=True)
                    for h in range(8):
                        ps, hc = slice((h % 2) * HD, (h % 2 + 1) * HD), slice(h * HD, (h + 1) * HD)
                        ins = E.matmul(bank(6 + t)[ps, (h // 2) * P:(h // 2 + 1) * P], vt[:, t, hc],
                                       A2[:, mat(t, h), :], start=True, stop=True)
                Ring.p = pe.count(ins.then_inc(pe.sem, 1))

            @block.vector
            def _(_e):
                V.wait_ge(*Ring.p)
                V.wait_ge(*gram_done)
                V.memset(ST, 0.0)
                V.tensor_copy(MV, banks(4, 2).rearrange("p (t d) -> p t d", t=NT))
                for t in range(NT):
                    Ring.q = vl(V.tensor_copy(y[:, :, t * P:(t + 1) * P], bank(6 + t).rearrange("p (c n) -> p c n", c=4)).then_inc(dve.sem, 1))
            s_ready = Ring.q
            for c4 in range(T // C64):
                t, hb = c4 // 2, (c4 % 2) * 64
                hs = slice(hb, hb + 64)
                tok = slice(t * P + hb, t * P + hb + 64)

                @block.tensor
                def _(_e):
                    E.wait_ge(*s_ready)
                    for h in (0, 2, 4, 6, 1, 3, 5, 7):
                        ps, c = slice((h % 2) * HD, (h % 2 + 1) * HD), h // 2
                        ins = E.matmul(bank(h % 2)[hs, c * HD:(c + 1) * HD], kap[ps, c, tok], ST[ps, c, :],
                                       start=True, stop=True)
                    Ring.p = pe.count(ins.then_inc(pe.sem, 1))

                @block.vector
                def _(_e):
                    V.wait_ge(*Ring.p)
                    for o in range(2):
                        Ring.q = dve.count(V.tensor_tensor(
                            Pv[hs, :].rearrange("p (c o i) -> p c o i", o=2, i=HD)[:, :, o, :],
                            bank(o)[hs, 0:T].rearrange("p (c i) -> p c i", c=4),
                            MV[hs, t, :].rearrange("p (c o i) -> p c o i", o=2, i=HD)[:, :, o, :], ALU.add).then_inc(dve.sem, 1))

                @block.tensor
                def _(_e):
                    E.wait_ge(*Ring.q)
                    for h in range(8):
                        ins = E.matmul(bank(2)[hs, h * HD:(h + 1) * HD], XT[hs, mat(t, h), hs],
                                       Pv[hs, h * HD:(h + 1) * HD], start=True, stop=True)
                    Ring.p = pe.count(ins.then_inc(pe.sem, 1))

                @block.vector
                def _(_e):
                    V.wait_ge(*Ring.p)
                    Ring.q = dve.count(V.tensor_copy(Uv[hs, :], bank(2)[hs, :]).then_inc(dve.sem, 1))

                @block.tensor
                def _(_e):
                    E.wait_ge(*Ring.q)
                    for h in range(8):
                        ps, c = slice((h % 2) * HD, (h % 2 + 1) * HD), h // 2
                        o, hc = bank(3)[ps, c * HD:(c + 1) * HD], slice(h * HD, (h + 1) * HD)
                        E.matmul(o, bt[hs, t, hc], Uv[hs, hc], start=True, stop=False)
                        ins = E.matmul(o, kt[hs, t, hc], vt[hs, t, hc], start=False, stop=True)
                    Ring.p = pe.count(ins.then_inc(pe.sem, 1))
                    for h in range(8):
                        ps, c = slice((h % 2) * HD, (h % 2 + 1) * HD), h // 2
                        E.matmul(bank(6)[ps, c * HD:(c + 1) * HD], Uv[hs, h * HD:(h + 1) * HD],
                                 A1[hs, mat(t, h), hs], start=True, stop=True)
                    for h in (0, 2, 4, 6, 1, 3, 5, 7):
                        ps, c = slice((h % 2) * HD, (h % 2 + 1) * HD), h // 2
                        ins = E.matmul(bank(4 + h % 2)[ps, c * HD:(c + 1) * HD], ST[ps, c, :], rh[ps, c, tok],
                                       start=True, stop=True)
                    Ring.q = pe.count(ins.then_inc(pe.sem, 1))

                @block.vector
                def _(_e):
                    V.wait_ge(*Ring.q)
                    for o in range(2):
                        ps = slice(o * HD, (o + 1) * HD)
                        V.tensor_tensor(y[ps, :, tok], y[ps, :, tok],
                                        bank(4 + o)[ps, 0:T].rearrange("p (c n) -> p c n", c=4), ALU.add)
                    vl(V.tensor_tensor(ST, ST, bank(3)[:, 0:T].rearrange("p (c n) -> p c n", c=4), ALU.add).then_inc(dve.sem, 1))
                    V.tensor_tensor(y[:, :, tok], y[:, :, tok],
                                    bank(6)[:, 0:T].rearrange("p (c n) -> p c n", c=4), ALU.add)
                    Ring.q = vl(V.tensor_tensor(ST, ST, spread(e1[:, :, c4 * 64 + 63:c4 * 64 + 64], [P, 4, HD]), ALU.mult).then_inc(dve.sem, 1))
                s_ready = Ring.q

            p = head_sum(t2_, s_ready)

            @block.vector
            def _(_e):
                V.wait_ge(*p)
                Ring.q = vl(V.scalar_tensor_tensor(t2_, banks(6, 2), -1.0 / HD, t2_, ALU.mult, ALU.add).then_inc(dve.sem, 1))

            @block.scalar
            def _(_e):
                A.wait_ge(*Ring.q)
                Ring.q = act.count(A.activation(t1_, t2_, ACT.Square).then_inc(act.sem, 1))
            p = head_sum(t1_, Ring.q)

            @block.vector
            def _(_e):
                V.wait_ge(*p)
                Ring.q = vl(V.tensor_scalar(t1_, banks(6, 2), 1.0 / HD, 64e-5, ALU.mult, ALU.add).then_inc(dve.sem, 1))

            @block.scalar
            def _(_e):
                A.wait_ge(*Ring.q)
                Ring.q = act.count(A.activation(t1_, t1_, ACT.Sqrt).then_inc(act.sem, 1))

            @block.vector
            def _(_e):
                V.wait_ge(*Ring.q)
                vl(V.reciprocal(t1_, t1_).then_inc(dve.sem, 1))
                vl(V.tensor_tensor(t2_, t2_, t1_, ALU.mult).then_inc(dve.sem, 1))
                for c in range(4):
                    p_ = dve.count(V.tensor_scalar(t2[:, c, :], t2[:, c, :], prm("ln_g")[:, c:c + 1],
                                                  prm("ln_b")[:, c:c + 1], ALU.mult, ALU.add).then_inc(dve.sem, 1))
                V.wait_ge(*p_)
                vl(V.tensor_tensor(t2_, t2_, bon_, ALU.add).then_inc(dve.sem, 1))
                Ring.q = vl(V.tensor_tensor(oT[:, 4:8, :], t2, g, ALU.mult).then_inc(dve.sem, 1))
            ar.close()
            r_row = row_of(prm("mix_post_g0"), 1.0, [Ring.q])
            done = out_project("w_hy_out", 8, oT, [(dve.sem, dve.n), (act.sem, act.n), (pe.sem, pe.n)])
            return add_normed(done + [r_row])

        def nsa(ready):
            ar = Arena()
            qT = ar.take(8 * T).rearrange("p (c t) -> p c t", c=8)
            kc2, vc2, ksT, kwT = (ar.take(4 * T).rearrange("p (c t) -> p c t", c=4) for _ in range(4))
            vs, vw = (ar.take(NT * T).rearrange("p (t d) -> p t d", t=NT) for _ in range(2))
            gates = ar.take(NT * 48).rearrange("p (t n) -> p t n", t=NT)

            def evac(c, b, p):
                @block.scalar
                def _(_e):
                    A.wait_ge(*p)
                    bt = b[:, 0:T]
                    if c < 8:
                        ins = A.activation(qT[:, c, :], bt, ACT.Copy, scale=HD ** -0.5)
                    elif c < 16:
                        dst = (kc2, vc2)[(c - 8) // 4][:, (c - 8) % 4, :]
                        A.activation(dst[0:64, :], bt[0:64, :], ACT.Copy)
                        ins = A.activation(dst[64:128, 0:T - 1], bt[64:128, 1:T], ACT.Copy)
                    elif c < 24:
                        ins = A.activation((ksT, kwT)[(c - 16) // 4][:, (c - 16) % 4, :], bt, ACT.Copy)
                    elif c < 28:
                        m = c - 24
                        ins = A.activation((vs, vw)[m // 2][:, :, (m % 2) * P:(m % 2 + 1) * P],
                                           bt.rearrange("p (t d) -> p t d", t=NT), ACT.Copy)
                    else:
                        ins = A.activation(gates, b[:, 0:96].rearrange("p (t n) -> p t n", t=NT), ACT.Sigmoid)
                    Ring.q = act.count(ins.then_inc(act.sem, 1))
                return (Ring.q,)

            proj = Arena()
            h = halves(proj, KC)
            wp = weight_parts(proj)
            h_ready = norm_transpose(prm("mix_pre_g1"), None, ready, h)
            project("w_ns_in", 29, evac, h_ready, h, wp, tokens=(24, 25, 26, 27, 28), widths={28: 48})
            proj.close()
            projected = [(act.sem, act.n), (dve.sem, dve.n), (pe.sem, pe.n)]
            oT = hT

            @block.scalar
            def _(_e):
                A.wait_ge(pe.sem, pe.n)
            blk = [ar.take(16 * 4 * N_CMP).rearrange("p (j g c) -> p j g c", j=16, g=4) for _ in range(2)]
            hdn = [ar.take(2 * 4 * N_CMP).rearrange("p (f n) -> p f n", f=2) for _ in range(2)]
            kcmp = ar.take(4 * N_CMP).rearrange("p (g c) -> p g c", g=4)
            vcmp = ar.take(4 * HD).rearrange("p (g d) -> p g d", g=4)
            gcmp = ar.take(NT * 16).rearrange("p (t h) -> p t h", t=NT)

            @block.vector
            def _(_e):
                for point in projected:
                    V.wait_ge(*point)
                for kv in range(2):
                    src, pos = (kc2, vc2)[kv], prm("pos_" + "kv"[kv])
                    for j in range(16):
                        p = dve.count(V.tensor_scalar(blk[kv][:, j, :, :], src[:, :, 2 * j:2 * j + 16 * (N_CMP - 1) + 1:16],
                                                     pos[:, j:j + 1], None, ALU.add).then_inc(dve.sem, 1))
                for t in range(NT):
                    p = dve.count(V.tensor_scalar(gcmp[:, t, :], gates[:, t, 0:48:3], cst(f"cmp_any{t}"), None, ALU.mult).then_inc(dve.sem, 1))
                Ring.q = p
            blocks_ready = Ring.q
            for kv in range(2):
                pts = []
                for half in range(2):
                    s, full = load(dram["w_cmp1"][2 * kv + half:2 * kv + half + 1], 1)
                    w = slot_ap(s, 2048).rearrange("p (j f) -> p j f", j=8)
                    pts.append((s, w, full))

                @block.tensor
                def _(_e):
                    E.wait_ge(*blocks_ready)
                    E.wait_ge(*pts[0][2])
                    E.wait_ge(*pts[1][2])
                    for f in range(2):
                        for j in range(16):
                            ins = E.matmul(bank(4 + f)[:, kv * 64:kv * 64 + 60], pts[j // 8][1][:, j % 8, f * P:(f + 1) * P],
                                           blk[kv][:, j, :, :], start=j == 0, stop=j == 15)
                    Ring.p = pe.count(ins.then_inc(pe.sem, 1))
                Ring.used[pts[0][0]] = Ring.used[pts[1][0]] = [Ring.p]

                @block.scalar
                def _(_e):
                    A.wait_ge(*Ring.p)
                    for f in range(2):
                        ins = A.activation(hdn[kv][:, f, :], bank(4 + f)[:, kv * 64:kv * 64 + 60], ACT.Gelu_apprx_tanh)
                    Ring.q = act.count(ins.then_inc(act.sem, 1))

                @block.tensor
                def _(_e):
                    E.wait_ge(*Ring.q)
                    if kv == 0:
                        w2 = prm("cw2_k").rearrange("p (f n) -> p f n", f=2)
                        for f in range(2):
                            ins = E.matmul(bank(6)[:, 0:60], w2[:, f, :], hdn[0][:, f, :], start=f == 0, stop=f == 1)
                    else:
                        w2 = prm("cw2_v").rearrange("p (f n) -> p f n", f=2)
                        for gq in range(4):
                            for f in range(2):
                                ins = E.matmul(bank(7)[0:N_CMP, gq * HD:(gq + 1) * HD],
                                               hdn[1][:, f, gq * N_CMP:(gq + 1) * N_CMP], w2[:, f, :],
                                               start=f == 0, stop=f == 1)
                    Ring.p = pe.count(ins.then_inc(pe.sem, 1))

                @block.scalar
                def _(_e):
                    A.wait_ge(*Ring.p)
                    if kv == 0:
                        al(A.activation(kcmp, bank(6)[:, 0:60].rearrange("p (g c) -> p g c", g=4), ACT.Copy).then_inc(act.sem, 1))
                    else:
                        al(A.activation(vcmp[0:N_CMP], bank(7)[0:N_CMP, 0:4 * HD].rearrange("p (g d) -> p g d", g=4), ACT.Copy).then_inc(act.sem, 1))
            slopes = alibi(16)
            units = []
            for gq in range(4):
                for t in range(NT):
                    parts = []
                    for br in range(3):
                        kk_ = (kcmp, ksT, kwT)[br]
                        nk = N_CMP if br == 0 else (t + 1) * P
                        u = dict(branch=br, scale=1.0, slopes=slopes[4 * gq:4 * gq + 4], keys=nk,
                                 blocks=1 if br == 0 else t + 1, last=br == 2,
                                 dist=cst(f"cmp{t}") if br == 0 else cst(f"causal{t}"),
                                 gates=gcmp[:, t, 4 * gq:4 * gq + 4] if br == 0 else
                                 gates[:, t, 12 * gq + br:12 * gq + 12:3],
                                 q=lambda i, gq=gq, t=t: qT[(i % 2) * HD:(i % 2 + 1) * HD, 2 * gq + i // 2, t * P:(t + 1) * P],
                                 k=lambda i, gq=gq, nk=nk, kk_=kk_: kk_[(i % 2) * HD:(i % 2 + 1) * HD, gq, 0:nk],
                                 out=oT[:, 2 * gq:2 * gq + 2, t * P:(t + 1) * P])
                        if br == 0:
                            u["v"] = lambda i, b, gq=gq: vcmp[0:N_CMP, gq, :]
                        else:
                            u["v"] = lambda i, b, gq=gq, br=br: (vs, vw)[br - 1][:, b, gq * HD:(gq + 1) * HD]
                        parts.append(u)
                        units.append(u)
                    parts[-1]["parts"] = parts
            o_ready = attend(units, T, [(act.sem, act.n), (dve.sem, dve.n), (pe.sem, pe.n)])
            ar.close()
            r_row = row_of(prm("mix_post_g1"), 1.0, o_ready)
            done = out_project("w_ns_out", 8, oT, o_ready)
            return add_normed(done + [r_row])

        def conv_ffn(l, ready):
            ar = Arena()
            h = halves(ar, KC)
            h_ready = norm_transpose(prm(f"ffn_pre_g{l}"), None, ready, h)
            r_row = row_of(prm(f"ffn_post_g{l}"), 1.0, h_ready)
            done = ffn(f"w_conv{l}", h_ready + [r_row], h, ar, conv=l, mod=(0, l))
            ar.close()
            return add_normed(done)

        gm = small[:, 48:56]

        def mod_col(l, s, kind):
            a = l * 72 + (3 * s + kind) * 8
            return modT[:, a:a + 8]

        def modulated(l, s, ready, parts):
            @block.vector
            def _(_e):
                for point in ready:
                    V.wait_ge(*point)
                vl(V.tensor_scalar(gm, mod_col(l, s, 1), 1.0, None, ALU.add).then_inc(dve.sem, 1))
                Ring.q = vl(V.tensor_tensor(gm, gm, prm(f"norm_g{l}{s}"), ALU.mult).then_inc(dve.sem, 1))
            return norm_transpose(gm, mod_col(l, s, 0), list(ready) + [Ring.q], parts)

        def silu_ffn(l, s, w, ready, mod=None):
            ar = Arena()
            h = halves(ar, KC)
            h_ready = modulated(l, s, ready, h)
            r_row = row_of(mod_col(l, s, 2), 0.5, h_ready)
            done = ffn(f"w_ffn{l}{w}", h_ready + [r_row], h, ar, mod=mod)
            ar.close()
            return add_gated(done + [r_row])

        def ssd(ready):
            y_ar, ar = Arena(), None
            xb_ = y_ar.take(16 * T)
            xb = xb_.rearrange("p (c t) -> p c t", t=T)
            ar = Arena()
            zs_ = ar.take(16 * T)
            zs = zs_.rearrange("p (c t) -> p c t", t=T)
            bc = ar.take(16 * T).rearrange("p (c t) -> p c t", t=T)
            pad = [ar.take(T + 4) for _ in range(2)]
            cv = [ar.take(T) for _ in range(2)]
            dt, dtA, acum = (ar.take(NT * 64) for _ in range(3))
            tmp = [ar.take(NT * 64) for _ in range(3)]
            acT = ar.take(T)
            Arow = ar.take(64)
            d3 = lambda z: z.rearrange("p (t n) -> p t n", t=NT)

            proj = Arena()
            h_ = halves(proj, KC)
            wp = weight_parts(proj, 2)
            h_ready = modulated(0, 1, ready, h_)

            @block.vector
            def _(_e):
                for point in h_ready:
                    V.wait_ge(*point)
                for q in range(2):
                    V.memset(pad[q][:, 0:2], 0.0)
                    vl(V.memset(pad[q][:, T + 2:T + 4], 0.0).then_inc(dve.sem, 1))
            pad_ready = (dve.sem, dve.n)
            cv_free = [loaded] * 2

            def evac(c, b, p):
                if c < 16:
                    @block.scalar
                    def _(_e):
                        A.wait_ge(*p)
                        A.wait_ge(*pad_ready)
                        Ring.q = act.count(A.activation(zs[:, c, :], b[:, 0:T], ACT.Silu).then_inc(act.sem, 1))
                    return (Ring.q,)
                if c < 48:
                    m = c - 16
                    q = m % 2

                    @block.scalar
                    def _(_e):
                        A.wait_ge(*p)
                        A.wait_ge(*cv_free[q])
                        Ring.q = act.count(A.activation(pad[q][:, 2:T + 2], b[:, 0:T], ACT.Copy).then_inc(act.sem, 1))
                    freed = Ring.q

                    @block.vector
                    def _(_e):
                        V.wait_ge(*Ring.q)
                        V.wait_ge(*cv_silu[q])
                        vl(V.tensor_scalar(cv[q], pad[q][:, 0:T], prm("sconv_w0")[:, m:m + 1], None, ALU.mult).then_inc(dve.sem, 1))
                        for j in range(1, 5):
                            Ring.q = vl(V.scalar_tensor_tensor(cv[q], pad[q][:, j:j + T], prm(f"sconv_w{j}")[:, m:m + 1],
                                                               cv[q], ALU.mult, ALU.add).then_inc(dve.sem, 1))
                    cv_free[q] = Ring.q
                    pend.append((m, q, Ring.q))
                    if len(pend) > 1:
                        silu_out()
                    return (freed,)
                while pend:
                    silu_out()

                @block.vector
                def _(_e):
                    V.wait_ge(*p)
                    bias = prm("dt_bias")
                    bb = spread(bias.rearrange("p (o n) -> p o n", o=1), [P, NT, 64])
                    vl(V.tensor_tensor(d3(dt), d3(b[:, 0:2 * 64]), bb, ALU.add).then_inc(dve.sem, 1))
                    vl(V.tensor_scalar(tmp[0], dt, -1.0, None, ALU.mult).then_inc(dve.sem, 1))
                    Ring.q = vl(V.tensor_tensor(tmp[0], tmp[0], dt, ALU.min).then_inc(dve.sem, 1))
                return (Ring.q,)

            pend, cv_silu = [], [loaded] * 2

            def silu_out():
                m, q, p = pend.pop(0)

                @block.scalar
                def _(_e):
                    A.wait_ge(*p)
                    cv_silu[q] = act.count(A.activation(xb[:, m, :] if m < 16 else bc[:, m - 16, :], cv[q], ACT.Silu, bias=prm("sconv_b")[:, m:m + 1]).then_inc(act.sem, 1))

            project("w_ssd_in", 49, evac, h_ready, h_, wp, tokens=(48,), widths={48: 64})
            proj.close()
            xt = [hT_[:, :], htok_[:, :]]
            neg_abs = Ring.q

            @block.scalar
            def _(_e):
                A.wait_ge(*neg_abs)
                A.activation(Arow, prm("a_log"), ACT.Exp)
                Ring.q = al(A.activation(tmp[0], tmp[0], ACT.Exp).then_inc(act.sem, 1))

            @block.vector
            def _(_e):
                V.wait_ge(*Ring.q)
                vl(V.tensor_scalar(tmp[1], tmp[0], 2.0, None, ALU.add).then_inc(dve.sem, 1))
                vl(V.reciprocal(tmp[1], tmp[1]).then_inc(dve.sem, 1))
                vl(V.tensor_tensor(tmp[0], tmp[0], tmp[1], ALU.mult).then_inc(dve.sem, 1))
                vl(V.tensor_tensor(tmp[1], tmp[0], tmp[0], ALU.mult).then_inc(dve.sem, 1))
                vl(V.tensor_scalar(tmp[2], tmp[1], 1.0 / 17, 1.0 / 15, ALU.mult, ALU.add).then_inc(dve.sem, 1))
                for n in range(13, 0, -2):
                    vl(V.tensor_tensor(tmp[2], tmp[2], tmp[1], ALU.mult).then_inc(dve.sem, 1))
                    vl(V.tensor_scalar(tmp[2], tmp[2], 1.0 / n, None, ALU.add).then_inc(dve.sem, 1))
                vl(V.tensor_tensor(tmp[2], tmp[2], tmp[0], ALU.mult).then_inc(dve.sem, 1))
                vl(V.tensor_scalar(dt, dt, 0.0, None, ALU.max).then_inc(dve.sem, 1))
                vl(V.scalar_tensor_tensor(dt, tmp[2], 2.0, dt, ALU.mult, ALU.add).then_inc(dve.sem, 1))
                Ring.q = vl(V.scalar_tensor_tensor(d3(dtA), d3(dt), -1.0,
                                                   spread(Arow.rearrange("p (o n) -> p o n", o=1), [P, NT, 64]),
                                                   ALU.mult, ALU.mult).then_inc(dve.sem, 1))
            trif, trib = (cst(n).rearrange("p (u t) -> p u t", u=NT) for n in ("tri_f", "tri_b"))
            in_done = [Ring.q, (act.sem, act.n), (pe.sem, pe.n)]

            @block.tensor
            def _(_e):
                for point in in_done:
                    E.wait_ge(*point)
                for t in range(NT):
                    for d, tri in enumerate((trif, trib)):
                        for u in range(NT):
                            E.matmul(bank(0)[:, t * 64 + d * 32:t * 64 + d * 32 + 32], tri[:, u, t * P:(t + 1) * P],
                                     d3(dtA)[:, u, d * 32:(d + 1) * 32], start=u == 0, stop=u == NT - 1)
                for d, tri in enumerate((trif, trib)):
                    for u in range(NT):
                        ins = E.matmul(bank(1)[d * 32:(d + 1) * 32, 0:T], d3(dtA)[:, u, d * 32:(d + 1) * 32],
                                       tri[:, u, :], start=u == 0, stop=u == NT - 1)
                Ring.p = pe.count(ins.then_inc(pe.sem, 1))

            @block.vector
            def _(_e):
                V.wait_ge(*Ring.p)
                V.tensor_copy(acum, bank(0)[:, 0:NT * 64])
                Ring.q = vl(V.tensor_copy(acT[0:64, :], bank(1)[0:64, 0:T]).then_inc(dve.sem, 1))
            ac_ready = Ring.q
            freed = [loaded] * 4
            for n in range(8):
                t, c0 = n // 4, (n % 4) * 4

                @block.tensor
                def _(_e):
                    for point in in_done:
                        E.wait_ge(*point)
                    E.wait_ge(*freed[n % 4])
                    for c in range(4):
                        ins = E.transpose(bank(4 + n % 4)[:, c * P:(c + 1) * P], xb[:, c0 + c, t * P:(t + 1) * P], ident)
                    Ring.p = pe.count(ins.then_inc(pe.sem, 1))

                @block.scalar
                def _(_e):
                    A.wait_ge(*Ring.p)
                    freed[n % 4] = act.count(A.activation(xt[t][:, c0 * P:(c0 + 4) * P], bank(4 + n % 4), ACT.Copy).then_inc(act.sem, 1))
            xt_ready = freed[3]
            G_ = [ar.take(768) for _ in range(2)]
            xd = [ar.take(NT * 2 * T).rearrange("p (u d n) -> p u d n", u=NT, d=2) for _ in range(2)]
            ee = [ar.take(768) for _ in range(3)]
            ee_free, g_free, arow_free, y_free = [loaded] * 3, [loaded] * 2, [loaded] * 2, [loaded] * 2
            ee_ready = [loaded] * 3
            acu, dt3 = d3(acum), d3(dt)
            negf, negb = cst("neg_f"), cst("neg_b")
            g_state = {}

            def group(gi):
                q = gi % 2

                @block.tensor
                def _(_e):
                    E.wait_ge(*xt_ready)
                    E.wait_ge(*ac_ready)
                    E.wait_ge(*g_free[q])
                    E.wait_ge(*g_state.get("psum", loaded))
                    for u in range(NT):
                        ins = E.matmul(bank(4)[:, u * T:(u + 1) * T], bc[:, gi, u * P:(u + 1) * P],
                                       bc[:, 8 + gi, :], start=True, stop=True)
                    Ring.p = pe.count(ins.then_inc(pe.sem, 1))

                @block.scalar
                def _(_e):
                    A.wait_ge(*Ring.p)
                    A.wait_ge(*g_free[q])
                    b = bank(4)
                    A.activation(G_[q][:, 0:256], b[:, 0:256], ACT.Copy)
                    A.activation(G_[q][:, 256:384], b[:, 384:512], ACT.Copy)
                    A.activation(G_[q][:, 384:512], b[:, 0:128], ACT.Copy)
                    Ring.q = act.count(A.activation(G_[q][:, 512:768], b[:, 256:512], ACT.Copy).then_inc(act.sem, 1))
                g_state["psum"] = g_state["G", q] = Ring.q

                @block.vector
                def _(_e):
                    V.wait_ge(*xt_ready)
                    V.wait_ge(*ac_ready)
                    V.wait_ge(*g_free[q])
                    for u in range(NT):
                        for d in range(2):
                            dd = dt3[:, u, d * 32 + 4 * gi:d * 32 + 4 * gi + 4].rearrange("p (r o) -> p r o", o=1)
                            Ring.q = dve.count(V.tensor_tensor(
                                xd[q][:, u, d, :].rearrange("p (r n) -> p r n", r=4),
                                xt[u][:, gi * T:(gi + 1) * T].rearrange("p (r n) -> p r n", r=4),
                                spread(dd, [P, 4, HD]), ALU.mult).then_inc(dve.sem, 1))
                g_state["x", q] = Ring.q

            def front(h):
                b = bank(h % 2)
                e = ee[h % 3]

                @block.tensor
                def _(_e):
                    E.wait_ge(*ac_ready)
                    E.wait_ge(*arow_free[h % 2])
                    for d in range(2):
                        ins = E.matmul(b[:, d * T:(d + 1) * T], spread(ident[0:64, d * 32 + h:d * 32 + h + 1], [64, P]),
                                       acT[0:64, :], start=True, stop=True)
                    Ring.p = pe.count(ins.then_inc(pe.sem, 1))

                @block.vector
                def _(_e):
                    V.wait_ge(*Ring.p)
                    V.wait_ge(*ee_free[h % 3])
                    for lo, w, src, u, d, neg in ((0, 128, 0, 0, 0, negf), (256, 128, 128, 1, 0, negf),
                                                  (384, 128, T, 0, 1, negb), (640, 128, T + 128, 1, 1, negb)):
                        V.scalar_tensor_tensor(e[:, lo:lo + w], b[:, src:src + w], acu[:, u, d * 32 + h:d * 32 + h + 1],
                                               neg, ALU.subtract, ALU.add)
                    V.tensor_scalar(e[:, 128:256], b[:, 128:256], acu[:, 0, h:h + 1], None, ALU.subtract)
                    arow_free[h % 2] = dve.count(V.tensor_scalar(e[:, 512:640], b[:, T:T + 128],
                                                                acu[:, 1, 32 + h:33 + h], None, ALU.subtract).then_inc(dve.sem, 1))

                @block.scalar
                def _(_e):
                    A.wait_ge(*arow_free[h % 2])
                    ee_ready[h % 3] = act.count(A.activation(e, e, ACT.Exp).then_inc(act.sem, 1))

            def back(h):
                gi, rr, q = h // 4, h % 4, (h // 4) % 2
                e = ee[h % 3]

                @block.vector
                def _(_e):
                    V.wait_ge(*ee_ready[h % 3])
                    V.wait_ge(*g_state["G", q])
                    Ring.q = dve.count(V.tensor_tensor(e, e, G_[q], ALU.mult).then_inc(dve.sem, 1))
                hp = (h % 2) * HD
                yb = bank(2 + (h // 2) % 2)

                @block.tensor
                def _(_e):
                    E.wait_ge(*Ring.q)
                    E.wait_ge(*g_state["x", q])
                    E.wait_ge(*(y_free[(h // 2) % 2] if h % 2 == 0 else loaded))
                    o = yb[hp:hp + HD, 0:T]
                    xr = lambda u, d: xd[q][:, u, d, rr * HD:(rr + 1) * HD]
                    E.matmul(o, xr(0, 0), e[:, 0:256], start=True, stop=False)
                    E.matmul(o, xr(1, 1), e[:, 512:768], start=False, stop=False)
                    E.matmul(o[:, 128:256], xr(1, 0), e[:, 256:384], start=False, stop=False)
                    ins = E.matmul(o[:, 0:128], xr(0, 1), e[:, 384:512], start=False, stop=True)
                    ee_free[h % 3] = pe.count(ins.then_inc(pe.sem, 1))
                if h % 4 == 3:
                    g_free[q] = ee_free[h % 3]
                if h % 2:
                    c = h // 2

                    @block.vector
                    def _(_e):
                        V.wait_ge(*ee_free[h % 3])
                        y_free[c % 2] = vl(V.scalar_tensor_tensor(xb[:, c, :], xb[:, c, :], prm("d_skip")[:, c:c + 1],
                                                                  yb[:, 0:T], ALU.mult, ALU.add).then_inc(dve.sem, 1))
                        vl(V.tensor_tensor(xb[:, c, :], xb[:, c, :], zs[:, c, :], ALU.mult).then_inc(dve.sem, 1))

            group(0)
            for h in range(32):
                front(h)
                if h % 4 == 1 and h // 4 + 1 < 8:
                    group(h // 4 + 1)
                if h:
                    back(h - 1)
            back(31)
            y_done = [(dve.sem, dve.n), (pe.sem, pe.n)]

            sq = zs_
            inv = htok_[:, :]

            @block.scalar
            def _(_e):
                for point in y_done:
                    A.wait_ge(*point)
                Ring.q = act.count(A.activation(sq, xb_, ACT.Square).then_inc(act.sem, 1))

            @block.vector
            def _(_e):
                for point in y_done:
                    V.wait_ge(*point)
                Ring.p = dve.count(V.memset(Arow[:, 0:1], 1.0).then_inc(dve.sem, 1))

            @block.tensor
            def _(_e):
                E.wait_ge(*Ring.q)
                E.wait_ge(*Ring.p)
                for gi in range(8):
                    for c in range(2):
                        ins = E.matmul(banks(gi // 2, 1)[:, (gi % 2) * T:(gi % 2 + 1) * T], spread(Arow[:, 0:1], [P, P]),
                                       zs[:, 2 * gi + c, :], start=c == 0, stop=c == 1)
                Ring.p = pe.count(ins.then_inc(pe.sem, 1))

            @block.vector
            def _(_e):
                V.wait_ge(*Ring.p)
                Ring.q = vl(V.tensor_scalar(inv, banks(0, 4), 1.0 / T, EPS, ALU.mult, ALU.add).then_inc(dve.sem, 1))

            @block.scalar
            def _(_e):
                A.wait_ge(*Ring.q)
                Ring.q = act.count(A.activation(inv, inv, ACT.Sqrt).then_inc(act.sem, 1))

            @block.vector
            def _(_e):
                V.wait_ge(*Ring.q)
                vl(V.reciprocal(inv, inv).then_inc(dve.sem, 1))
                for c in range(16):
                    Ring.q = dve.count(V.scalar_tensor_tensor(xb[:, c, :], xb[:, c, :], prm("snorm_g")[:, c:c + 1],
                                                             inv[:, (c // 2) * T:(c // 2 + 1) * T], ALU.mult, ALU.mult).then_inc(dve.sem, 1))
            ar.close()
            r_row = row_of(mod_col(0, 1, 2), 1.0, [Ring.q])
            done = out_project("w_ssd_out", 16, xb, [(dve.sem, dve.n), (act.sem, act.n), (pe.sem, pe.n)])
            y_ar.close()
            return add_gated(done + [r_row])

        def mla(ready):
            ar = Arena()
            zt = ar.take(NT * 672).rearrange("p (t n) -> p t n", t=NT)
            qlT = ar.take(3 * T).rearrange("p (c t) -> p c t", c=3)
            klT = ar.take(2 * T).rearrange("p (c t) -> p c t", c=2)
            vt = ar.take(NT * 1024).rearrange("p (t h n) -> p t h n", t=NT, h=16)
            qT = ar.take(16 * T).rearrange("p (h t) -> p h t", h=16)
            kT = ar.take(16 * T).rearrange("p (h t) -> p h t", h=16)
            qk = Arena()
            qt = qk.take(NT * 1536).rearrange("p (t h n) -> p t h n", t=NT, h=16)
            kt = qk.take(NT * 1536).rearrange("p (t h n) -> p t h n", t=NT, h=16)
            h_ready = modulated(1, 1, ready, None)
            ang, cosr, sinr, rn = (small[:, 64 + 32 * n:96 + 32 * n] for n in range(4))
            sc = small[:, 192:256]
            t3 = lambda z, n: z.rearrange("p (t n) -> p t n", t=n)

            def evac(c, b, p):
                w = 32 if c == 5 else P

                @block.scalar
                def _(_e):
                    A.wait_ge(*p)
                    Ring.q = act.count(A.activation(zt[:, :, c * P:c * P + w],
                                                   b[:, 0:2 * w].rearrange("p (t d) -> p t d", t=NT), ACT.Copy).then_inc(act.sem, 1))
                return (Ring.q,)
            project("w_mla_in", 6, evac, h_ready, None, (), tokens=range(6), widths={5: 32})
            z_ready = Ring.q
            ss = small[:, 0:4]

            @block.scalar
            def _(_e):
                A.wait_ge(*z_ready)
                for t in range(NT):
                    al(A.activation(htok[:, 0, 0:384], zt[:, t, 0:384], ACT.Square, accum_out=ss[:, t:t + 1]).then_inc(act.sem, 1))
                    Ring.q = al(A.activation(htok[:, 1, 0:256], zt[:, t, 384:640], ACT.Square, accum_out=ss[:, 2 + t:3 + t]).then_inc(act.sem, 1))

            @block.vector
            def _(_e):
                V.wait_ge(*Ring.q)
                V.tensor_scalar(ss[:, 0:2], ss[:, 0:2], 1.0 / 384, EPS, ALU.mult, ALU.add)
                Ring.q = vl(V.tensor_scalar(ss[:, 2:4], ss[:, 2:4], 1.0 / 256, EPS, ALU.mult, ALU.add).then_inc(dve.sem, 1))
                V.tensor_copy(sc[:, 0:NT], posi[:, :])
                vl(V.memset(rn, 0.0).then_inc(dve.sem, 1))
                for t in range(NT):
                    vl(V.tensor_scalar(ang[:, 16 * t:16 * t + 16], cst("inv_freq"), sc[:, t:t + 1], None, ALU.mult).then_inc(dve.sem, 1))
                two_pi = 2 * math.pi
                c1 = 6.28125
                c2 = float(np.float32(math.floor((two_pi - c1) * 2 ** 20) / 2 ** 20))
                c3 = two_pi - c1 - c2
                magic = 12582912.0
                lim = 3.1415925
                for dst, quarter in ((sinr, 0.0), (cosr, 0.25)):
                    vl(V.tensor_scalar(rn, ang, 1.0 / two_pi, quarter, ALU.mult, ALU.add).then_inc(dve.sem, 1))
                    vl(V.tensor_scalar(rn, rn, magic, None, ALU.add).then_inc(dve.sem, 1))
                    vl(V.tensor_scalar(rn, rn, -magic, None, ALU.add).then_inc(dve.sem, 1))
                    vl(V.scalar_tensor_tensor(dst, rn, -c1, ang, ALU.mult, ALU.add).then_inc(dve.sem, 1))
                    vl(V.scalar_tensor_tensor(dst, rn, -c2, dst, ALU.mult, ALU.add).then_inc(dve.sem, 1))
                    vl(V.scalar_tensor_tensor(dst, rn, -c3, dst, ALU.mult, ALU.add).then_inc(dve.sem, 1))
                    if quarter:
                        vl(V.tensor_scalar(dst, dst, math.pi / 2, None, ALU.add).then_inc(dve.sem, 1))
                    Ring.p = vl(V.tensor_scalar(dst, dst, lim, -lim, ALU.min, ALU.max).then_inc(dve.sem, 1))

            @block.scalar
            def _(_e):
                A.wait_ge(*Ring.q)
                Ring.q = act.count(A.activation(ss, ss, ACT.Sqrt).then_inc(act.sem, 1))
                A.wait_ge(*Ring.p)
                A.activation(sinr, sinr, ACT.Sin)
                Ring.p = act.count(A.activation(cosr, cosr, ACT.Sin).then_inc(act.sem, 1))
            rope_ready = Ring.p

            @block.vector
            def _(_e):
                V.wait_ge(*Ring.q)
                vl(V.reciprocal(ss, ss).then_inc(dve.sem, 1))
                for t in range(NT):
                    V.tensor_scalar(zt[:, t, 0:384], zt[:, t, 0:384], ss[:, t:t + 1], None, ALU.mult)
                    Ring.q = dve.count(V.tensor_scalar(zt[:, t, 384:640], zt[:, t, 384:640], ss[:, 2 + t:3 + t], None, ALU.mult).then_inc(dve.sem, 1))
            lat = Ring.q
            pts = []
            for c in range(5):
                @block.tensor
                def _(_e):
                    E.wait_ge(*lat)
                    for t in range(NT):
                        ins = E.transpose(bank(c)[:, t * P:(t + 1) * P], zt[:, t, c * P:(c + 1) * P], ident)
                    Ring.p = pe.count(ins.then_inc(pe.sem, 1))

                @block.vector
                def _(_e):
                    V.wait_ge(*Ring.p)
                    dst = qlT[:, c, :] if c < 3 else klT[:, c - 3, :]
                    gain = prm("q_norm_g")[:, c:c + 1] if c < 3 else prm("kv_norm_g")[:, c - 3:c - 2]
                    pts.append(dve.count(V.tensor_scalar(dst, bank(c)[:, 0:T], gain, None, ALU.mult).then_inc(dve.sem, 1)))
            lat_ready = pts[-1]
            freed = [lat_ready] * 8
            n = 0
            for name, nb_, kk_, src in (("w_uq", 3, 3, qlT), ("w_ukv", 4, 2, klT)):
                for c in range(nb_):
                    s, full = load(dram[name][c:c + 1], 1)
                    w = slot_ap(s, kk_ * 512).rearrange("p (k n) -> p k n", k=kk_)
                    for t in range(NT):
                        b = n % 8
                        n += 1

                        @block.tensor
                        def _(_e):
                            E.wait_ge(*full)
                            E.wait_ge(*lat_ready)
                            E.wait_ge(*freed[b])
                            for k in range(kk_):
                                ins = E.matmul(bank(b), src[:, k, t * P:(t + 1) * P], w[:, k, :],
                                               start=k == 0, stop=k == kk_ - 1)
                            Ring.p = pe.count(ins.then_inc(pe.sem, 1))

                        @block.scalar
                        def _(_e):
                            A.wait_ge(*Ring.p)
                            if name == "w_uq":
                                ins = A.activation(qt[:, t].rearrange("p h n -> p (h n)")[:, c * 512:(c + 1) * 512],
                                                   bank(b), ACT.Copy)
                            else:
                                v4 = bank(b).rearrange("p (h n) -> p h n", h=4)
                                A.activation(kt[:, t, 4 * c:4 * c + 4, 0:64], v4[:, :, 0:64], ACT.Copy)
                                ins = A.activation(vt[:, t, 4 * c:4 * c + 4, :], v4[:, :, 64:128], ACT.Copy)
                            freed[b] = act.count(ins.then_inc(act.sem, 1))
                    Ring.used[s] = [(pe.sem, pe.n)]
            up_ready = (act.sem, act.n)
            scr = qT.rearrange("p h t -> p (h t)")[:, 0:1536].rearrange("p (h n) -> p h n", h=16)
            rot = kT.rearrange("p h t -> p (h t)")[:, 0:1024].rearrange("p (a h n) -> p a h n", a=4, h=16)
            hs_ = sc.rearrange("p (a t h) -> p a t h", a=2, t=NT)

            @block.vector
            def _(_e):
                V.wait_ge(*up_ready)
                for t in range(NT):
                    vl(V.tensor_copy(kt[:, t, :, 64:96], spread(zt[:, t, 640:672].rearrange("p (o n) -> p o n", o=1),
                                                                [P, 16, 32])).then_inc(dve.sem, 1))
                for a_, src in enumerate((qt, kt)):
                    for t in range(NT):
                        vl(V.tensor_tensor(scr, src[:, t], src[:, t], ALU.mult).then_inc(dve.sem, 1))
                        vl(V.tensor_reduce(hs_[:, a_, t, :], scr, AXX, ALU.add).then_inc(dve.sem, 1))
                Ring.q = (dve.sem, dve.n)
            rstd_of(sc, 64, 1.0 / 96, EPS, Ring.q)

            @block.vector
            def _(_e):
                V.wait_ge(*rope_ready)
                for a_, (src, gain) in enumerate(((qt, prm("q_head_g")), (kt, prm("k_head_g")))):
                    for t in range(NT):
                        vl(V.tensor_tensor(src[:, t], src[:, t], spread(hs_[:, a_, t, :].rearrange("p (h o) -> p h o", o=1),
                                                                        [P, 16, 96]), ALU.mult).then_inc(dve.sem, 1))
                        vl(V.tensor_tensor(src[:, t], src[:, t], spread(gain.rearrange("p (o n) -> p o n", o=1),
                                                                        [P, 16, 96]), ALU.mult).then_inc(dve.sem, 1))
                        co, si = (spread(z[:, 16 * t:16 * t + 16].rearrange("p (o n) -> p o n", o=1), [P, 16, 16])
                                  for z in (cosr, sinr))
                        x1, x2 = src[:, t, :, 64:80], src[:, t, :, 80:96]
                        V.tensor_tensor(rot[:, 0], x1, co, ALU.mult)
                        V.tensor_tensor(rot[:, 1], x2, si, ALU.mult)
                        V.tensor_tensor(rot[:, 2], x2, co, ALU.mult)
                        vl(V.tensor_tensor(rot[:, 3], x1, si, ALU.mult).then_inc(dve.sem, 1))
                        V.tensor_tensor(x1, rot[:, 0], rot[:, 1], ALU.subtract)
                        vl(V.tensor_tensor(x2, rot[:, 2], rot[:, 3], ALU.add).then_inc(dve.sem, 1))
                Ring.q = (dve.sem, dve.n)
            roped = Ring.q
            n = 0
            for src, dst in ((qt, qT), (kt, kT)):
                for t in range(NT):
                    for h0 in range(0, 16, 4):
                        b = n % 8
                        n += 1

                        @block.tensor
                        def _(_e):
                            E.wait_ge(*roped)
                            E.wait_ge(*freed[b])
                            for i in range(4):
                                ins = E.transpose(bank(b)[0:96, i * P:(i + 1) * P], src[:, t, h0 + i, :], ident)
                            Ring.p = pe.count(ins.then_inc(pe.sem, 1))

                        @block.scalar
                        def _(_e):
                            A.wait_ge(*Ring.p)
                            A.wait_ge(*roped)
                            freed[b] = act.count(A.activation(dst[0:96, h0:h0 + 4, t * P:(t + 1) * P],
                                                             bank(b)[0:96, :].rearrange("p (h n) -> p h n", h=4), ACT.Copy).then_inc(act.sem, 1))
            oT = hT
            qk.close()
            units = []
            for gq in range(4):
                for t in range(NT):
                    u = dict(branch=0, scale=96 ** -0.5, keys=T, blocks=2, last=True, dist=None,
                             q=lambda i, gq=gq, t=t: qT[0:96, 4 * gq + i, t * P:(t + 1) * P],
                             k=lambda i, gq=gq: kT[0:96, 4 * gq + i, :],
                             v=lambda i, b, gq=gq: vt[:, b, 4 * gq + i, :],
                             out=oT[:, 2 * gq:2 * gq + 2, t * P:(t + 1) * P])
                    u["parts"] = [u]
                    units.append(u)
            o_ready = attend(units, T, [(act.sem, act.n), (pe.sem, pe.n), (dve.sem, dve.n)])
            ar.close()
            r_row = row_of(mod_col(1, 1, 2), 1.0, o_ready)
            done = out_project("w_mla_out", 8, oT, o_ready)
            return add_gated(done + [r_row])

        @block.scalar
        def _(_e):
            Ring.q = al(A.activation(cond, prm("c"), ACT.Silu).then_inc(act.sem, 1))

        @block.vector
        def _(_e):
            V.wait_ge(*Ring.q)
            vl(V.memset(one_col, 1.0).then_inc(dve.sem, 1))

        stages = [hybrid, lambda r: conv_ffn(0, r), nsa, lambda r: conv_ffn(1, r),
                  lambda r: silu_ffn(0, 0, 0, r, (1, 0)), ssd, lambda r: silu_ffn(0, 2, 1, r, (1, 1)),
                  lambda r: silu_ffn(1, 0, 0, r), mla, lambda r: silu_ffn(1, 2, 1, r)]
        at = [(act.sem, act.n), (dve.sem, dve.n)]
        for n, stage in enumerate(stages):
            if dbg is not None and n not in dbg:
                continue
            at = stage(at)

        @block.sync
        def _(sp):
            for point in at:
                sp.wait_ge(*point)
            sp.dma_start(out, xs_[:, :]).then_inc(stored, 16)
            sp.wait_ge(stored, 16)


def kernel(**inputs):
    import concourse.bacc as bacc
    from concourse.bass_utils import run_bass_kernel_spmd

    arrays, pat = lay_out(inputs)
    cat = constant_table()[1]
    nc = bacc.Bacc("TRN2", target_bir_lowering=False, num_devices=1)
    dram = {}
    for name, a in arrays.items():
        dram[name] = nc.dram_tensor("in_" + name, a.shape, mybir.dt.from_np(a.dtype), kind="ExternalInput").ap()
    out = nc.dram_tensor("out_x", (P, NT * D), F32, kind="ExternalOutput").ap()
    build(nc, dram, out, pat, cat)
    r = run_bass_kernel_spmd(nc, [{"in_" + n: a for n, a in arrays.items()}], core_ids=[0])
    y = r.results[0]["out_x"].reshape(P, NT, D).transpose(1, 0, 2).reshape(1, T, D)
    return np.ascontiguousarray(y)
```

```python
import math
from contextlib import ExitStack

import numpy as np
import concourse.bass as bass
from concourse import mybir

F32 = mybir.dt.float32
F32R = mybir.dt.float32r
I32 = mybir.dt.int32
ALU = mybir.AluOpType
ACT = mybir.ActivationFunctionType
AXX = mybir.AxisListType.X

P = 128
T = 256
NT = T // P
D = 1024
KC = D // P
DFF = 2816
NF = DFF // P
HD = 64
EPS = 1e-6
BIG = 1e30
CHUNK = 1024
RING = 4
SLOT = 3 * CHUNK
C64 = 64
LEVELS = 6
N_CMP = (T - 32) // 16 + 1


def alibi(n):
    return [2.0 ** (-8.0 * (i + 1) / n) for i in range(n)]


def constant_table():
    i = np.arange(P)
    col, row = i[None, :], i[:, None]
    out, at, pos = [], {}, 0

    def add(name, a):
        nonlocal pos
        a = np.ascontiguousarray(a, dtype=np.float32).reshape(P, -1)
        at[name] = (pos, a.shape[1])
        pos += a.shape[1]
        out.append(a)

    add("ident", np.eye(P))
    add("headsum", (row // HD == col // HD))
    same = row // C64 == col // C64
    add("lower", same & (col < row))
    add("upper", same & (col > row))
    add("upper_in", same & (col >= row))
    levels, levels_t = [], []
    for l in range(LEVELS):
        m = 1 << l
        low = (row // (2 * m) == col // (2 * m)) & (row % (2 * m) >= m) & (col % (2 * m) < m)
        levels.append(low)
        levels_t.append(low.T)
    add("level", np.stack(levels, 1))
    add("level_t", np.stack(levels_t, 1))
    t = np.arange(T)
    add("scan_keep", np.broadcast_to(t % C64 != 0, (P, T)))
    dist = (i[:, None] - i[None, :]).astype(np.float32)
    add("causal0", np.where(dist >= 0, dist, BIG))
    dist1 = (P + i[:, None] - t[None, :]).astype(np.float32)
    add("causal1", np.where(dist1 >= 0, dist1, BIG))
    add("window1", np.where((dist1 >= 0) & (dist1 < 128), dist1, BIG))
    ends = np.arange(N_CMP) * 16 + 31
    for n in range(NT):
        dc = (n * P + i)[:, None] - ends[None, :]
        add(f"cmp{n}", np.where(dc >= 0, dc, BIG))
        add(f"cmp_any{n}", ((n * P + i)[:, None] >= 31))
    u = (np.arange(NT)[:, None] * P + i[None, :]).T[:, :, None]
    add("tri_f", u <= t[None, None, :])
    add("tri_b", u >= t[None, None, :])
    add("neg_f", np.where(row <= col, 0.0, -BIG))
    add("neg_b", np.where(row >= col, 0.0, -BIG))
    add("inv_freq", np.broadcast_to(10000.0 ** (-np.arange(0, 32, 2) / 32.0), (P, 16)))
    return np.concatenate(out, 1), at


def cols(v):
    return np.asarray(v).reshape(-1, P).T


def col_chunks(w):
    w = np.asarray(w)
    n = w.shape[1] // P
    return np.ascontiguousarray(w.reshape(KC, P, n, P).transpose(2, 1, 0, 3)).reshape(n, P, CHUNK)


def row_chunks(w):
    w = np.asarray(w)
    return np.ascontiguousarray(w.reshape(-1, P, D))


def ffn_chunks(gate, up, down):
    return np.stack([col_chunks(gate), col_chunks(up), row_chunks(down)], 1)


def twice(w, heads):
    w = np.asarray(w).reshape(w.shape[0], heads, HD)
    return np.concatenate([w, w], 2).reshape(w.shape[0], heads * P)


def padded(w, n):
    w = np.asarray(w)
    return np.concatenate([w, np.zeros((w.shape[0], n - w.shape[1]), w.dtype)], 1)


def lay_out(i):
    i = {k: np.asarray(v) for k, v in i.items()}
    params, at, pos = [], {}, 0

    def add(name, a):
        nonlocal pos
        a = np.asarray(a)
        a = a.reshape(P, -1)
        at[name] = (pos, a.shape[1])
        pos += a.shape[1]
        params.append(a)

    def row(name, v):
        v = np.asarray(v).reshape(-1)
        add(name, np.broadcast_to(v, (P, v.size)))

    for name in ("mix_pre_g", "mix_post_g", "ffn_pre_g", "ffn_post_g"):
        for l in range(2):
            add(f"{name}{l}", cols(i[name][l]))
    add("mu", cols(i["rwkv_mu"][0]))
    for name in ("w0", "a0", "k_k", "k_a", "ln_g", "ln_b"):
        add(name, cols(i["rwkv_" + name][0]))
    add("r_k", cols(i["rwkv_r_k"][0].reshape(-1)))
    add("wa2", np.concatenate([i["rwkv_w2"][0], i["rwkv_a2"][0]], 0))
    add("g2", i["rwkv_g2"][0])
    row("sinks", i["swa_sinks"][0])
    for l in range(2):
        for j in range(3):
            add(f"conv_w{l}{j}", cols(i["ffn_conv_w"][l, j]))
        add(f"conv_b{l}", cols(i["ffn_conv_b"][l]))
    for l in range(2):
        for s in range(3):
            add(f"norm_g{l}{s}", cols(i["norm_g_2"][l, s]))
        add(f"b_mod{l}", cols(i["b_mod_2"][l]))
    add("c", cols(i["c_2"][0]))
    for kv in "kv":
        pos_ = i[f"nsa_cmp_pos_{kv}"][0]
        add("pos_" + kv, pos_.reshape(16, 2, HD).transpose(1, 2, 0).reshape(P, 16))
    w2k = i["nsa_cmp_w2_k"][0].reshape(2, P, HD).transpose(1, 0, 2)
    add("cw2_k", np.concatenate([w2k, w2k], 2))
    add("cw2_v", i["nsa_cmp_w2_v"][0].reshape(2, P, HD).transpose(1, 0, 2))
    for j in range(5):
        add(f"sconv_w{j}", cols(i["ssd_conv_w_2"][0, j]))
    add("sconv_b", cols(i["ssd_conv_b_2"][0]))
    add("snorm_g", cols(i["ssd_norm_g_2"][0]))
    add("d_skip", cols(np.repeat(i["ssd_d_2"][0], HD)))
    row("dt_bias", i["ssd_dt_bias_2"][0])
    row("a_log", i["ssd_a_log_2"][0])
    add("q_norm_g", cols(i["mla_q_norm_g_2"][0]))
    add("kv_norm_g", cols(i["mla_kv_norm_g_2"][0]))
    row("q_head_g", i["mla_q_head_g_2"][0])
    row("k_head_g", i["mla_k_head_g_2"][0])

    hy = i["hy_w_in"][0]
    hy = np.concatenate([hy[:, 0:512], twice(hy[:, 512:640], 2), hy[:, 768:2560], hy[:, 640:768]], 1)
    ns = i["nsa_w_in"][0]
    kc, vc, ks, vs, kw, vw = (ns[:, 1024 + 256 * j:1280 + 256 * j] for j in range(6))
    ns = np.concatenate([ns[:, 0:1024], twice(kc, 4), twice(vc, 4), twice(ks, 4), twice(kw, 4), vs, vw,
                         padded(ns[:, 2560:2608], P)], 1)
    cw1 = [i[f"nsa_cmp_w1_{kv}"][0].reshape(2, 8, 2, HD, 256).transpose(0, 2, 3, 1, 4).reshape(2, P, 2048)
           for kv in "kv"]
    arrays = {
        "x": np.ascontiguousarray(i["x"][0].reshape(NT, P, D).transpose(1, 0, 2)).reshape(P, NT * D),
        "params": np.concatenate(params, 1),
        "consts": constant_table()[0],
        "positions": np.ascontiguousarray(i["positions_2"].reshape(NT, P).T),
        "w_hy_in": col_chunks(hy),
        "w_hy_out": row_chunks(i["hy_w_out"][0]),
        "w_ns_in": col_chunks(ns),
        "w_ns_out": row_chunks(i["nsa_w_out"][0]),
        "w_cmp1": np.concatenate(cw1, 0),
        "w_ssd_in": col_chunks(padded(i["ssd_w_in_2"][0], 49 * P)),
        "w_ssd_out": row_chunks(i["ssd_w_out_2"][0]),
        "w_mla_in": col_chunks(padded(i["mla_w_in_2"][0], 6 * P)),
        "w_uq": i["mla_w_uq_2"][0].reshape(3, P, 3, 512).transpose(2, 1, 0, 3).reshape(3, P, 1536),
        "w_ukv": i["mla_w_ukv_2"][0].reshape(2, P, 4, 512).transpose(2, 1, 0, 3).reshape(4, P, 1024),
        "w_mla_out": row_chunks(i["mla_w_out_2"][0]),
    }
    for l in range(2):
        up = i["ffn_w_up"][l]
        arrays[f"w_conv{l}"] = ffn_chunks(up[:, :DFF], up[:, DFF:], i["ffn_w_down"][l])
        arrays[f"w_mod{l}"] = col_chunks(i["w_mod_2"][l])
        for s in range(2):
            arrays[f"w_ffn{l}{s}"] = ffn_chunks(i["ffn_w_gate_2"][l, s], i["ffn_w_up_2"][l, s],
                                                i["ffn_w_down_2"][l, s])
    return {k: np.ascontiguousarray(v) for k, v in arrays.items()}, at


class Progress:

    def __init__(self, sem):
        self.sem, self.n = sem, 0

    def count(self, _ins):
        self.n += 1
        return (self.sem, self.n)


def build(nc, dram, out, pat, cat):
    V, A, E = nc.vector, nc.scalar, nc.tensor
    ctx = ExitStack()
    with ctx:
        def sb(name, n, dt=F32):
            return ctx.enter_context(nc.sbuf_tensor(name, [P, n], dt))

        params = sb("params", dram["params"].shape[1])
        consts = sb("consts", dram["consts"].shape[1])
        xs_ = sb("x_res", NT * D)
        hT_ = sb("hT", KC * T)
        htok_ = sb("htok", NT * D)
        ring = sb("ring", RING * SLOT)
        rowb = sb("rowb", D)
        modT = sb("modT", 2 * 72)
        small = sb("small", 512)
        modw = sb("modw", SLOT)
        posi = sb("posi", NT, I32)
        psum = ctx.enter_context(nc.psum_tensor("psum", [P, 8, 512], F32))

        pe = Progress(ctx.enter_context(nc.semaphore("pe_done")))
        act = Progress(ctx.enter_context(nc.semaphore("act_done")))
        dve = Progress(ctx.enter_context(nc.semaphore("dve_done")))
        start_loaded = ctx.enter_context(nc.semaphore("start_loaded"))
        stored = ctx.enter_context(nc.semaphore("stored"))
        slot_full = [ctx.enter_context(nc.semaphore(f"slot_full{n}")) for n in range(RING)]

        block = ctx.enter_context(nc.Block())

        def prm(name):
            a, n = pat[name]
            return params[:, a:a + n]

        def cst(name):
            a, n = cat[name]
            return consts[:, a:a + n]

        x = xs_[:, :].rearrange("p (t d) -> p t d", t=NT)
        hT = hT_[:, :].rearrange("p (k t) -> p k t", k=KC)
        htok = htok_[:, :].rearrange("p (t d) -> p t d", t=NT)
        ident = cst("ident")
        acc = psum[:, 0:4, :].rearrange("p (t b) n -> p t (b n)", t=NT)

        def bank(b):
            return psum[:, b, :]

        def banks(b, n):
            return psum[:, b:b + n, :].rearrange("p b n -> p (b n)")

        class Arena:
            made = 0

            def __init__(self):
                self.stack = ctx.enter_context(ExitStack())

            def take(self, n, dt=F32):
                Arena.made += 1
                return self.stack.enter_context(nc.sbuf_tensor(f"buf{Arena.made}", [P, n], dt))[:, :]

            def close(self):
                self.stack.close()

        def spread(ap, shape):
            return ap.to_broadcast(shape)

        def vl(ins):
            p = dve.count(ins)
            V.wait_ge(*p)
            return p

        def al(ins):
            p = act.count(ins)
            A.wait_ge(*p)
            return p

        @block.sync
        def _(sp):
            sp.dma_start(xs_[:, :], dram["x"]).then_inc(start_loaded, 16)
            sp.dma_start(consts[:, :], dram["consts"]).then_inc(start_loaded, 16)
            sp.dma_start(params[:, :], dram["params"]).then_inc(start_loaded, 16)
            sp.dma_start(posi[:, :], dram["positions"]).then_inc(start_loaded, 16)
        loaded = (start_loaded, 64)

        @block.vector
        def _(_e):
            V.wait_ge(*loaded)

        @block.scalar
        def _(_e):
            A.wait_ge(*loaded)

        @block.tensor
        def _(_e):
            E.wait_ge(*loaded)

        class Ring:
            n = 0
            used = [[] for _ in range(RING)]
            fills = [0] * RING

        def slot_ap(s, w):
            return ring[:, s * SLOT:s * SLOT + w]

        def load(src, chunks):
            s = Ring.n % RING
            Ring.n += 1
            Ring.fills[s] += 1
            w = src.shape[-1]
            waits = Ring.used[s]

            @block.sync
            def _(sp):
                for point in waits:
                    sp.wait_ge(*point)
                sp.dma_start(slot_ap(s, chunks * w).rearrange("p (c w) -> p c w", c=chunks),
                             src.rearrange("c p w -> p c w")).then_inc(slot_full[s], 16)
            return s, (slot_full[s], 16 * Ring.fills[s])

        def rstd_of(ss, n, scale, eps, ready):
            @block.vector
            def _(_e):
                V.wait_ge(*ready)
                Ring.p = vl(V.tensor_scalar(ss, ss, scale, eps, ALU.mult, ALU.add).then_inc(dve.sem, 1))

            @block.scalar
            def _(_e):
                A.wait_ge(*Ring.p)
                Ring.p = act.count(A.activation(ss, ss, ACT.Sqrt).then_inc(act.sem, 1))

            @block.vector
            def _(_e):
                V.wait_ge(*Ring.p)
                Ring.p = vl(V.reciprocal(ss, ss).then_inc(dve.sem, 1))
            return Ring.p

        def whole(ap):
            return ap.bitcast(F32)

        def halves(ar, n):
            return ar.take(2 * n * T, F32R).rearrange("p (a k t) -> p a k t", a=2, k=n)

        def norm_transpose(gain, shift, ready, parts, meanwhile=None):
            ss = small[:, 0:NT]

            @block.scalar
            def _(_e):
                for point in ready[:-1]:
                    A.wait_ge(*point)
                for t in range(NT):
                    if t:
                        A.wait_ge(*ready[-1])
                    p = al(A.activation(htok[:, t, :], x[:, t, :], ACT.Square, accum_out=ss[:, t:t + 1]).then_inc(act.sem, 1))
                Ring.q = p
            rstd_of(ss, NT, 1.0 / D, EPS, Ring.q)

            @block.vector
            def _(_e):
                for t in range(NT):
                    Ring.q = dve.count(V.tensor_scalar(htok[:, t, :], x[:, t, :], ss[:, t:t + 1], None, ALU.mult).then_inc(dve.sem, 1))
            normed = Ring.q
            freed = [loaded if meanwhile is None else meanwhile()] * 4
            for k in range(KC):
                b = bank(4 + k % 4)

                @block.tensor
                def _(_e):
                    E.wait_ge(*normed)
                    E.wait_ge(*freed[k % 4])
                    for t in range(NT):
                        ins = E.transpose(b[:, t * P:(t + 1) * P], htok[:, t, k * P:(k + 1) * P], ident)
                    Ring.p = pe.count(ins.then_inc(pe.sem, 1))

                @block.scalar
                def _(_e):
                    A.wait_ge(*Ring.p)
                    bias = 0.0 if shift is None else shift[:, k:k + 1]
                    freed[k % 4] = act.count(A.activation(hT[:, k, :], b[:, 0:T], ACT.Identity, bias=bias,
                                                          scale=gain[:, k:k + 1]).then_inc(act.sem, 1))

                if parts is None:
                    Ring.q = freed[k % 4]
                    continue
                if k % 2 == 0:
                    continue

                @block.vector
                def _(_e):
                    V.wait_ge(*freed[k % 4])
                    kk = slice(k - 1, k + 1)
                    vl(V.tensor_copy(parts[:, 0, kk, :], hT[:, kk, :]).then_inc(dve.sem, 1))
                    Ring.q = dve.count(V.tensor_tensor(parts[:, 1, kk, :], hT[:, kk, :], whole(parts[:, 0, kk, :]),
                                                       ALU.subtract).then_inc(dve.sem, 1))
            return [Ring.q]

        def row_of(col, scale, ready):
            @block.tensor
            def _(_e):
                for point in ready:
                    E.wait_ge(*point)
                for k in range(KC):
                    ins = E.matmul(bank(4 + k // 4)[:, (k % 4) * P:(k % 4 + 1) * P],
                                   spread(col[:, k:k + 1], [P, P]), ident, start=True, stop=True)
                Ring.p = pe.count(ins.then_inc(pe.sem, 1))

            @block.scalar
            def _(_e):
                A.wait_ge(*Ring.p)
                Ring.p = al(A.activation(rowb[:, :], banks(4, 2), ACT.Copy, scale=scale).then_inc(act.sem, 1))
            return Ring.p

        def add_normed(ready):
            ss = small[:, 0:NT]

            @block.scalar
            def _(_e):
                for point in ready:
                    A.wait_ge(*point)
                for t in range(NT):
                    Ring.q = al(A.activation(htok[:, t, :], acc[:, t, :], ACT.Square, accum_out=ss[:, t:t + 1]).then_inc(act.sem, 1))
            rstd_of(ss, NT, 1.0 / D, EPS, Ring.q)

            done = []

            @block.vector
            def _(_e):
                for t in range(NT):
                    vl(V.scalar_tensor_tensor(htok[:, t, :], acc[:, t, :], ss[:, t:t + 1], rowb[:, :],
                                              ALU.mult, ALU.mult).then_inc(dve.sem, 1))
                    done.append(dve.count(V.tensor_tensor(x[:, t, :], x[:, t, :], htok[:, t, :], ALU.add).then_inc(dve.sem, 1)))
                V.wait_ge(*done[-1])
            return done

        def add_gated(ready):
            done = []

            @block.vector
            def _(_e):
                for point in ready:
                    V.wait_ge(*point)
                for t in range(NT):
                    vl(V.tensor_tensor(htok[:, t, :], acc[:, t, :], rowb[:, :], ALU.mult).then_inc(dve.sem, 1))
                    done.append(dve.count(V.tensor_tensor(x[:, t, :], x[:, t, :], htok[:, t, :], ALU.add).then_inc(dve.sem, 1)))
                V.wait_ge(*done[-1])
            return done

        PASSES = ((0, 0), (0, 1), (1, 0))

        def split_chunk(raw, parts, full, free):
            @block.scalar
            def _(_e):
                A.wait_ge(*full)
                A.wait_ge(*free)
                Ring.p = act.count(A.activation(parts[:, 0, :], raw, ACT.Copy).then_inc(act.sem, 1))

            @block.vector
            def _(_e):
                V.wait_ge(*Ring.p)
                V.wait_ge(*full)
                Ring.p = dve.count(V.tensor_tensor(parts[:, 1, :], raw, whole(parts[:, 0, :]),
                                                   ALU.subtract).then_inc(dve.sem, 1))
            return Ring.p

        def weight_parts(ar, n=3):
            return [ar.take(2 * CHUNK, F32R).rearrange("p (a w) -> p a w", a=2) for _ in range(n)]

        def project(name, n, evac, ready, h, wp, tokens=(), widths={}):
            freed = [()] * 4
            done = []
            wp_free = [loaded] * len(wp)
            made = {}

            def prepare(c):
                if c % 3 == 0:
                    m = min(3, n - c)
                    made["slot"], made["full"] = load(dram[name][c:c + m], m)
                s, full = made["slot"], made["full"]
                raw = slot_ap(s, SLOT)[:, (c % 3) * CHUNK:(c % 3 + 1) * CHUNK]
                if c in tokens:
                    made[c] = (s, raw, full)
                else:
                    p = split_chunk(raw, wp[c % len(wp)], full, wp_free[c % len(wp)])
                    made[c] = (s, raw, p)
                    Ring.used[s] = [p]

            prepare(0)
            for c in range(n):
                if c + 1 < n:
                    prepare(c + 1)
                s, raw, point_w = made[c]
                b = bank(4 + c % 4)

                @block.tensor
                def _(_e):
                    E.wait_ge(*point_w)
                    for point in ready:
                        E.wait_ge(*point)
                    for point in freed[c % 4]:
                        E.wait_ge(*point)
                    if c in tokens:
                        w = raw.rearrange("p (k n) -> p k n", k=KC)
                        width = widths.get(c, P)
                        for t in range(NT):
                            for k in range(KC):
                                ins = E.matmul(b[:, t * width:(t + 1) * width], hT[:, k, t * P:(t + 1) * P],
                                               w[:, k, 0:width], start=k == 0, stop=k == KC - 1)
                    else:
                        w = wp[c % len(wp)].rearrange("p a (k n) -> p a k n", k=KC)
                        for k in range(KC):
                            for n_, (wa, ha) in enumerate(PASSES):
                                ins = E.matmul(b[:, 0:T], w[:, wa, k, :], h[:, ha, k, :], start=k + n_ == 0,
                                               stop=k == KC - 1 and n_ == 2)
                    done.append(pe.count(ins.then_inc(pe.sem, 1)))
                if c in tokens:
                    Ring.used[s] = Ring.used[s][-1:] + [done[c]] if c % 3 else [done[c]]
                else:
                    wp_free[c % len(wp)] = done[c]
                if c:
                    freed[(c - 1) % 4] = evac(c - 1, bank(4 + (c - 1) % 4), done[c - 1])
            evac(n - 1, bank(4 + (n - 1) % 4), done[n - 1])

        def out_project(name, n, lhs, ready):
            ar = Arena()
            parts = halves(ar, n)
            wp = weight_parts(ar)
            wp_free = [loaded] * 3
            for k in range(n):
                if k % 3 == 0:
                    m = min(3, n - k)
                    s, full = load(dram[name][k:k + m], m)

                @block.scalar
                def _(_e):
                    for point in ready:
                        A.wait_ge(*point)
                    Ring.p = act.count(A.activation(parts[:, 0, k, :], lhs[:, k, :], ACT.Copy).then_inc(act.sem, 1))

                @block.vector
                def _(_e):
                    V.wait_ge(*Ring.p)
                    dve.count(V.tensor_tensor(parts[:, 1, k, :], lhs[:, k, :], whole(parts[:, 0, k, :]),
                                              ALU.subtract).then_inc(dve.sem, 1))
                Ring.used[s] = [split_chunk(slot_ap(s, SLOT)[:, (k % 3) * D:(k % 3 + 1) * D], wp[k % 3], full,
                                            wp_free[k % 3])]

                @block.tensor
                def _(_e):
                    E.wait_ge(*Ring.used[s][0])
                    for t in range(NT):
                        for h in range(2):
                            for n_, (wa, la) in enumerate(PASSES):
                                ins = E.matmul(acc[:, t, h * 512:(h + 1) * 512], parts[:, la, k, t * P:(t + 1) * P],
                                               wp[k % 3][:, wa, h * 512:(h + 1) * 512], start=k + n_ == 0,
                                               stop=k == n - 1 and n_ == 2)
                    wp_free[k % 3] = pe.count(ins.then_inc(pe.sem, 1))
            load_table(ACT.Sqrt)
            ar.close()
            return [(pe.sem, pe.n)]

        cond = small[:, 40:48]
        one_col = small[:, 4:5]

        mod_full = [ctx.enter_context(nc.semaphore(f"mod_full{h}")) for h in range(2)]
        mod_loads = [0]
        mod_used = []
        mod_finish = []

        def finish_mod():
            return [mod_finish.pop()()] if mod_finish else []
        table_col = small[:, 5:6]

        def load_table(func):
            @block.scalar
            def _(_e):
                al(A.activation(table_col, one_col, func).then_inc(act.sem, 1))
        MOD_PIECES = 12

        def ffn(name, h, ar, conv=None, mod=None):
            src = dram[name]
            wu = [ar.take(4 * CHUNK, F32R).rearrange("p (a w) -> p a w", a=2) for _ in range(2)]
            wd = [ar.take(2 * CHUNK, F32R).rearrange("p (a w) -> p a w", a=2) for _ in range(2)]
            hr = [ar.take(2 * T, F32R).rearrange("p (a w) -> p a w", a=2) for _ in range(2)]
            sg = [htok_[:, q * T:(q + 1) * T] for q in range(2)]
            cv = [htok_[:, (2 + q) * T:(3 + q) * T] for q in range(2)]
            hf = [htok_[:, 4 * T:5 * T]] * 2 if conv is not None else cv
            gp = [htok_[:, 5 * T + 4 + q * (T + 4):6 * T + 6 + q * (T + 4)] for q in range(2)]
            if mod is not None:
                macc = ar.take(MOD_PIECES * 3 * P)
                msrc = dram[f"w_mod{mod[0]}"]
                mod0 = 36 * mod[1]
            c3 = conv is not None
            AM = 5 if c3 else 3
            DM = 9 if c3 else 5
            MODS = KC // 2 if mod is not None else 0
            mod_at = (3, 5, DM + 1, DM + 2) if c3 else tuple(DM + 1 + k for k in range(4))
            DS = DM + (0 if mod is None else 2 if c3 else MODS)

            P0 = A0 = D0 = PB = AB = DB = None

            def zero(j):
                return isinstance(j, int) and j == 0

            def up_done(j):
                return (pe.sem, P0 + 1) if zero(j) else (pe.sem, PB + 2 * j + 1)

            def down_done(j):
                return (pe.sem, PB + 2 * (j + 1) + 2)

            def act_at(j, k):
                return (act.sem, A0 + (1 if k == 1 else 2)) if zero(j) else (act.sem, AB + AM * j + k)

            def dve_at(q, u, k):
                if zero(q) and u == 0:
                    return (dve.sem, D0 + (1 if k == 1 else 2))
                return (dve.sem, DB + DS * 2 * q + DS * u + k)

            def prev(q, u, back):
                return q + (u - back) // 2, (u - back) % 2

            slots0 = Ring.n
            fills0 = list(Ring.fills)

            def slot(ju):
                return (slots0 + ju) % RING

            def full(q, ju):
                return (slot_full[slot(ju)], 16 * (fills0[slot(ju)] + 1 + ju // RING) + 16 * q)

            def sp_step(sp, q4, ju, waits):
                j = q4 * 4 + ju
                for point in waits:
                    sp.wait_ge(*point)
                sp.dma_start(slot_ap(slot(ju), SLOT).rearrange("p (c w) -> p c w", c=3),
                             (src[j] if isinstance(j, int) else
                              src[bass.ds(j, 1)].rearrange("a c p w -> (a c) p w")).rearrange("c p w -> p c w")
                             ).then_inc(slot_full[slot(ju)], 16)

            def sp_mod(sp, m, half, waits):
                for point in waits:
                    sp.wait_ge(*point)
                rows = msrc[mod0 + 3 * m:mod0 + 3 * m + 3] if isinstance(m, int) else msrc[bass.ds(m * 3 + mod0, 3)]
                sp.dma_start(modw[:, half * 1536:(half + 1) * 1536].rearrange("p (c w) -> p c w", c=3),
                             rows.rearrange("c p w -> p c w")[:, :, half * 512:(half + 1) * 512]
                             ).then_inc(mod_full[half], 16)

            def pe_up(q, u, ju):
                E.wait_ge(*dve_at(q, u, 1))
                if not (isinstance(q, int) and q == 0):
                    E.wait_ge(*dve_at(*prev(q, u, 1), DM - 3))
                w = wu[u].rearrange("p a (c k n) -> p a c k n", c=2, k=KC)
                b = bank(4 + u)
                for g in range(2):
                    for k in range(KC):
                        for n_, (wa, ha) in enumerate(PASSES):
                            ins = E.matmul(b[:, g * T:(g + 1) * T], w[:, wa, g, k, :], h[:, ha, k, :],
                                           start=k + n_ == 0, stop=k == KC - 1 and n_ == 2)
                ins.then_inc(pe.sem, 1)

            def pe_down(q, u, start=False, stop=False, last=None):
                E.wait_ge(*(last or dve_at(q, u, DM - 1)))
                z = 1 - u
                for t in range(NT):
                    for g in range(2):
                        for n_, (wa, ha) in enumerate(PASSES):
                            ins = E.matmul(acc[:, t, g * 512:(g + 1) * 512], hr[z][:, ha, t * P:(t + 1) * P],
                                           wd[z][:, wa, g * 512:(g + 1) * 512], start=start and n_ == 0,
                                           stop=stop and n_ == 2)
                ins.then_inc(pe.sem, 1)

            def act_hidden(q, u, j):
                z = 1 - u
                b = bank(4 + z)
                A.wait_ge(*up_done(j - 1))
                if not c3:
                    if not isinstance(j, int):
                        A.wait_ge(*dve_at(*prev(q, u, 2), DM - 3))
                    A.activation(sg[z], b[:, 0:T], ACT.Silu).then_inc(act.sem, 1)
                else:
                    A.activation(gp[z][:, 2:T + 2], b[:, 0:T], ACT.Copy).then_inc(act.sem, 1)
                    A.wait_ge(*act_at(j, 2))
                    A.activation(cv[z], gp[z][:, 0:T], ACT.Identity, scale=one(f"conv_w{conv}0", j - 1),
                                 bias=one(f"conv_b{conv}", j - 1)).then_inc(act.sem, 1)
                    A.wait_ge(*dve_at(q, u, 4))
                    A.activation(sg[z], cv[z], ACT.Gelu_apprx_tanh).then_inc(act.sem, 1)

            def act_step(q, u, ju, q4):
                j = q * 2 + u
                raw = slot_ap(slot(ju), SLOT)
                A.wait_ge(*full(q4, ju))
                if not isinstance(j, int):
                    A.wait_ge(*up_done(j - 2))
                A.activation(wu[u][:, 0, :], raw[:, 0:2 * CHUNK], ACT.Copy).then_inc(act.sem, 1)
                if not zero(j):
                    act_hidden(q, u, j)
                if not isinstance(j, int):
                    A.wait_ge(*down_done(j - 2))
                A.activation(wd[u][:, 0, :], raw[:, 2 * CHUNK:], ACT.Copy).then_inc(act.sem, 1)

            def one(name_, j):
                v = prm(name_)
                return v[:, j:j + 1] if isinstance(j, int) else v[:, bass.ds(j, 1)]

            def dve_hidden(q, u, j):
                z = 1 - u
                b = bank(4 + z)
                if c3:
                    for w in (1, 2):
                        V.wait_ge(*(act_at(j, 3) if w == 1 else dve_at(q, u, 2)))
                        V.scalar_tensor_tensor(cv[z], gp[z][:, w:w + T], one(f"conv_w{conv}{w}", j - 1), cv[z],
                                               ALU.mult, ALU.add).then_inc(dve.sem, 1)
                        mod_op(q, u, w - 1, mod_before(q, u, w - 1))
                V.wait_ge(*act_at(j, AM - 1))
                V.wait_ge(*up_done(j - 1))
                V.tensor_tensor(hf[z], sg[z], b[:, T:2 * T], ALU.mult).then_inc(dve.sem, 1)
                V.wait_ge(*dve_at(q, u, DM - 3))
                if not isinstance(j, int):
                    V.wait_ge(*down_done(j - 3))
                V.tensor_copy(hr[z][:, 0, :], hf[z]).then_inc(dve.sem, 1)
                V.wait_ge(*dve_at(q, u, DM - 2))
                V.tensor_tensor(hr[z][:, 1, :], hf[z], whole(hr[z][:, 0, :]), ALU.subtract).then_inc(dve.sem, 1)

            def dve_step(q, u, ju, q4):
                j = q * 2 + u
                raw = slot_ap(slot(ju), SLOT)
                V.wait_ge(*full(q4, ju))
                V.wait_ge(*act_at(j, 1))
                V.tensor_tensor(wu[u][:, 1, :], raw[:, 0:2 * CHUNK], whole(wu[u][:, 0, :]),
                                ALU.subtract).then_inc(dve.sem, 1)
                if not zero(j):
                    dve_hidden(q, u, j)
                V.wait_ge(*act_at(j, AM))
                V.tensor_tensor(wd[u][:, 1, :], raw[:, 2 * CHUNK:], whole(wd[u][:, 0, :]),
                                ALU.subtract).then_inc(dve.sem, 1)
                if mod is not None and not zero(j):
                    for k in range(2 if c3 else 0, MODS):
                        mod_op(q, u, k, mod_before(q, u, k))

            def mod_op(m, half, k, before):
                w = modw[:, half * 1536:(half + 1) * 1536].rearrange("p (c k n) -> p c k n", c=3, k=KC // 2)
                o = (macc[:, m * 3 * P:(m + 1) * 3 * P] if isinstance(m, int) else
                     macc[:, bass.ds(m * (3 * P), 3 * P)]).rearrange("p (c n) -> p c n", c=3)
                kc = half * (KC // 2) + k
                if k == 0:
                    V.wait_ge(mod_full[half], 16 * (mod_loads[0] + 1) + m * 16)
                V.wait_ge(dve.sem, before)
                if kc == 0:
                    V.tensor_scalar(o, w[:, :, 0, :], cond[:, 0:1], None, ALU.mult).then_inc(dve.sem, 1)
                else:
                    V.scalar_tensor_tensor(o, w[:, :, k, :], cond[:, kc:kc + 1], o, ALU.mult, ALU.add
                                           ).then_inc(dve.sem, 1)

            def mod_before(q, u, k):
                return dve_at(q, u, mod_at[k - 1] if k else 0)[1]

            def first(ready):
                nonlocal A0, D0
                before = [Ring.used[slot(j)] for j in range(2)]

                @block.sync
                def _(sp):
                    sp_step(sp, 0, 0, before[0])
                    sp_step(sp, 0, 1, before[1])
                    if mod is not None:
                        sp_mod(sp, 0, 0, mod_used)
                        sp_mod(sp, 0, 1, mod_used)
                load_table(ACT.Gelu_apprx_tanh if c3 else ACT.Silu)
                A0, D0 = act.n, dve.n

                @block.scalar
                def _(_e):
                    for point in ready:
                        A.wait_ge(*point)
                    act_step(0, 0, 0, 0)
                act.n += 2

                @block.vector
                def _(_e):
                    for point in ready:
                        V.wait_ge(*point)
                    dve_step(0, 0, 0, 0)
                dve.n += 2

            def rest(ready):
                nonlocal P0, PB, AB, DB
                if c3:
                    @block.vector
                    def _(_e):
                        for point in ready:
                            V.wait_ge(*point)
                        for q in range(2):
                            vl(V.memset(gp[q][:, 0:2], 0.0).then_inc(dve.sem, 1))
                    gp_ready = (dve.sem, dve.n)

                    @block.scalar
                    def _(_e):
                        A.wait_ge(*gp_ready)
                P0, PB, AB, DB = pe.n, pe.n - 1, act.n - AM, dve.n + MODS - DS
                @block.tensor
                def _(_e):
                    for point in ready:
                        E.wait_ge(*point)
                    pe_up(0, 0, 0)
                    pe_up(0, 1, 1)
                    pe_down(0, 1, start=True)

                @block.scalar
                def _(_e):
                    for point in ready:
                        A.wait_ge(*point)
                    act_step(0, 1, 1, 0)

                @block.vector
                def _(_e):
                    for point in ready:
                        V.wait_ge(*point)
                    if mod is not None:
                        for k in range(MODS):
                            mod_op(0, 0, k, DB + DS - MODS + k)
                    dve_step(0, 1, 1, 0)

                @block.sync
                def _(sp):
                    with sp.Fori(0, (NF - 2) // 4) as i:
                        for u in range(4):
                            q = i * 2 + (1 + u // 2)
                            sp_step(sp, i, 2 + u, [(dve.sem, DB + DS * 4 * i + DS * u + DM)])
                            if mod is not None:
                                sp_mod(sp, q, u % 2, [(dve.sem, DB + DS * 4 * i + DS * u + DS)])
                if mod is not None:
                    @block.sync
                    def _(sp):
                        for half in range(2):
                            sp_mod(sp, MOD_PIECES - 1, half, [(dve.sem, DB + DS * (NF - 2 + half) + DS)])

                @block.tensor
                def _(_e):
                    with E.Fori(0, (NF - 2) // 4) as i:
                        for u in range(4):
                            q = i * 2 + (1 + u // 2)
                            pe_up(q, u % 2, 2 + u)
                            pe_down(q, u % 2)

                @block.scalar
                def _(_e):
                    with A.Fori(0, (NF - 2) // 4) as i:
                        for u in range(4):
                            act_step(i * 2 + (1 + u // 2), u % 2, 2 + u, i)

                @block.vector
                def _(_e):
                    with V.Fori(0, (NF - 2) // 4) as i:
                        for u in range(4):
                            q = i * 2 + (1 + u // 2)
                            dve_step(q, u % 2, 2 + u, i)

                D1 = DB + DS * NF
                A1 = AB + AM * NF

                @block.scalar
                def _(_e):
                    z = 1
                    b = bank(4 + z)
                    A.wait_ge(*up_done(NF - 1))
                    if not c3:
                        A.activation(sg[z], b[:, 0:T], ACT.Silu).then_inc(act.sem, 1)
                    else:
                        A.activation(gp[z][:, 2:T + 2], b[:, 0:T], ACT.Copy).then_inc(act.sem, 1)
                        A.wait_ge(act.sem, A1 + 1)
                        A.activation(cv[z], gp[z][:, 0:T], ACT.Identity, scale=one(f"conv_w{conv}0", NF - 1),
                                     bias=one(f"conv_b{conv}", NF - 1)).then_inc(act.sem, 1)
                        A.wait_ge(dve.sem, D1 + 2)
                        A.activation(sg[z], cv[z], ACT.Gelu_apprx_tanh).then_inc(act.sem, 1)

                @block.vector
                def _(_e):
                    z = 1
                    b = bank(4 + z)
                    k = 0
                    if c3:
                        for w in (1, 2):
                            V.wait_ge(*((act.sem, A1 + 2) if w == 1 else (dve.sem, D1 + 1)))
                            V.scalar_tensor_tensor(cv[z], gp[z][:, w:w + T], one(f"conv_w{conv}{w}", NF - 1), cv[z],
                                                   ALU.mult, ALU.add).then_inc(dve.sem, 1)
                        k = 2
                    V.wait_ge(act.sem, A1 + AM - 2)
                    V.tensor_tensor(hf[z], sg[z], b[:, T:2 * T], ALU.mult).then_inc(dve.sem, 1)
                    V.wait_ge(dve.sem, D1 + k + 1)
                    V.wait_ge(*down_done(NF - 3))
                    V.tensor_copy(hr[z][:, 0, :], hf[z]).then_inc(dve.sem, 1)
                    V.wait_ge(dve.sem, D1 + k + 2)
                    V.tensor_tensor(hr[z][:, 1, :], hf[z], whole(hr[z][:, 0, :]), ALU.subtract).then_inc(dve.sem, 1)
                dve.n = D1 + (5 if c3 else 3)
                act.n = A1 + AM - 2
                load_table(ACT.Sqrt)
                hidden = (dve.sem, dve.n)

                @block.tensor
                def _(_e):
                    pe_down(0, 0, stop=True, last=hidden)
                pe.n = PB + 1 + 2 * NF
                final = (pe.sem, pe.n)
                for k in range(NF):
                    Ring.fills[(slots0 + k) % RING] += 1
                Ring.n = slots0 + NF
                Ring.used = [[(dve.sem, D1)] for _ in range(RING)]
                if mod is None:
                    return [final]

                @block.vector
                def _(_e):
                    for k in range(2 * MODS):
                        mod_op(MOD_PIECES - 1, k // MODS, k % MODS, dve.n + k)
                dve.n += 2 * MODS
                mod_loads[0] += MOD_PIECES
                mod_used[:] = [(dve.sem, dve.n)]

                @block.tensor
                def _(_e):
                    E.wait_ge(*mod_used[0])
                    for c in range(3 * MOD_PIECES):
                        ins = E.matmul(bank(6)[:, c:c + 1], macc[:, c * P:(c + 1) * P], one_col, start=True, stop=True)
                    Ring.p = pe.count(ins.then_inc(pe.sem, 1))

                summed = Ring.p

                def finish():
                    @block.vector
                    def _(_e):
                        V.wait_ge(*summed)
                        Ring.q = vl(V.tensor_tensor(modT[:, 72 * mod[0] + mod0:72 * mod[0] + mod0 + 36], bank(6)[:, 0:36],
                                           prm(f"b_mod{mod[0]}")[:, mod0:mod0 + 36], ALU.add).then_inc(dve.sem, 1))
                    return Ring.q
                mod_finish.append(finish)
                return [final]

            return first, rest

        def attend(units, keys, ready):
            ar = Arena()
            s_buf = [ar.take(4 * keys).rearrange("p (h k) -> p h k", h=4) for _ in range(3)]
            pT = [[[ar.take(4 * P) for _ in range(u_blocks)] for u_blocks in
                   [max(u["blocks"] for u in units if u["branch"] == b) for b in sorted({u["branch"] for u in units})]]
                  for _ in range(2)]
            st = ar.take(3 * 16)
            state = {"s_free": [loaded] * 2, "p_free": [loaded] * 3, "t_free": loaded, "o_free": [loaded] * 2,
                     "pT_free": [loaded] * 2}
            group = 0
            for u in units:
                u["group"] = group % 2
                group += u["last"]

            def scores(n, u):
                q = n % 2
                nk = u["keys"]
                sc = banks(2 * q, 2).rearrange("p (o e k) -> p e o k", o=2, e=2)

                @block.tensor
                def _(_e):
                    for point in ready:
                        E.wait_ge(*point)
                    E.wait_ge(*state["s_free"][q])
                    for i in range(4):
                        ins = E.matmul(sc[:, i // 2, i % 2, 0:nk], u["q"](i), u["k"](i), start=True, stop=True)
                    u["scores"] = pe.count(ins.then_inc(pe.sem, 1))

            def exponentials(n, u):
                q = n % 2
                nk = u["keys"]
                sc = banks(2 * q, 2).rearrange("p (o e k) -> p e o k", o=2, e=2)
                s = s_buf[n % 3]
                stats = st[:, 16 * (n % 3):16 * (n % 3) + 16]
                mx, rs, nm, xtra = (stats[:, 4 * a:4 * a + 4] for a in range(4))

                @block.vector
                def _(_e):
                    V.wait_ge(*u["scores"])
                    V.wait_ge(*state["p_free"][n % 3])
                    if u["dist"] is not None:
                        for i in range(4):
                            p = dve.count(V.scalar_tensor_tensor(s[:, i, 0:nk], u["dist"], -u["slopes"][i],
                                                                sc[:, i // 2, i % 2, 0:nk], ALU.mult, ALU.add).then_inc(dve.sem, 1))
                        V.wait_ge(*p)
                        state["s_free"][q] = p
                        vl(V.tensor_reduce(mx, s[:, :, 0:nk], AXX, ALU.max).then_inc(dve.sem, 1))
                    else:
                        vl(V.tensor_reduce(mx.rearrange("p (e o) -> p e o", e=2), sc[:, :, :, 0:nk], AXX, ALU.max).then_inc(dve.sem, 1))
                    if u.get("sinks") is not None:
                        vl(V.tensor_tensor(mx, mx, u["sinks"], ALU.max).then_inc(dve.sem, 1))
                        vl(V.tensor_tensor(xtra, u["sinks"], mx, ALU.subtract).then_inc(dve.sem, 1))
                    Ring.p = vl(V.tensor_scalar(nm, mx, -u["scale"], None, ALU.mult).then_inc(dve.sem, 1))

                @block.scalar
                def _(_e):
                    A.wait_ge(*Ring.p)
                    for i in range(4):
                        src = s[:, i, 0:nk] if u["dist"] is not None else sc[:, i // 2, i % 2, 0:nk]
                        p = act.count(A.activation(s[:, i, 0:nk], src, ACT.Exp, bias=nm[:, i:i + 1],
                                                  scale=u["scale"], accum_out=rs[:, i:i + 1]).then_inc(act.sem, 1))
                    if u["dist"] is None:
                        state["s_free"][q] = p
                    if u.get("sinks") is not None:
                        p = act.count(A.activation(xtra, xtra, ACT.Exp).then_inc(act.sem, 1))
                    u["exp"] = p

            def back(n, u):
                q = n % 2
                nk = u["keys"]
                s = s_buf[n % 3]
                stats = st[:, 16 * (n % 3):16 * (n % 3) + 16]
                mx, rs, nm, xtra = (stats[:, 4 * a:4 * a + 4] for a in range(4))

                @block.vector
                def _(_e):
                    V.wait_ge(*u["exp"])
                    if u.get("sinks") is not None:
                        vl(V.tensor_tensor(rs, rs, xtra, ALU.add).then_inc(dve.sem, 1))
                    vl(V.reciprocal(rs, rs).then_inc(dve.sem, 1))
                    if u.get("gates") is not None:
                        vl(V.tensor_tensor(rs, rs, u["gates"], ALU.mult).then_inc(dve.sem, 1))
                    Ring.p = vl(V.tensor_tensor(s[:, :, 0:nk], s[:, :, 0:nk],
                                                spread(rs.rearrange("p (h o) -> p h o", o=1), [P, 4, nk]), ALU.mult).then_inc(dve.sem, 1))
                normed = Ring.p

                @block.tensor
                def _(_e):
                    E.wait_ge(*normed)
                    E.wait_ge(*state["t_free"])
                    for b in range(u["blocks"]):
                        w = min(P, nk - b * P)
                        for i in range(4):
                            ins = E.transpose(bank(4 + b)[0:w, i * P:(i + 1) * P], s[:, i, b * P:b * P + w], ident)
                    Ring.p = pe.count(ins.then_inc(pe.sem, 1))
                state["p_free"][n % 3] = Ring.p

                @block.scalar
                def _(_e):
                    A.wait_ge(*Ring.p)
                    A.wait_ge(*state["pT_free"][u["group"]])
                    for b in range(u["blocks"]):
                        w = min(P, nk - b * P)
                        state["t_free"] = act.count(A.activation(pT[u["group"]][u["branch"]][b][0:w, :],
                                                                bank(4 + b)[0:w, :], ACT.Copy).then_inc(act.sem, 1))
                u["transposed"] = state["t_free"]

            def outputs(u):
                z = u["group"]
                ob = bank(6 + z)

                @block.tensor
                def _(_e):
                    E.wait_ge(*u["transposed"])
                    E.wait_ge(*state["o_free"][z])
                    for i in range(4):
                        o = ob[(i % 2) * HD:(i % 2 + 1) * HD, (i // 2) * P:(i // 2 + 1) * P]
                        todo = [(v, b) for v in u["parts"] for b in range(v["blocks"])]
                        for m, (v, b) in enumerate(todo):
                            w = min(P, v["keys"] - b * P)
                            ins = E.matmul(o, v["v"](i, b), pT[z][v["branch"]][b][0:w, i * P:(i + 1) * P],
                                           start=m == 0, stop=m == len(todo) - 1)
                    u["summed"] = state["pT_free"][z] = pe.count(ins.then_inc(pe.sem, 1))

            def outputs_copy(u):
                z = u["group"]
                ob = bank(6 + z)

                @block.vector
                def _(_e):
                    V.wait_ge(*u["summed"])
                    state["o_free"][z] = dve.count(V.tensor_copy(
                        u["out"], ob[:, 0:2 * P].rearrange("p (c n) -> p c n", c=2)).then_inc(dve.sem, 1))

            scores(0, units[0])
            for n in range(len(units) + 3):
                if n + 1 < len(units):
                    scores(n + 1, units[n + 1])
                if n < len(units):
                    exponentials(n, units[n])
                if 2 <= n < len(units) + 2 and units[n - 2]["last"]:
                    outputs(units[n - 2])
                if 1 <= n <= len(units):
                    back(n - 1, units[n - 1])
                if n >= 3 and units[n - 3]["last"]:
                    outputs_copy(units[n - 3])
            ar.close()
            return [(dve.sem, dve.n), (act.sem, act.n), (pe.sem, pe.n)]

        def hybrid(ready):
            ar = Arena()
            r_, k_, v_, ld_, cum_, a_, g_, kk_, bon_ = (ar.take(4 * T) for _ in range(9))
            t12 = ar.take(8 * T)
            t1_, t2_ = t12[:, 0:4 * T], t12[:, 4 * T:8 * T]
            wa, glo = g_[:, 0:T], g_[:, T:2 * T]
            omm = small[:, 16:30]
            omka = small[:, 32:36]
            swa = Arena()
            qT = swa.take(4 * T).rearrange("p (c t) -> p c t", c=4)
            kT = swa.take(2 * T).rearrange("p (c t) -> p c t", c=2)
            vtok = swa.take(NT * P).rearrange("p (t d) -> p t d", t=NT)
            mu = prm("mu")
            proj = Arena()
            h = halves(proj, KC)
            wp = weight_parts(proj, 2)
            h_ready = norm_transpose(prm("mix_pre_g0"), None, ready, h)

            @block.vector
            def _(_e):
                vl(V.tensor_scalar(omm, mu, -1.0, 1.0, ALU.mult, ALU.add).then_inc(dve.sem, 1))
                Ring.q = vl(V.tensor_scalar(omka, prm("k_a"), -1.0, 1.0, ALU.mult, ALU.add).then_inc(dve.sem, 1))
            coef = Ring.q

            def evac(c, b, p):
                if c < 4:
                    @block.scalar
                    def _(_e):
                        A.wait_ge(*p)
                        Ring.q = act.count(A.activation(qT[:, c, :], b[:, 0:T], ACT.Copy, scale=HD ** -0.5).then_inc(act.sem, 1))
                elif c < 6:
                    @block.scalar
                    def _(_e):
                        A.wait_ge(*p)
                        Ring.q = act.count(A.activation(kT[:, c - 4, :], b[:, 0:T], ACT.Copy).then_inc(act.sem, 1))
                elif c == 20:
                    @block.scalar
                    def _(_e):
                        A.wait_ge(*p)
                        Ring.q = act.count(A.activation(vtok, b[:, 0:T].rearrange("p (t d) -> p t d", t=NT), ACT.Copy).then_inc(act.sem, 1))
                else:
                    m = c - 6
                    dst = ([r_] * 4 + [k_] * 4 + [v_] * 4)[m][:, (m % 4) * T:(m % 4 + 1) * T] if m < 12 else \
                        (wa if m == 12 else glo)

                    @block.scalar
                    def _(_e):
                        A.wait_ge(*p)
                        A.wait_ge(*coef)
                        Ring.q = act.count(A.activation(dst, b[:, 0:T], ACT.Copy, scale=omm[:, m:m + 1]).then_inc(act.sem, 1))

                    @block.vector
                    def _(_e):
                        V.wait_ge(*Ring.q)
                        Ring.q = dve.count(V.scalar_tensor_tensor(dst[:, 1:T], b[:, 0:T - 1], mu[:, m:m + 1],
                                                                 dst[:, 1:T], ALU.mult, ALU.add).then_inc(dve.sem, 1))
                return (Ring.q,)

            project("w_hy_in", 21, evac, h_ready, h, wp, tokens=(20,))
            proj.close()
            projected = [(dve.sem, dve.n), (act.sem, act.n), (pe.sem, pe.n)]
            oT = hT

            slopes = alibi(8)
            sinks = prm("sinks")
            units = []
            for g in range(2):
                for t in range(NT):
                    u = dict(branch=0, scale=1.0, slopes=slopes[4 * g:4 * g + 4], sinks=sinks[:, 4 * g:4 * g + 4],
                             keys=(t + 1) * P, blocks=t + 1, last=True,
                             dist=cst("causal0") if t == 0 else cst("window1"),
                             q=lambda i, g=g, t=t: qT[(i % 2) * HD:(i % 2 + 1) * HD, 2 * g + i // 2, t * P:(t + 1) * P],
                             k=lambda i, g=g, t=t: kT[(i % 2) * HD:(i % 2 + 1) * HD, g, 0:(t + 1) * P],
                             v=lambda i, b, g=g: vtok[:, b, g * HD:(g + 1) * HD],
                             out=oT[:, 2 * g:2 * g + 2, t * P:(t + 1) * P])
                    u["parts"] = [u]
                    units.append(u)
            attend(units, T, projected)
            swa.close()
            swa_done = [(dve.sem, dve.n), (act.sem, act.n), (pe.sem, pe.n)]

            r, k, v, ld, cum, a, g, kk, bon, t1, t2 = (
                z.rearrange("p (c t) -> p c t", c=4) for z in (r_, k_, v_, ld_, cum_, a_, g_, kk_, bon_, t1_, t2_))

            @block.scalar
            def _(_e):
                for point in swa_done:
                    A.wait_ge(*point)
                A.activation(wa[0:64, :], wa[0:64, :], ACT.Tanh)
                Ring.p = act.count(A.activation(glo, glo, ACT.Sigmoid).then_inc(act.sem, 1))
            wps, aps, gps = (banks(2 * n, 2).rearrange("p (c t) -> p c t", c=4) for n in range(3))

            @block.tensor
            def _(_e):
                E.wait_ge(*Ring.p)
                for point in swa_done:
                    E.wait_ge(*point)
                wa2, g2 = prm("wa2"), prm("g2")
                for c in range(4):
                    cs = slice(c * P, (c + 1) * P)
                    E.matmul(wps[:, c, :], wa2[0:64, cs], wa[0:64, :], start=True, stop=True)
                    E.matmul(aps[:, c, :], wa2[64:128, cs], wa[64:128, :], start=True, stop=True)
                    ins = E.matmul(gps[:, c, :], g2[:, cs], glo, start=True, stop=True)
                Ring.p = pe.count(ins.then_inc(pe.sem, 1))

            @block.scalar
            def _(_e):
                A.wait_ge(*Ring.p)
                for c in range(4):
                    A.activation(ld[:, c, :], wps[:, c, :], ACT.Sigmoid, bias=prm("w0")[:, c:c + 1])
                Ring.q = act.count(A.activation(a[:, 0, :], aps[:, 0, :], ACT.Sigmoid, bias=prm("a0")[:, 0:1]).then_inc(act.sem, 1))
                for c in range(1, 4):
                    A.activation(a[:, c, :], aps[:, c, :], ACT.Sigmoid, bias=prm("a0")[:, c:c + 1])
                Ring.p = act.count(A.activation(g_, banks(4, 2), ACT.Copy).then_inc(act.sem, 1))

            @block.vector
            def _(_e):
                V.wait_ge(*Ring.q)
                for point in swa_done:
                    V.wait_ge(*point)
                vl(V.tensor_scalar(ld_, ld_, -math.exp(-0.5), None, ALU.mult).then_inc(dve.sem, 1))
                for c in range(4):
                    V.tensor_tensor_scan(cum[:, c, :], cst("scan_keep"), ld[:, c, :], 0.0, ALU.mult, ALU.add)
                for c in range(4):
                    p = dve.count(V.tensor_scalar(kk[:, c, :], k[:, c, :], prm("k_k")[:, c:c + 1], None, ALU.mult).then_inc(dve.sem, 1))
                V.wait_ge(*p)
                Ring.q = vl(V.tensor_tensor(t1_, kk_, kk_, ALU.mult).then_inc(dve.sem, 1))

            def head_sum(src, ready_):
                @block.tensor
                def _(_e):
                    E.wait_ge(*ready_)
                    for h in range(2):
                        ins = E.matmul(bank(6 + h), cst("headsum"), src[:, h * 512:(h + 1) * 512], start=True, stop=True)
                    Ring.p = pe.count(ins.then_inc(pe.sem, 1))
                return Ring.p

            act_gate = Ring.p
            p = head_sum(t1_, Ring.q)

            @block.scalar
            def _(_e):
                A.wait_ge(*p)
                Ring.p = act.count(A.activation(t2_, banks(6, 2), ACT.Sqrt).then_inc(act.sem, 1))

            @block.vector
            def _(_e):
                V.wait_ge(*Ring.p)
                V.wait_ge(*act_gate)
                vl(V.tensor_scalar(t2_, t2_, 1e-12, None, ALU.max).then_inc(dve.sem, 1))
                vl(V.reciprocal(t2_, t2_).then_inc(dve.sem, 1))
                vl(V.tensor_tensor(kk_, kk_, t2_, ALU.mult).then_inc(dve.sem, 1))
                for c in range(4):
                    p_ = dve.count(V.tensor_scalar(t1[:, c, :], a[:, c, :], prm("k_a")[:, c:c + 1], omka[:, c:c + 1],
                                                  ALU.mult, ALU.add).then_inc(dve.sem, 1))
                V.wait_ge(*p_)
                vl(V.tensor_tensor(k_, k_, t1_, ALU.mult).then_inc(dve.sem, 1))
                vl(V.scalar_tensor_tensor(a_, kk_, -1.0, a_, ALU.mult, ALU.mult).then_inc(dve.sem, 1))
                for c in range(4):
                    p_ = dve.count(V.scalar_tensor_tensor(t1[:, c, :], r[:, c, :], prm("r_k")[:, c:c + 1], k[:, c, :],
                                                         ALU.mult, ALU.mult).then_inc(dve.sem, 1))
                Ring.q = p_
            p = head_sum(t1_, Ring.q)

            @block.vector
            def _(_e):
                V.wait_ge(*p)
                vl(V.tensor_tensor(bon_, banks(6, 2), v_, ALU.mult).then_inc(dve.sem, 1))
                Ring.q = vl(V.tensor_tensor(t1_, cum_, ld_, ALU.subtract).then_inc(dve.sem, 1))

            @block.scalar
            def _(_e):
                A.wait_ge(*Ring.q)
                A.activation(t1_, t1_, ACT.Exp)
                A.activation(t2_, cum_, ACT.Exp, scale=-1.0)
                al(A.activation(ld_, cum_, ACT.Exp).then_inc(act.sem, 1))
                Ring.q = (act.sem, act.n)
            e1 = ld

            @block.vector
            def _(_e):
                V.wait_ge(*Ring.q)
                V.tensor_tensor(kk_, kk_, t1_, ALU.mult)
                V.tensor_tensor(a_, a_, t2_, ALU.mult)
                V.tensor_tensor(k_, k_, t2_, ALU.mult)
                Ring.q = vl(V.tensor_tensor(r_, r_, ld_, ALU.mult).then_inc(dve.sem, 1))
            scaled = Ring.q
            kap, bet, kh, rh = kk, a, k, r

            vt = htok_[:, 0:1024].rearrange("p (t d) -> p t d", t=NT)
            bt = htok_[:, 1024:2048].rearrange("p (t d) -> p t d", t=NT)
            kt = cum_.rearrange("p (t d) -> p t d", t=NT)
            n = 0
            for src, dst in ((v, vt), (bet, bt), (kh, kt)):
                for t in range(NT):
                    @block.tensor
                    def _(_e):
                        E.wait_ge(*scaled)
                        for c in range(4):
                            ins = E.transpose(bank(n)[:, c * P:(c + 1) * P], src[:, c, t * P:(t + 1) * P], ident)
                        Ring.p = pe.count(ins.then_inc(pe.sem, 1))

                    @block.scalar
                    def _(_e):
                        A.wait_ge(*Ring.p)
                        Ring.p = act.count(A.activation(dst[:, t, :], bank(n), ACT.Copy).then_inc(act.sem, 1))
                    n += 1
            tok_done = Ring.p

            def mat(t, h):
                return 8 * t + 4 * (h % 2) + h // 2

            L, LT, X, XT, A2 = (ar.take(16 * P).rearrange("p (m s) -> p m s", m=16) for _ in range(5))
            L_, LT_, X_, XT_, A2_ = (z.rearrange("p m s -> p (m s)") for z in (L, LT, X, XT, A2))
            bank_free = [tok_done] * 8

            def gram(lhs, rhs, mask, dst, first, ready_):
                for q in range(4):
                    b = first + q

                    @block.tensor
                    def _(_e):
                        for point in ready_:
                            E.wait_ge(*point)
                        E.wait_ge(*bank_free[b])
                        for m in range(4 * q, 4 * q + 4):
                            t, h = m // 8, 2 * (m % 4) + (m // 4) % 2
                            hs, ts = slice((h % 2) * HD, (h % 2 + 1) * HD), slice(t * P, (t + 1) * P)
                            ins = E.matmul(bank(b)[:, (m % 4) * P:(m % 4 + 1) * P], lhs[hs, h // 2, ts],
                                           rhs[hs, h // 2, ts], start=True, stop=True)
                        Ring.p = pe.count(ins.then_inc(pe.sem, 1))

                    @block.vector
                    def _(_e):
                        V.wait_ge(*Ring.p)
                        bank_free[b] = dve.count(V.tensor_tensor(
                            dst[:, 4 * q:4 * q + 4, :], bank(b).rearrange("p (m s) -> p m s", m=4),
                            spread(mask.rearrange("p (o s) -> p o s", o=1), [P, 4, P]), ALU.mult).then_inc(dve.sem, 1))
                return bank_free[first + 3]

            gram(kap, bet, cst("lower"), L, 0, [scaled])
            gram(bet, kap, cst("upper"), LT, 4, [scaled])
            lev = cst("level").rearrange("p (l s) -> p l s", l=LEVELS)
            levt = cst("level_t").rearrange("p (l s) -> p l s", l=LEVELS)

            def levels(m):
                return spread(m.rearrange("p (o s) -> p o s", o=1), [P, 16, P])

            @block.vector
            def _(_e):
                V.wait_ge(dve.sem, dve.n)
                V.tensor_tensor(X, L, levels(lev[:, 0, :]), ALU.mult)
                vl(V.tensor_tensor(XT, LT, levels(levt[:, 0, :]), ALU.mult).then_inc(dve.sem, 1))
                V.tensor_tensor(X, X, levels(ident), ALU.add)
                Ring.q = vl(V.tensor_tensor(XT, XT, levels(ident), ALU.add).then_inc(dve.sem, 1))
            LMv = t12.rearrange("p (m s) -> p m s", m=16)
            x_ready, lm_read = [Ring.q] * 4, [Ring.q] * 4
            lm_pts = [None] * 4

            def level_mask(l, q):
                @block.vector
                def _(_e):
                    V.wait_ge(*lm_read[q])
                    lm_pts[q] = dve.count(V.tensor_tensor(
                        LMv[:, 4 * q:4 * q + 4, :], LT[:, 4 * q:4 * q + 4, :],
                        spread(levt[:, l:l + 1, :], [P, 4, P]), ALU.mult).then_inc(dve.sem, 1))

            for q in range(4):
                level_mask(1, q)
            for l in range(1, LEVELS):
                t_pts = []
                for q in range(4):
                    @block.tensor
                    def _(_e):
                        E.wait_ge(*lm_pts[q])
                        E.wait_ge(*x_ready[q])
                        E.wait_ge(*bank_free[q])
                        for m in range(4 * q, 4 * q + 4):
                            ins = E.matmul(bank(q)[:, (m % 4) * P:(m % 4 + 1) * P], LMv[:, m, :], X[:, m, :],
                                           start=True, stop=True)
                        lm_read[q] = pe.count(ins.then_inc(pe.sem, 1))

                    @block.scalar
                    def _(_e):
                        A.wait_ge(*lm_read[q])
                        A.wait_ge(*x_ready[q])
                        t_pts.append(act.count(A.activation(A2_[:, q * 512:(q + 1) * 512], bank(q), ACT.Copy).then_inc(act.sem, 1)))
                if l + 1 < LEVELS:
                    for q in range(4):
                        level_mask(l + 1, q)
                for q in range(4):
                    todo = ((XT, A2, X_, 4), (A2, XT, XT_, 0))[l == LEVELS - 1:]
                    upd = []
                    for lhs, rhs, dst, first in todo:
                        @block.tensor
                        def _(_e):
                            E.wait_ge(*t_pts[q])
                            E.wait_ge(*bank_free[first + q])
                            for m in range(4 * q, 4 * q + 4):
                                ins = E.matmul(bank(first + q)[:, (m % 4) * P:(m % 4 + 1) * P], lhs[:, m, :],
                                               rhs[:, m, :], start=True, stop=True)
                            upd.append((pe.count(ins.then_inc(pe.sem, 1)), dst, first + q))
                    for p, dst, b in upd:
                        @block.vector
                        def _(_e):
                            V.wait_ge(*p)
                            bank_free[b] = dve.count(V.tensor_tensor(dst[:, q * 512:(q + 1) * 512],
                                                                    dst[:, q * 512:(q + 1) * 512], bank(b), ALU.add).then_inc(dve.sem, 1))
                    x_ready[q] = bank_free[q]
            inv_done = [x_ready[3], (pe.sem, pe.n)]
            MT, A1 = L, LT

            @block.vector
            def _(_e):
                for point in inv_done:
                    V.wait_ge(*point)
                V.wait_ge(act.sem, act.n)
            gram(kh, kap, cst("upper"), MT, 0, inv_done)
            gram(bet, rh, cst("upper_in"), A1, 4, inv_done)
            gram(kh, rh, cst("upper_in"), A2, 0, inv_done)
            gram_done = (dve.sem, dve.n)
            ST = ar.take(4 * HD).rearrange("p (c i) -> p c i", c=4)
            MV = X_[:, 0:1024].rearrange("p (t d) -> p t d", t=NT)
            Pv, Uv = t1_[:, 0:512], t1_[:, 512:1024]
            y = t2

            @block.tensor
            def _(_e):
                E.wait_ge(*gram_done)
                for t in range(NT):
                    for h in range(8):
                        hc = slice(h * HD, (h + 1) * HD)
                        E.matmul(bank(4 + t)[:, hc], MT[:, mat(t, h), :], vt[:, t, hc], start=True, stop=True)
                    for h in range(8):
                        ps, hc = slice((h % 2) * HD, (h % 2 + 1) * HD), slice(h * HD, (h + 1) * HD)
                        ins = E.matmul(bank(6 + t)[ps, (h // 2) * P:(h // 2 + 1) * P], vt[:, t, hc],
                                       A2[:, mat(t, h), :], start=True, stop=True)
                Ring.p = pe.count(ins.then_inc(pe.sem, 1))

            @block.vector
            def _(_e):
                V.wait_ge(*Ring.p)
                V.wait_ge(*gram_done)
                V.memset(ST, 0.0)
                V.tensor_copy(MV, banks(4, 2).rearrange("p (t d) -> p t d", t=NT))
                for t in range(NT):
                    Ring.q = vl(V.tensor_copy(y[:, :, t * P:(t + 1) * P], bank(6 + t).rearrange("p (c n) -> p c n", c=4)).then_inc(dve.sem, 1))
            s_ready = y_free = Ring.q
            for c4 in range(T // C64):
                t, hb = c4 // 2, (c4 % 2) * 64
                hs = slice(hb, hb + 64)
                tok = slice(t * P + hb, t * P + hb + 64)

                @block.tensor
                def _(_e):
                    E.wait_ge(*s_ready)
                    for h in (0, 2, 4, 6, 1, 3, 5, 7):
                        ps, c = slice((h % 2) * HD, (h % 2 + 1) * HD), h // 2
                        ins = E.matmul(bank(h % 2)[hs, c * HD:(c + 1) * HD], kap[ps, c, tok], ST[ps, c, :],
                                       start=True, stop=True)
                    Ring.p = pe.count(ins.then_inc(pe.sem, 1))
                    E.wait_ge(*y_free)
                    for h in (0, 2, 4, 6, 1, 3, 5, 7):
                        ps, c = slice((h % 2) * HD, (h % 2 + 1) * HD), h // 2
                        ins = E.matmul(bank(4 + h % 2)[ps, c * HD:(c + 1) * HD], ST[ps, c, :], rh[ps, c, tok],
                                       start=True, stop=True)
                    pe.count(ins.then_inc(pe.sem, 1))

                @block.vector
                def _(_e):
                    V.wait_ge(*Ring.p)
                    for o in range(2):
                        Ring.q = dve.count(V.tensor_tensor(
                            Pv[hs, :].rearrange("p (c o i) -> p c o i", o=2, i=HD)[:, :, o, :],
                            bank(o)[hs, 0:T].rearrange("p (c i) -> p c i", c=4),
                            MV[hs, t, :].rearrange("p (c o i) -> p c o i", o=2, i=HD)[:, :, o, :], ALU.add).then_inc(dve.sem, 1))

                @block.tensor
                def _(_e):
                    E.wait_ge(*Ring.q)
                    for h in range(8):
                        ins = E.matmul(bank(2)[hs, h * HD:(h + 1) * HD], XT[hs, mat(t, h), hs],
                                       Pv[hs, h * HD:(h + 1) * HD], start=True, stop=True)
                    Ring.p = pe.count(ins.then_inc(pe.sem, 1))

                @block.vector
                def _(_e):
                    V.wait_ge(*Ring.p)
                    Ring.q = dve.count(V.tensor_copy(Uv[hs, :], bank(2)[hs, :]).then_inc(dve.sem, 1))

                @block.tensor
                def _(_e):
                    E.wait_ge(*Ring.q)
                    for h in range(8):
                        ps, c = slice((h % 2) * HD, (h % 2 + 1) * HD), h // 2
                        o, hc = bank(3)[ps, c * HD:(c + 1) * HD], slice(h * HD, (h + 1) * HD)
                        E.matmul(o, bt[hs, t, hc], Uv[hs, hc], start=True, stop=False)
                        ins = E.matmul(o, kt[hs, t, hc], vt[hs, t, hc], start=False, stop=True)
                    Ring.p = pe.count(ins.then_inc(pe.sem, 1))
                    for h in range(8):
                        ps, c = slice((h % 2) * HD, (h % 2 + 1) * HD), h // 2
                        ins = E.matmul(bank(6)[ps, c * HD:(c + 1) * HD], Uv[hs, h * HD:(h + 1) * HD],
                                       A1[hs, mat(t, h), hs], start=True, stop=True)
                    Ring.q = pe.count(ins.then_inc(pe.sem, 1))

                @block.vector
                def _(_e):
                    V.wait_ge(*Ring.p)
                    vl(V.tensor_tensor(ST, ST, bank(3)[:, 0:T].rearrange("p (c n) -> p c n", c=4), ALU.add).then_inc(dve.sem, 1))
                    Ring.p = vl(V.tensor_tensor(ST, ST, spread(e1[:, :, c4 * 64 + 63:c4 * 64 + 64], [P, 4, HD]), ALU.mult).then_inc(dve.sem, 1))
                    V.wait_ge(*Ring.q)
                    for o in range(2):
                        ps = slice(o * HD, (o + 1) * HD)
                        vl(V.tensor_tensor(y[ps, :, tok], y[ps, :, tok],
                                           bank(4 + o)[ps, 0:T].rearrange("p (c n) -> p c n", c=4), ALU.add).then_inc(dve.sem, 1))
                    Ring.q = vl(V.tensor_tensor(y[:, :, tok], y[:, :, tok],
                                                bank(6)[:, 0:T].rearrange("p (c n) -> p c n", c=4), ALU.add).then_inc(dve.sem, 1))
                s_ready, y_free = Ring.p, Ring.q

            p = head_sum(t2_, y_free)

            @block.vector
            def _(_e):
                V.wait_ge(*p)
                Ring.q = vl(V.scalar_tensor_tensor(t2_, banks(6, 2), -1.0 / HD, t2_, ALU.mult, ALU.add).then_inc(dve.sem, 1))

            @block.scalar
            def _(_e):
                A.wait_ge(*Ring.q)
                Ring.q = act.count(A.activation(t1_, t2_, ACT.Square).then_inc(act.sem, 1))
            p = head_sum(t1_, Ring.q)

            @block.vector
            def _(_e):
                V.wait_ge(*p)
                Ring.q = vl(V.tensor_scalar(t1_, banks(6, 2), 1.0 / HD, 64e-5, ALU.mult, ALU.add).then_inc(dve.sem, 1))

            @block.scalar
            def _(_e):
                A.wait_ge(*Ring.q)
                Ring.q = act.count(A.activation(t1_, t1_, ACT.Sqrt).then_inc(act.sem, 1))

            @block.vector
            def _(_e):
                V.wait_ge(*Ring.q)
                vl(V.reciprocal(t1_, t1_).then_inc(dve.sem, 1))
                vl(V.tensor_tensor(t2_, t2_, t1_, ALU.mult).then_inc(dve.sem, 1))
                for c in range(4):
                    p_ = dve.count(V.tensor_scalar(t2[:, c, :], t2[:, c, :], prm("ln_g")[:, c:c + 1],
                                                  prm("ln_b")[:, c:c + 1], ALU.mult, ALU.add).then_inc(dve.sem, 1))
                V.wait_ge(*p_)
                vl(V.tensor_tensor(t2_, t2_, bon_, ALU.add).then_inc(dve.sem, 1))
                Ring.q = vl(V.tensor_tensor(oT[:, 4:8, :], t2, g, ALU.mult).then_inc(dve.sem, 1))
            ar.close()
            r_row = row_of(prm("mix_post_g0"), 1.0, [Ring.q])
            done = out_project("w_hy_out", 8, oT, [(dve.sem, dve.n), (act.sem, act.n), (pe.sem, pe.n)])
            return add_normed(done + [r_row])

        def nsa(ready):
            ar = Arena()
            qT = ar.take(8 * T).rearrange("p (c t) -> p c t", c=8)
            kc2, vc2, ksT, kwT = (ar.take(4 * T).rearrange("p (c t) -> p c t", c=4) for _ in range(4))
            vs, vw = (ar.take(NT * T).rearrange("p (t d) -> p t d", t=NT) for _ in range(2))
            gates = ar.take(NT * 48).rearrange("p (t n) -> p t n", t=NT)

            def evac(c, b, p):
                @block.scalar
                def _(_e):
                    A.wait_ge(*p)
                    bt = b[:, 0:T]
                    if c < 8:
                        ins = A.activation(qT[:, c, :], bt, ACT.Copy, scale=HD ** -0.5)
                    elif c < 16:
                        dst = (kc2, vc2)[(c - 8) // 4][:, (c - 8) % 4, :]
                        A.activation(dst[0:64, :], bt[0:64, :], ACT.Copy)
                        ins = A.activation(dst[64:128, 0:T - 1], bt[64:128, 1:T], ACT.Copy)
                    elif c < 24:
                        ins = A.activation((ksT, kwT)[(c - 16) // 4][:, (c - 16) % 4, :], bt, ACT.Copy)
                    elif c < 28:
                        m = c - 24
                        ins = A.activation((vs, vw)[m // 2][:, :, (m % 2) * P:(m % 2 + 1) * P],
                                           bt.rearrange("p (t d) -> p t d", t=NT), ACT.Copy)
                    else:
                        ins = A.activation(gates, b[:, 0:96].rearrange("p (t n) -> p t n", t=NT), ACT.Sigmoid)
                    Ring.q = act.count(ins.then_inc(act.sem, 1))
                return (Ring.q,)

            proj = Arena()
            h = halves(proj, KC)
            wp = weight_parts(proj)
            h_ready = norm_transpose(prm("mix_pre_g1"), None, ready, h)
            project("w_ns_in", 29, evac, h_ready, h, wp, tokens=(24, 25, 26, 27, 28), widths={28: 48})
            proj.close()
            projected = [(act.sem, act.n), (dve.sem, dve.n), (pe.sem, pe.n)]
            oT = hT

            @block.scalar
            def _(_e):
                A.wait_ge(pe.sem, pe.n)
            blk = [ar.take(16 * 4 * N_CMP).rearrange("p (j g c) -> p j g c", j=16, g=4) for _ in range(2)]
            hdn = [ar.take(2 * 4 * N_CMP).rearrange("p (f n) -> p f n", f=2) for _ in range(2)]
            kcmp = ar.take(4 * N_CMP).rearrange("p (g c) -> p g c", g=4)
            vcmp = ar.take(4 * HD).rearrange("p (g d) -> p g d", g=4)
            gcmp = ar.take(NT * 16).rearrange("p (t h) -> p t h", t=NT)

            @block.vector
            def _(_e):
                for point in projected:
                    V.wait_ge(*point)
                for kv in range(2):
                    src, pos = (kc2, vc2)[kv], prm("pos_" + "kv"[kv])
                    for j in range(16):
                        p = dve.count(V.tensor_scalar(blk[kv][:, j, :, :], src[:, :, 2 * j:2 * j + 16 * (N_CMP - 1) + 1:16],
                                                     pos[:, j:j + 1], None, ALU.add).then_inc(dve.sem, 1))
                for t in range(NT):
                    p = dve.count(V.tensor_scalar(gcmp[:, t, :], gates[:, t, 0:48:3], cst(f"cmp_any{t}"), None, ALU.mult).then_inc(dve.sem, 1))
                Ring.q = p
            blocks_ready = Ring.q
            for kv in range(2):
                pts = []
                for half in range(2):
                    s, full = load(dram["w_cmp1"][2 * kv + half:2 * kv + half + 1], 1)
                    w = slot_ap(s, 2048).rearrange("p (j f) -> p j f", j=8)
                    pts.append((s, w, full))

                @block.tensor
                def _(_e):
                    E.wait_ge(*blocks_ready)
                    E.wait_ge(*pts[0][2])
                    E.wait_ge(*pts[1][2])
                    for f in range(2):
                        for j in range(16):
                            ins = E.matmul(bank(4 + f)[:, kv * 64:kv * 64 + 60], pts[j // 8][1][:, j % 8, f * P:(f + 1) * P],
                                           blk[kv][:, j, :, :], start=j == 0, stop=j == 15)
                    Ring.p = pe.count(ins.then_inc(pe.sem, 1))
                Ring.used[pts[0][0]] = Ring.used[pts[1][0]] = [Ring.p]

                @block.scalar
                def _(_e):
                    A.wait_ge(*Ring.p)
                    for f in range(2):
                        ins = A.activation(hdn[kv][:, f, :], bank(4 + f)[:, kv * 64:kv * 64 + 60], ACT.Gelu_apprx_tanh)
                    Ring.q = act.count(ins.then_inc(act.sem, 1))

                @block.tensor
                def _(_e):
                    E.wait_ge(*Ring.q)
                    if kv == 0:
                        w2 = prm("cw2_k").rearrange("p (f n) -> p f n", f=2)
                        for f in range(2):
                            ins = E.matmul(bank(6)[:, 0:60], w2[:, f, :], hdn[0][:, f, :], start=f == 0, stop=f == 1)
                    else:
                        w2 = prm("cw2_v").rearrange("p (f n) -> p f n", f=2)
                        for gq in range(4):
                            for f in range(2):
                                ins = E.matmul(bank(7)[0:N_CMP, gq * HD:(gq + 1) * HD],
                                               hdn[1][:, f, gq * N_CMP:(gq + 1) * N_CMP], w2[:, f, :],
                                               start=f == 0, stop=f == 1)
                    Ring.p = pe.count(ins.then_inc(pe.sem, 1))

                @block.scalar
                def _(_e):
                    A.wait_ge(*Ring.p)
                    if kv == 0:
                        al(A.activation(kcmp, bank(6)[:, 0:60].rearrange("p (g c) -> p g c", g=4), ACT.Copy).then_inc(act.sem, 1))
                    else:
                        al(A.activation(vcmp[0:N_CMP], bank(7)[0:N_CMP, 0:4 * HD].rearrange("p (g d) -> p g d", g=4), ACT.Copy).then_inc(act.sem, 1))
            slopes = alibi(16)
            units = []
            for gq in range(4):
                for t in range(NT):
                    parts = []
                    for br in range(3):
                        kk_ = (kcmp, ksT, kwT)[br]
                        nk = N_CMP if br == 0 else (t + 1) * P
                        u = dict(branch=br, scale=1.0, slopes=slopes[4 * gq:4 * gq + 4], keys=nk,
                                 blocks=1 if br == 0 else t + 1, last=br == 2,
                                 dist=cst(f"cmp{t}") if br == 0 else cst(f"causal{t}"),
                                 gates=gcmp[:, t, 4 * gq:4 * gq + 4] if br == 0 else
                                 gates[:, t, 12 * gq + br:12 * gq + 12:3],
                                 q=lambda i, gq=gq, t=t: qT[(i % 2) * HD:(i % 2 + 1) * HD, 2 * gq + i // 2, t * P:(t + 1) * P],
                                 k=lambda i, gq=gq, nk=nk, kk_=kk_: kk_[(i % 2) * HD:(i % 2 + 1) * HD, gq, 0:nk],
                                 out=oT[:, 2 * gq:2 * gq + 2, t * P:(t + 1) * P])
                        if br == 0:
                            u["v"] = lambda i, b, gq=gq: vcmp[0:N_CMP, gq, :]
                        else:
                            u["v"] = lambda i, b, gq=gq, br=br: (vs, vw)[br - 1][:, b, gq * HD:(gq + 1) * HD]
                        parts.append(u)
                        units.append(u)
                    parts[-1]["parts"] = parts
            o_ready = attend(units, T, [(act.sem, act.n), (dve.sem, dve.n), (pe.sem, pe.n)])
            ar.close()
            r_row = row_of(prm("mix_post_g1"), 1.0, o_ready)
            done = out_project("w_ns_out", 8, oT, o_ready)
            return add_normed(done + [r_row])

        def conv_ffn(l, ready):
            ar = Arena()
            h = halves(ar, KC)
            first, rest = ffn(f"w_conv{l}", h, ar, conv=l, mod=(0, l))

            def meanwhile():
                row = row_of(prm(f"ffn_post_g{l}"), 1.0, ready)
                first(ready)
                return row
            h_ready = norm_transpose(prm(f"ffn_pre_g{l}"), None, ready, h, meanwhile)
            done = rest(h_ready)
            ar.close()
            x_ready = add_normed(done)
            return finish_mod() + x_ready

        gm = small[:, 48:56]

        def mod_col(l, s, kind):
            a = l * 72 + (3 * s + kind) * 8
            return modT[:, a:a + 8]

        def modulated(l, s, ready, parts, meanwhile=None):
            @block.vector
            def _(_e):
                for point in ready:
                    V.wait_ge(*point)
                vl(V.tensor_scalar(gm, mod_col(l, s, 1), 1.0, None, ALU.add).then_inc(dve.sem, 1))
                Ring.q = vl(V.tensor_tensor(gm, gm, prm(f"norm_g{l}{s}"), ALU.mult).then_inc(dve.sem, 1))
            return norm_transpose(gm, mod_col(l, s, 0), ready, parts, meanwhile)

        def silu_ffn(l, s, w, ready, mod=None):
            ar = Arena()
            h = halves(ar, KC)
            first, rest = ffn(f"w_ffn{l}{w}", h, ar, mod=mod)

            def meanwhile():
                row = row_of(mod_col(l, s, 2), 0.5, ready)
                first(ready)
                return row
            h_ready = modulated(l, s, ready, h, meanwhile)
            done = rest(h_ready)
            ar.close()
            x_ready = add_gated(done)
            return finish_mod() + x_ready

        def ssd(ready):
            y_ar, ar = Arena(), None
            xb_ = y_ar.take(16 * T)
            xb = xb_.rearrange("p (c t) -> p c t", t=T)
            ar = Arena()
            zs_ = ar.take(16 * T)
            zs = zs_.rearrange("p (c t) -> p c t", t=T)
            bc = ar.take(16 * T).rearrange("p (c t) -> p c t", t=T)
            pad = [ar.take(T + 4) for _ in range(2)]
            cv = [ar.take(T) for _ in range(2)]
            dt, dtA, acum = (ar.take(NT * 64) for _ in range(3))
            tmp = [ar.take(NT * 64) for _ in range(3)]
            acT = ar.take(T)
            Arow = ar.take(64)
            d3 = lambda z: z.rearrange("p (t n) -> p t n", t=NT)

            proj = Arena()
            h_ = halves(proj, KC)
            wp = weight_parts(proj, 2)
            h_ready = modulated(0, 1, ready, h_)

            @block.vector
            def _(_e):
                for point in h_ready:
                    V.wait_ge(*point)
                for q in range(2):
                    V.memset(pad[q][:, 0:2], 0.0)
                    vl(V.memset(pad[q][:, T + 2:T + 4], 0.0).then_inc(dve.sem, 1))
            pad_ready = (dve.sem, dve.n)
            cv_free = [loaded] * 2

            def evac(c, b, p):
                if c < 16:
                    @block.scalar
                    def _(_e):
                        A.wait_ge(*p)
                        A.wait_ge(*pad_ready)
                        Ring.q = act.count(A.activation(zs[:, c, :], b[:, 0:T], ACT.Silu).then_inc(act.sem, 1))
                    return (Ring.q,)
                if c < 48:
                    m = c - 16
                    q = m % 2

                    @block.scalar
                    def _(_e):
                        A.wait_ge(*p)
                        A.wait_ge(*cv_free[q])
                        A.wait_ge(*cv_silu[q])
                        al(A.activation(pad[q][:, 2:T + 2], b[:, 0:T], ACT.Copy).then_inc(act.sem, 1))
                        Ring.q = act.count(A.activation(cv[q], pad[q][:, 0:T], ACT.Copy,
                                                        scale=prm("sconv_w0")[:, m:m + 1]).then_inc(act.sem, 1))
                    freed = Ring.q

                    @block.vector
                    def _(_e):
                        V.wait_ge(*Ring.q)
                        for j in range(1, 5):
                            Ring.q = vl(V.scalar_tensor_tensor(cv[q], pad[q][:, j:j + T], prm(f"sconv_w{j}")[:, m:m + 1],
                                                               cv[q], ALU.mult, ALU.add).then_inc(dve.sem, 1))
                    cv_free[q] = Ring.q
                    pend.append((m, q, Ring.q))
                    if len(pend) > 1:
                        silu_out()
                    return (freed,)
                while pend:
                    silu_out()

                @block.vector
                def _(_e):
                    V.wait_ge(*p)
                    bias = prm("dt_bias")
                    bb = spread(bias.rearrange("p (o n) -> p o n", o=1), [P, NT, 64])
                    vl(V.tensor_tensor(d3(dt), d3(b[:, 0:2 * 64]), bb, ALU.add).then_inc(dve.sem, 1))
                    vl(V.tensor_scalar(tmp[0], dt, -1.0, None, ALU.mult).then_inc(dve.sem, 1))
                    Ring.q = vl(V.tensor_tensor(tmp[0], tmp[0], dt, ALU.min).then_inc(dve.sem, 1))
                return (Ring.q,)

            pend, cv_silu = [], [loaded] * 2

            def silu_out():
                m, q, p = pend.pop(0)

                @block.scalar
                def _(_e):
                    A.wait_ge(*p)
                    cv_silu[q] = act.count(A.activation(xb[:, m, :] if m < 16 else bc[:, m - 16, :], cv[q], ACT.Silu, bias=prm("sconv_b")[:, m:m + 1]).then_inc(act.sem, 1))

            project("w_ssd_in", 49, evac, h_ready, h_, wp, tokens=(48,), widths={48: 64})
            proj.close()
            xt = [hT_[:, :], htok_[:, :]]
            neg_abs = Ring.q

            @block.scalar
            def _(_e):
                A.wait_ge(*neg_abs)
                A.activation(Arow, prm("a_log"), ACT.Exp)
                Ring.q = al(A.activation(tmp[0], tmp[0], ACT.Exp).then_inc(act.sem, 1))

            @block.vector
            def _(_e):
                V.wait_ge(*Ring.q)
                vl(V.tensor_scalar(tmp[1], tmp[0], 2.0, None, ALU.add).then_inc(dve.sem, 1))
                vl(V.reciprocal(tmp[1], tmp[1]).then_inc(dve.sem, 1))
                vl(V.tensor_tensor(tmp[0], tmp[0], tmp[1], ALU.mult).then_inc(dve.sem, 1))
                vl(V.tensor_tensor(tmp[1], tmp[0], tmp[0], ALU.mult).then_inc(dve.sem, 1))
                vl(V.tensor_scalar(tmp[2], tmp[1], 1.0 / 17, 1.0 / 15, ALU.mult, ALU.add).then_inc(dve.sem, 1))
                for n in range(13, 0, -2):
                    vl(V.tensor_tensor(tmp[2], tmp[2], tmp[1], ALU.mult).then_inc(dve.sem, 1))
                    vl(V.tensor_scalar(tmp[2], tmp[2], 1.0 / n, None, ALU.add).then_inc(dve.sem, 1))
                vl(V.tensor_tensor(tmp[2], tmp[2], tmp[0], ALU.mult).then_inc(dve.sem, 1))
                vl(V.tensor_scalar(dt, dt, 0.0, None, ALU.max).then_inc(dve.sem, 1))
                vl(V.scalar_tensor_tensor(dt, tmp[2], 2.0, dt, ALU.mult, ALU.add).then_inc(dve.sem, 1))
                Ring.q = vl(V.scalar_tensor_tensor(d3(dtA), d3(dt), -1.0,
                                                   spread(Arow.rearrange("p (o n) -> p o n", o=1), [P, NT, 64]),
                                                   ALU.mult, ALU.mult).then_inc(dve.sem, 1))
            trif, trib = (cst(n).rearrange("p (u t) -> p u t", u=NT) for n in ("tri_f", "tri_b"))
            in_done = [Ring.q, (act.sem, act.n), (pe.sem, pe.n)]

            @block.tensor
            def _(_e):
                for point in in_done:
                    E.wait_ge(*point)
                for t in range(NT):
                    for d, tri in enumerate((trif, trib)):
                        for u in range(NT):
                            E.matmul(bank(0)[:, t * 64 + d * 32:t * 64 + d * 32 + 32], tri[:, u, t * P:(t + 1) * P],
                                     d3(dtA)[:, u, d * 32:(d + 1) * 32], start=u == 0, stop=u == NT - 1)
                for d, tri in enumerate((trif, trib)):
                    for u in range(NT):
                        ins = E.matmul(bank(1)[d * 32:(d + 1) * 32, 0:T], d3(dtA)[:, u, d * 32:(d + 1) * 32],
                                       tri[:, u, :], start=u == 0, stop=u == NT - 1)
                Ring.p = pe.count(ins.then_inc(pe.sem, 1))

            @block.vector
            def _(_e):
                V.wait_ge(*Ring.p)
                V.tensor_copy(acum, bank(0)[:, 0:NT * 64])
                Ring.q = vl(V.tensor_copy(acT[0:64, :], bank(1)[0:64, 0:T]).then_inc(dve.sem, 1))
            ac_ready = Ring.q
            freed = [loaded] * 4
            for n in range(8):
                t, c0 = n // 4, (n % 4) * 4

                @block.tensor
                def _(_e):
                    for point in in_done:
                        E.wait_ge(*point)
                    E.wait_ge(*freed[n % 4])
                    for c in range(4):
                        ins = E.transpose(bank(4 + n % 4)[:, c * P:(c + 1) * P], xb[:, c0 + c, t * P:(t + 1) * P], ident)
                    Ring.p = pe.count(ins.then_inc(pe.sem, 1))

                @block.scalar
                def _(_e):
                    A.wait_ge(*Ring.p)
                    freed[n % 4] = act.count(A.activation(xt[t][:, c0 * P:(c0 + 4) * P], bank(4 + n % 4), ACT.Copy).then_inc(act.sem, 1))
            xt_ready = freed[3]
            G_ = [ar.take(768) for _ in range(2)]
            xd = [ar.take(NT * 2 * T).rearrange("p (u d n) -> p u d n", u=NT, d=2) for _ in range(2)]
            ee = [ar.take(768) for _ in range(3)]
            ee_free, g_free, arow_free, y_free = [loaded] * 3, [loaded] * 2, [loaded] * 2, [loaded] * 2
            ee_ready = [loaded] * 3
            acu, dt3 = d3(acum), d3(dt)
            negf, negb = cst("neg_f"), cst("neg_b")
            g_state = {}

            def group(gi):
                q = gi % 2

                @block.tensor
                def _(_e):
                    E.wait_ge(*xt_ready)
                    E.wait_ge(*ac_ready)
                    E.wait_ge(*g_free[q])
                    E.wait_ge(*g_state.get("psum", loaded))
                    for u in range(NT):
                        ins = E.matmul(bank(4)[:, u * T:(u + 1) * T], bc[:, gi, u * P:(u + 1) * P],
                                       bc[:, 8 + gi, :], start=True, stop=True)
                    Ring.p = pe.count(ins.then_inc(pe.sem, 1))

                @block.scalar
                def _(_e):
                    A.wait_ge(*Ring.p)
                    A.wait_ge(*g_free[q])
                    b = bank(4)
                    A.activation(G_[q][:, 0:256], b[:, 0:256], ACT.Copy)
                    A.activation(G_[q][:, 256:384], b[:, 384:512], ACT.Copy)
                    A.activation(G_[q][:, 384:512], b[:, 0:128], ACT.Copy)
                    Ring.q = act.count(A.activation(G_[q][:, 512:768], b[:, 256:512], ACT.Copy).then_inc(act.sem, 1))
                g_state["psum"] = g_state["G", q] = Ring.q

                @block.vector
                def _(_e):
                    V.wait_ge(*xt_ready)
                    V.wait_ge(*ac_ready)
                    V.wait_ge(*g_free[q])
                    for u in range(NT):
                        for d in range(2):
                            dd = dt3[:, u, d * 32 + 4 * gi:d * 32 + 4 * gi + 4].rearrange("p (r o) -> p r o", o=1)
                            Ring.q = dve.count(V.tensor_tensor(
                                xd[q][:, u, d, :].rearrange("p (r n) -> p r n", r=4),
                                xt[u][:, gi * T:(gi + 1) * T].rearrange("p (r n) -> p r n", r=4),
                                spread(dd, [P, 4, HD]), ALU.mult).then_inc(dve.sem, 1))
                g_state["x", q] = Ring.q

            rows_ready, back_done = {}, {}

            def rows(h):
                b = bank(h % 2)

                @block.tensor
                def _(_e):
                    E.wait_ge(*ac_ready)
                    E.wait_ge(*arow_free[h % 2])
                    for d in range(2):
                        ins = E.matmul(b[:, d * T:(d + 1) * T], spread(ident[0:64, d * 32 + h:d * 32 + h + 1], [64, P]),
                                       acT[0:64, :], start=True, stop=True)
                    rows_ready[h] = pe.count(ins.then_inc(pe.sem, 1))

            def decays(h):
                b = bank(h % 2)
                e = ee[h % 3]

                @block.vector
                def _(_e):
                    V.wait_ge(*rows_ready[h])
                    V.wait_ge(*ee_free[h % 3])
                    for lo, w, src, u, d, neg in ((0, 128, 0, 0, 0, negf), (256, 128, 128, 1, 0, negf),
                                                  (384, 128, T, 0, 1, negb), (640, 128, T + 128, 1, 1, negb)):
                        V.scalar_tensor_tensor(e[:, lo:lo + w], b[:, src:src + w], acu[:, u, d * 32 + h:d * 32 + h + 1],
                                               neg, ALU.subtract, ALU.add)
                    V.tensor_scalar(e[:, 128:256], b[:, 128:256], acu[:, 0, h:h + 1], None, ALU.subtract)
                    arow_free[h % 2] = dve.count(V.tensor_scalar(e[:, 512:640], b[:, T:T + 128],
                                                                acu[:, 1, 32 + h:33 + h], None, ALU.subtract).then_inc(dve.sem, 1))

                @block.scalar
                def _(_e):
                    A.wait_ge(*arow_free[h % 2])
                    ee_ready[h % 3] = act.count(A.activation(e, e, ACT.Exp).then_inc(act.sem, 1))

            def sums(h):
                gi, rr, q = h // 4, h % 4, (h // 4) % 2
                e = ee[h % 3]

                @block.vector
                def _(_e):
                    V.wait_ge(*ee_ready[h % 3])
                    V.wait_ge(*g_state["G", q])
                    Ring.q = dve.count(V.tensor_tensor(e, e, G_[q], ALU.mult).then_inc(dve.sem, 1))
                hp = (h % 2) * HD
                yb = bank(2 + (h // 2) % 2)

                @block.tensor
                def _(_e):
                    E.wait_ge(*Ring.q)
                    E.wait_ge(*g_state["x", q])
                    E.wait_ge(*(y_free[(h // 2) % 2] if h % 2 == 0 else loaded))
                    o = yb[hp:hp + HD, 0:T]
                    xr = lambda u, d: xd[q][:, u, d, rr * HD:(rr + 1) * HD]
                    E.matmul(o, xr(0, 0), e[:, 0:256], start=True, stop=False)
                    E.matmul(o, xr(1, 1), e[:, 512:768], start=False, stop=False)
                    E.matmul(o[:, 128:256], xr(1, 0), e[:, 256:384], start=False, stop=False)
                    ins = E.matmul(o[:, 0:128], xr(0, 1), e[:, 384:512], start=False, stop=True)
                    ee_free[h % 3] = pe.count(ins.then_inc(pe.sem, 1))
                if h % 4 == 3:
                    g_free[q] = ee_free[h % 3]
                back_done[h] = ee_free[h % 3]

            def finish(h):
                if h % 2:
                    c = h // 2
                    yb = bank(2 + c % 2)

                    @block.vector
                    def _(_e):
                        V.wait_ge(*back_done[h])
                        y_free[c % 2] = vl(V.scalar_tensor_tensor(xb[:, c, :], xb[:, c, :], prm("d_skip")[:, c:c + 1],
                                                                  yb[:, 0:T], ALU.mult, ALU.add).then_inc(dve.sem, 1))
                        vl(V.tensor_tensor(xb[:, c, :], xb[:, c, :], zs[:, c, :], ALU.mult).then_inc(dve.sem, 1))

            group(0)
            rows(0)
            for h in range(34):
                if h + 1 < 32:
                    rows(h + 1)
                if h < 32:
                    decays(h)
                if h % 4 == 1 and h // 4 + 1 < 8:
                    group(h // 4 + 1)
                if 1 <= h <= 32:
                    sums(h - 1)
                if h >= 2:
                    finish(h - 2)
            y_done = [(dve.sem, dve.n), (pe.sem, pe.n)]

            sq = zs_
            inv = htok_[:, :]

            @block.scalar
            def _(_e):
                for point in y_done:
                    A.wait_ge(*point)
                Ring.q = act.count(A.activation(sq, xb_, ACT.Square).then_inc(act.sem, 1))

            @block.vector
            def _(_e):
                for point in y_done:
                    V.wait_ge(*point)
                Ring.p = dve.count(V.memset(Arow[:, 0:1], 1.0).then_inc(dve.sem, 1))

            @block.tensor
            def _(_e):
                E.wait_ge(*Ring.q)
                E.wait_ge(*Ring.p)
                for gi in range(8):
                    for c in range(2):
                        ins = E.matmul(banks(gi // 2, 1)[:, (gi % 2) * T:(gi % 2 + 1) * T], spread(Arow[:, 0:1], [P, P]),
                                       zs[:, 2 * gi + c, :], start=c == 0, stop=c == 1)
                Ring.p = pe.count(ins.then_inc(pe.sem, 1))

            @block.vector
            def _(_e):
                V.wait_ge(*Ring.p)
                Ring.q = vl(V.tensor_scalar(inv, banks(0, 4), 1.0 / T, EPS, ALU.mult, ALU.add).then_inc(dve.sem, 1))

            @block.scalar
            def _(_e):
                A.wait_ge(*Ring.q)
                Ring.q = act.count(A.activation(inv, inv, ACT.Sqrt).then_inc(act.sem, 1))

            @block.vector
            def _(_e):
                V.wait_ge(*Ring.q)
                vl(V.reciprocal(inv, inv).then_inc(dve.sem, 1))
                for c in range(16):
                    Ring.q = dve.count(V.scalar_tensor_tensor(xb[:, c, :], xb[:, c, :], prm("snorm_g")[:, c:c + 1],
                                                             inv[:, (c // 2) * T:(c // 2 + 1) * T], ALU.mult, ALU.mult).then_inc(dve.sem, 1))
            ar.close()
            r_row = row_of(mod_col(0, 1, 2), 1.0, [Ring.q])
            done = out_project("w_ssd_out", 16, xb, [(dve.sem, dve.n), (act.sem, act.n), (pe.sem, pe.n)])
            y_ar.close()
            return add_gated(done + [r_row])

        def mla(ready):
            ar = Arena()
            zt = ar.take(NT * 672).rearrange("p (t n) -> p t n", t=NT)
            qlT = ar.take(3 * T).rearrange("p (c t) -> p c t", c=3)
            klT = ar.take(2 * T).rearrange("p (c t) -> p c t", c=2)
            vt = ar.take(NT * 1024).rearrange("p (t h n) -> p t h n", t=NT, h=16)
            qT = ar.take(16 * T).rearrange("p (h t) -> p h t", h=16)
            kT = ar.take(16 * T).rearrange("p (h t) -> p h t", h=16)
            qk = Arena()
            qt = qk.take(NT * 1536).rearrange("p (t h n) -> p t h n", t=NT, h=16)
            kt = qk.take(NT * 1536).rearrange("p (t h n) -> p t h n", t=NT, h=16)
            h_ready = modulated(1, 1, ready, None)
            ang, cosr, sinr, rn = (small[:, 64 + 32 * n:96 + 32 * n] for n in range(4))
            sc = small[:, 192:256]
            t3 = lambda z, n: z.rearrange("p (t n) -> p t n", t=n)

            def evac(c, b, p):
                w = 32 if c == 5 else P

                @block.scalar
                def _(_e):
                    A.wait_ge(*p)
                    Ring.q = act.count(A.activation(zt[:, :, c * P:c * P + w],
                                                   b[:, 0:2 * w].rearrange("p (t d) -> p t d", t=NT), ACT.Copy).then_inc(act.sem, 1))
                return (Ring.q,)
            project("w_mla_in", 6, evac, h_ready, None, (), tokens=range(6), widths={5: 32})
            z_ready = Ring.q
            ss = small[:, 0:4]

            @block.scalar
            def _(_e):
                A.wait_ge(*z_ready)
                for t in range(NT):
                    al(A.activation(htok[:, 0, 0:384], zt[:, t, 0:384], ACT.Square, accum_out=ss[:, t:t + 1]).then_inc(act.sem, 1))
                    Ring.q = al(A.activation(htok[:, 1, 0:256], zt[:, t, 384:640], ACT.Square, accum_out=ss[:, 2 + t:3 + t]).then_inc(act.sem, 1))

            @block.vector
            def _(_e):
                V.wait_ge(*Ring.q)
                V.tensor_scalar(ss[:, 0:2], ss[:, 0:2], 1.0 / 384, EPS, ALU.mult, ALU.add)
                Ring.q = vl(V.tensor_scalar(ss[:, 2:4], ss[:, 2:4], 1.0 / 256, EPS, ALU.mult, ALU.add).then_inc(dve.sem, 1))
                V.tensor_copy(sc[:, 0:NT], posi[:, :])
                vl(V.memset(rn, 0.0).then_inc(dve.sem, 1))
                for t in range(NT):
                    vl(V.tensor_scalar(ang[:, 16 * t:16 * t + 16], cst("inv_freq"), sc[:, t:t + 1], None, ALU.mult).then_inc(dve.sem, 1))
                two_pi = 2 * math.pi
                c1 = 6.28125
                c2 = float(np.float32(math.floor((two_pi - c1) * 2 ** 20) / 2 ** 20))
                c3 = two_pi - c1 - c2
                magic = 12582912.0
                lim = 3.1415925
                for dst, quarter in ((sinr, 0.0), (cosr, 0.25)):
                    vl(V.tensor_scalar(rn, ang, 1.0 / two_pi, quarter, ALU.mult, ALU.add).then_inc(dve.sem, 1))
                    vl(V.tensor_scalar(rn, rn, magic, None, ALU.add).then_inc(dve.sem, 1))
                    vl(V.tensor_scalar(rn, rn, -magic, None, ALU.add).then_inc(dve.sem, 1))
                    vl(V.scalar_tensor_tensor(dst, rn, -c1, ang, ALU.mult, ALU.add).then_inc(dve.sem, 1))
                    vl(V.scalar_tensor_tensor(dst, rn, -c2, dst, ALU.mult, ALU.add).then_inc(dve.sem, 1))
                    vl(V.scalar_tensor_tensor(dst, rn, -c3, dst, ALU.mult, ALU.add).then_inc(dve.sem, 1))
                    if quarter:
                        vl(V.tensor_scalar(dst, dst, math.pi / 2, None, ALU.add).then_inc(dve.sem, 1))
                    Ring.p = vl(V.tensor_scalar(dst, dst, lim, -lim, ALU.min, ALU.max).then_inc(dve.sem, 1))

            @block.scalar
            def _(_e):
                A.wait_ge(*Ring.q)
                Ring.q = act.count(A.activation(ss, ss, ACT.Sqrt).then_inc(act.sem, 1))
                A.wait_ge(*Ring.p)
                A.activation(sinr, sinr, ACT.Sin)
                Ring.p = act.count(A.activation(cosr, cosr, ACT.Sin).then_inc(act.sem, 1))
            rope_ready = Ring.p

            @block.vector
            def _(_e):
                V.wait_ge(*Ring.q)
                vl(V.reciprocal(ss, ss).then_inc(dve.sem, 1))
                for t in range(NT):
                    V.tensor_scalar(zt[:, t, 0:384], zt[:, t, 0:384], ss[:, t:t + 1], None, ALU.mult)
                    Ring.q = dve.count(V.tensor_scalar(zt[:, t, 384:640], zt[:, t, 384:640], ss[:, 2 + t:3 + t], None, ALU.mult).then_inc(dve.sem, 1))
            lat = Ring.q
            pts = []
            for c in range(5):
                @block.tensor
                def _(_e):
                    E.wait_ge(*lat)
                    for t in range(NT):
                        ins = E.transpose(bank(c)[:, t * P:(t + 1) * P], zt[:, t, c * P:(c + 1) * P], ident)
                    Ring.p = pe.count(ins.then_inc(pe.sem, 1))

                @block.vector
                def _(_e):
                    V.wait_ge(*Ring.p)
                    dst = qlT[:, c, :] if c < 3 else klT[:, c - 3, :]
                    gain = prm("q_norm_g")[:, c:c + 1] if c < 3 else prm("kv_norm_g")[:, c - 3:c - 2]
                    pts.append(dve.count(V.tensor_scalar(dst, bank(c)[:, 0:T], gain, None, ALU.mult).then_inc(dve.sem, 1)))
            lat_ready = pts[-1]
            freed = [lat_ready] * 8
            n = 0
            for name, nb_, kk_, src in (("w_uq", 3, 3, qlT), ("w_ukv", 4, 2, klT)):
                for c in range(nb_):
                    s, full = load(dram[name][c:c + 1], 1)
                    w = slot_ap(s, kk_ * 512).rearrange("p (k n) -> p k n", k=kk_)
                    for t in range(NT):
                        b = n % 8
                        n += 1

                        @block.tensor
                        def _(_e):
                            E.wait_ge(*full)
                            E.wait_ge(*lat_ready)
                            E.wait_ge(*freed[b])
                            for k in range(kk_):
                                ins = E.matmul(bank(b), src[:, k, t * P:(t + 1) * P], w[:, k, :],
                                               start=k == 0, stop=k == kk_ - 1)
                            Ring.p = pe.count(ins.then_inc(pe.sem, 1))

                        @block.scalar
                        def _(_e):
                            A.wait_ge(*Ring.p)
                            if name == "w_uq":
                                ins = A.activation(qt[:, t].rearrange("p h n -> p (h n)")[:, c * 512:(c + 1) * 512],
                                                   bank(b), ACT.Copy)
                            else:
                                v4 = bank(b).rearrange("p (h n) -> p h n", h=4)
                                A.activation(kt[:, t, 4 * c:4 * c + 4, 0:64], v4[:, :, 0:64], ACT.Copy)
                                ins = A.activation(vt[:, t, 4 * c:4 * c + 4, :], v4[:, :, 64:128], ACT.Copy)
                            freed[b] = act.count(ins.then_inc(act.sem, 1))
                    Ring.used[s] = [(pe.sem, pe.n)]
            up_ready = (act.sem, act.n)
            scr = [z.rearrange("p h t -> p (h t)")[:, o:o + 1536].rearrange("p (h n) -> p h n", h=16)
                   for z in (qT, kT) for o in (0, 1536)]
            rot = hT_[:, 0:1024].rearrange("p (a h n) -> p a h n", a=4, h=16)
            hs_ = sc.rearrange("p (a t h) -> p a t h", a=2, t=NT)

            squared = []

            @block.vector
            def _(_e):
                V.wait_ge(*up_ready)
                for t in range(NT):
                    vl(V.tensor_copy(kt[:, t, :, 64:96], spread(zt[:, t, 640:672].rearrange("p (o n) -> p o n", o=1),
                                                                [P, 16, 32])).then_inc(dve.sem, 1))
            k_whole = (dve.sem, dve.n)

            @block.scalar
            def _(_e):
                A.wait_ge(*up_ready)
                for a_, src in enumerate((qt, kt)):
                    for t in range(NT):
                        if a_:
                            A.wait_ge(*k_whole)
                        squared.append(act.count(A.activation(scr[2 * a_ + t], src[:, t], ACT.Square).then_inc(act.sem, 1)))

            @block.vector
            def _(_e):
                for a_, src in enumerate((qt, kt)):
                    for t in range(NT):
                        V.wait_ge(*squared[2 * a_ + t])
                        vl(V.tensor_reduce(hs_[:, a_, t, :], scr[2 * a_ + t], AXX, ALU.add).then_inc(dve.sem, 1))
                Ring.q = (dve.sem, dve.n)
            rstd_of(sc, 64, 1.0 / 96, EPS, Ring.q)

            roped = []

            @block.vector
            def _(_e):
                V.wait_ge(*rope_ready)
                for a_, (src, gain) in enumerate(((qt, prm("q_head_g")), (kt, prm("k_head_g")))):
                    for t in range(NT):
                        vl(V.tensor_tensor(src[:, t], src[:, t], spread(hs_[:, a_, t, :].rearrange("p (h o) -> p h o", o=1),
                                                                        [P, 16, 96]), ALU.mult).then_inc(dve.sem, 1))
                        vl(V.tensor_tensor(src[:, t], src[:, t], spread(gain.rearrange("p (o n) -> p o n", o=1),
                                                                        [P, 16, 96]), ALU.mult).then_inc(dve.sem, 1))
                        co, si = (spread(z[:, 16 * t:16 * t + 16].rearrange("p (o n) -> p o n", o=1), [P, 16, 16])
                                  for z in (cosr, sinr))
                        x1, x2 = src[:, t, :, 64:80], src[:, t, :, 80:96]
                        V.tensor_tensor(rot[:, 0], x1, co, ALU.mult)
                        V.tensor_tensor(rot[:, 1], x2, si, ALU.mult)
                        V.tensor_tensor(rot[:, 2], x2, co, ALU.mult)
                        vl(V.tensor_tensor(rot[:, 3], x1, si, ALU.mult).then_inc(dve.sem, 1))
                        V.tensor_tensor(x1, rot[:, 0], rot[:, 1], ALU.subtract)
                        roped.append(vl(V.tensor_tensor(x2, rot[:, 2], rot[:, 3], ALU.add).then_inc(dve.sem, 1)))
            n = 0
            for a_, (src, dst) in enumerate(((qt, qT), (kt, kT))):
                for t in range(NT):
                    roped_ = roped[2 * a_ + t]
                    for h0 in range(0, 16, 4):
                        b = n % 8
                        n += 1

                        @block.tensor
                        def _(_e):
                            E.wait_ge(*roped_)
                            E.wait_ge(*freed[b])
                            for i in range(4):
                                ins = E.transpose(bank(b)[0:96, i * P:(i + 1) * P], src[:, t, h0 + i, :], ident)
                            Ring.p = pe.count(ins.then_inc(pe.sem, 1))

                        @block.scalar
                        def _(_e):
                            A.wait_ge(*Ring.p)
                            A.wait_ge(*roped_)
                            freed[b] = act.count(A.activation(dst[0:96, h0:h0 + 4, t * P:(t + 1) * P],
                                                             bank(b)[0:96, :].rearrange("p (h n) -> p h n", h=4), ACT.Copy).then_inc(act.sem, 1))
            oT = hT
            qk.close()
            units = []
            for gq in range(4):
                for t in range(NT):
                    u = dict(branch=0, scale=96 ** -0.5, keys=T, blocks=2, last=True, dist=None,
                             q=lambda i, gq=gq, t=t: qT[0:96, 4 * gq + i, t * P:(t + 1) * P],
                             k=lambda i, gq=gq: kT[0:96, 4 * gq + i, :],
                             v=lambda i, b, gq=gq: vt[:, b, 4 * gq + i, :],
                             out=oT[:, 2 * gq:2 * gq + 2, t * P:(t + 1) * P])
                    u["parts"] = [u]
                    units.append(u)
            o_ready = attend(units, T, [(act.sem, act.n), (pe.sem, pe.n), (dve.sem, dve.n)])
            ar.close()
            r_row = row_of(mod_col(1, 1, 2), 1.0, o_ready)
            done = out_project("w_mla_out", 8, oT, o_ready)
            return add_gated(done + [r_row])

        @block.scalar
        def _(_e):
            Ring.q = al(A.activation(cond, prm("c"), ACT.Silu).then_inc(act.sem, 1))

        @block.vector
        def _(_e):
            V.wait_ge(*Ring.q)
            vl(V.memset(one_col, 1.0).then_inc(dve.sem, 1))

        stages = [hybrid, lambda r: conv_ffn(0, r), nsa, lambda r: conv_ffn(1, r),
                  lambda r: silu_ffn(0, 0, 0, r, (1, 0)), ssd, lambda r: silu_ffn(0, 2, 1, r, (1, 1)),
                  lambda r: silu_ffn(1, 0, 0, r), mla, lambda r: silu_ffn(1, 2, 1, r)]
        at = [(act.sem, act.n), (dve.sem, dve.n)]
        for stage in stages:
            at = stage(at)

        @block.sync
        def _(sp):
            for point in at:
                sp.wait_ge(*point)
            sp.dma_start(out, xs_[:, :]).then_inc(stored, 16)
            sp.wait_ge(stored, 16)


def kernel(**inputs):
    import concourse.bacc as bacc
    from concourse.bass_utils import run_bass_kernel_spmd

    arrays, pat = lay_out(inputs)
    cat = constant_table()[1]
    nc = bacc.Bacc("TRN2", target_bir_lowering=False, num_devices=1)
    dram = {}
    for name, a in arrays.items():
        dram[name] = nc.dram_tensor("in_" + name, a.shape, mybir.dt.from_np(a.dtype), kind="ExternalInput").ap()
    out = nc.dram_tensor("out_x", (P, NT * D), F32, kind="ExternalOutput").ap()
    build(nc, dram, out, pat, cat)
    r = run_bass_kernel_spmd(nc, [{"in_" + n: a for n, a in arrays.items()}], core_ids=[0])
    y = r.results[0]["out_x"].reshape(P, NT, D).transpose(1, 0, 2).reshape(1, T, D)
    return np.ascontiguousarray(y)
```
